# Optimizing a Trainium2 kernel written in Bass

```python
import numpy as np
import jax
import jax.numpy as jnp
from jax import lax

D_MODEL = 1024
BATCH = 1
SEQ = 256
DEPTH = 2

HEAD_DIM = 64
ROPE_THETA = 10000.0
EPS = 1e-6
Q_BLOCK = 128
NEG_INF = -1e30
FORCE_SCORE = 1e4
N_MOD = 9
D_FF = 2816
A_HEADS = 4
A_KV_HEADS = 2
A_WINDOW = 128
B_HEADS = 4
B_Q_LORA = 256
B_KV_LORA = 128
B_NOPE = 64
B_ROPE = 32
B_V = 64
C_HEADS = 8
C_KV_HEADS = 2
C_CMP_BLOCK = 32
C_CMP_STRIDE = 16
C_SLC_BLOCK = 64
C_N_SEL = 8
C_WINDOW = 256
C_CMP_HID = 128
C_GATE_HID = 64
IN_WIDTHS = (A_HEADS * HEAD_DIM, A_KV_HEADS * HEAD_DIM, A_KV_HEADS * HEAD_DIM,
             B_Q_LORA, B_KV_LORA, B_ROPE,
             C_HEADS * HEAD_DIM) + (C_KV_HEADS * HEAD_DIM,) * 6 + (C_GATE_HID,)
D_IN = sum(IN_WIDTHS)
D_MIX = A_HEADS * HEAD_DIM + B_HEADS * B_V + C_HEADS * HEAD_DIM

kernel_name = 'hybrid_swa_mla_nsa_macaron_adaln'

def rms_norm(x, g):
    xf = x.astype(jnp.float32)
    y = xf * lax.rsqrt(jnp.mean(xf * xf, axis=-1, keepdims=True) + EPS)
    return (y * g.astype(jnp.float32)).astype(x.dtype)

def rope_tables(positions, dim):
    inv_freq = 1.0 / (ROPE_THETA ** (jnp.arange(0, dim, 2, dtype=jnp.float32) / dim))
    ang = positions.astype(jnp.float32)[..., None] * inv_freq
    return jnp.cos(ang), jnp.sin(ang)

def apply_rope(x, cos, sin):
    xf = x.astype(jnp.float32)
    x1, x2 = jnp.split(xf, 2, axis=-1)
    c, s = cos[:, :, None, :], sin[:, :, None, :]
    return jnp.concatenate([x1 * c - x2 * s, x2 * c + x1 * s], axis=-1).astype(x.dtype)

def swiglu(u, w_in, w_out):
    gate, up = jnp.split(u @ w_in, 2, axis=-1)
    return (jax.nn.silu(gate) * up) @ w_out

def banded_attention(q, k, v, window, sinks=None):
    b, t, h, d = q.shape
    hkv = k.shape[2]
    g = h // hkv
    nb = t // Q_BLOCK
    npv = window // Q_BLOCK
    qb = q.reshape(b, nb, Q_BLOCK, hkv, g, d)

    def band(z):
        zb = z.reshape(b, nb, Q_BLOCK, hkv, z.shape[-1])
        zp = jnp.pad(zb, ((0, 0), (npv, 0), (0, 0), (0, 0), (0, 0)))
        return jnp.concatenate([zp[:, i:i + nb] for i in range(npv + 1)], axis=2)

    kb, vb = band(k), band(v)
    s = jnp.einsum('bnqhgd,bnkhd->bhgnqk', qb, kb).astype(jnp.float32) * (d ** -0.5)
    n_keys = (npv + 1) * Q_BLOCK
    rel = (jnp.arange(Q_BLOCK)[:, None] + npv * Q_BLOCK) - jnp.arange(n_keys)[None, :]
    k_abs = jnp.arange(nb)[:, None] * Q_BLOCK + jnp.arange(n_keys)[None, :] - npv * Q_BLOCK
    mask = ((rel >= 0) & (rel < window))[None] & (k_abs >= 0)[:, None, :]
    s = jnp.where(mask, s, NEG_INF)
    if sinks is None:
        p = jax.nn.softmax(s, axis=-1)
    else:
        sink = jnp.broadcast_to(sinks.astype(jnp.float32).reshape(1, hkv, g, 1, 1, 1), s.shape[:-1] + (1,))
        p = jax.nn.softmax(jnp.concatenate([s, sink], axis=-1), axis=-1)[..., :-1]
    o = jnp.einsum('bhgnqk,bnkhd->bnqhgd', p.astype(v.dtype), vb)
    return o.reshape(b, t, h, v.shape[-1])

def causal_attention(q, k, v):
    b, t, h, dq = q.shape
    nb = t // Q_BLOCK
    scale = dq ** -0.5
    qb = jnp.moveaxis(q.reshape(b, nb, Q_BLOCK, h, dq), 1, 0)
    k_pos = jnp.arange(t)

    def one(args):
        qi, n = args
        s = jnp.einsum('bqhd,bkhd->bhqk', qi, k).astype(jnp.float32) * scale
        q_pos = n * Q_BLOCK + jnp.arange(Q_BLOCK)
        s = jnp.where(k_pos[None, :] <= q_pos[:, None], s, NEG_INF)
        p = jax.nn.softmax(s, axis=-1).astype(v.dtype)
        return jnp.einsum('bhqk,bkhd->bqhd', p, v)

    o = lax.map(one, (qb, jnp.arange(nb)))
    return jnp.moveaxis(o, 0, 1).reshape(b, t, h, v.shape[-1])

def compress_blocks(z, pe, w1, w2):
    b, t, hkv, d = z.shape
    n_chunk = t // C_CMP_STRIDE
    r = C_CMP_BLOCK // C_CMP_STRIDE
    n_cmp = n_chunk - r + 1
    zc = z.reshape(b, n_chunk, C_CMP_STRIDE, hkv, d)
    blocks = jnp.concatenate([zc[:, i:i + n_cmp] for i in range(r)], axis=2)
    blocks = blocks + pe[None, None, :, None, :]
    flat = jnp.moveaxis(blocks, 3, 2).reshape(b, n_cmp, hkv, C_CMP_BLOCK * d)
    return jax.nn.silu(flat @ w1) @ w2

def nsa_compressed_selected(q, q_rot, k_cmp, v_cmp, k_slc, v_slc):
    b, t, h, d = q.shape
    hkv = k_cmp.shape[2]
    g = h // hkv
    n_cmp = k_cmp.shape[1]
    n_slc = t // C_SLC_BLOCK
    n_sel = min(C_N_SEL, n_slc)
    nb = t // Q_BLOCK
    scale = d ** -0.5
    ci = np.arange(n_cmp)[:, None] * C_CMP_STRIDE
    sj = np.arange(n_slc)[None, :] * C_SLC_BLOCK
    overlap = jnp.asarray((ci <= sj + C_SLC_BLOCK - 1) & (ci + C_CMP_BLOCK - 1 >= sj), dtype=jnp.float32)
    cmp_end = jnp.arange(n_cmp) * C_CMP_STRIDE + (C_CMP_BLOCK - 1)
    s_blk = jnp.arange(n_slc)
    kb = jnp.moveaxis(k_slc.reshape(b, n_slc, C_SLC_BLOCK, hkv, d), 3, 1)
    vb = jnp.moveaxis(v_slc.reshape(b, n_slc, C_SLC_BLOCK, hkv, d), 3, 1)
    gather = jax.vmap(jax.vmap(lambda blocks, i: blocks[i]))

    def to_blocks(z):
        return jnp.moveaxis(z.reshape(b, nb, Q_BLOCK, hkv, g, d), 1, 0)

    def one(args):
        qc, qr, n = args
        q_pos = n * Q_BLOCK + jnp.arange(Q_BLOCK)
        s = jnp.einsum('bqhgd,bjhd->bhgqj', qc, k_cmp).astype(jnp.float32) * scale
        vis = cmp_end[None, :] <= q_pos[:, None]
        p = jnp.where(vis, jax.nn.softmax(jnp.where(vis, s, NEG_INF), axis=-1), 0.0)
        o_cmp = jnp.einsum('bhgqj,bjhd->bqhgd', p.astype(v_cmp.dtype), v_cmp)
        imp = jnp.einsum('bhgqj,js->bhqs', p, overlap)
        cur = q_pos // C_SLC_BLOCK
        forced = (s_blk[None, :] == 0) | (s_blk[None, :] == cur[:, None]) | (s_blk[None, :] == cur[:, None] - 1)
        future = s_blk[None, :] > cur[:, None]
        score = jnp.where(future, NEG_INF, jnp.where(forced, FORCE_SCORE, imp))
        top_val, idx = lax.top_k(score, n_sel)
        blk_ok = top_val > 0.5 * NEG_INF
        kg = gather(kb, idx)
        vg = gather(vb, idx)
        s2 = jnp.einsum('bqhgd,bhqnld->bhgqnl', qr, kg).astype(jnp.float32) * scale
        tok = idx[..., None] * C_SLC_BLOCK + jnp.arange(C_SLC_BLOCK)
        ok = blk_ok[..., None] & (tok <= q_pos[None, None, :, None, None])
        s2 = jnp.where(ok[:, :, None], s2, NEG_INF)
        p2 = jax.nn.softmax(s2.reshape(b, hkv, g, Q_BLOCK, -1), axis=-1).reshape(s2.shape)
        o_slc = jnp.einsum('bhgqnl,bhqnld->bqhgd', p2.astype(vg.dtype), vg)
        return o_cmp.reshape(b, Q_BLOCK, h, d), o_slc.reshape(b, Q_BLOCK, h, d)

    o_cmp, o_slc = lax.map(one, (to_blocks(q), to_blocks(q_rot), jnp.arange(nb)))
    o_cmp = jnp.moveaxis(o_cmp, 0, 1).reshape(b, t, h, d)
    o_slc = jnp.moveaxis(o_slc, 0, 1).reshape(b, t, h, d)
    return o_cmp, o_slc

def hybrid_mixer(u, cos64, sin64, cos32, sin32, w_in, w_out, a_sinks, a_qk_g,
                 b_q_lat_g, b_kv_lat_g, b_w_uq, b_w_ukv, b_qk_nope_g, b_qk_rope_g,
                 c_qk_g, c_cmp_pe, c_cmp_w1, c_cmp_w2, c_gate_w, c_gate_b):
    b, t, _ = u.shape
    splits = np.cumsum(IN_WIDTHS)[:-1].tolist()
    (a_q, a_k, a_v, b_cq, b_ckv, b_kr, c_q,
     c_kc, c_vc, c_ks, c_vs, c_kw, c_vw, c_gf) = jnp.split(u @ w_in, splits, axis=-1)

    def heads(z, n):
        return z.reshape(b, t, n, z.shape[-1] // n)

    qa = apply_rope(rms_norm(heads(a_q, A_HEADS), a_qk_g[0]), cos64, sin64)
    ka = apply_rope(rms_norm(heads(a_k, A_KV_HEADS), a_qk_g[1]), cos64, sin64)
    o_a = banded_attention(qa, ka, heads(a_v, A_KV_HEADS), A_WINDOW, a_sinks)

    q_b = heads(rms_norm(b_cq, b_q_lat_g) @ b_w_uq, B_HEADS)
    kv_b = heads(rms_norm(b_ckv, b_kv_lat_g) @ b_w_ukv, B_HEADS)
    q_nope = rms_norm(q_b[..., :B_NOPE], b_qk_nope_g[0])
    q_pe = apply_rope(rms_norm(q_b[..., B_NOPE:], b_qk_rope_g[0]), cos32, sin32)
    k_nope = rms_norm(kv_b[..., :B_NOPE], b_qk_nope_g[1])
    v_b = kv_b[..., B_NOPE:]
    k_pe = apply_rope(rms_norm(b_kr[:, :, None, :], b_qk_rope_g[1]), cos32, sin32)
    k_b = jnp.concatenate([k_nope, jnp.broadcast_to(k_pe, (b, t, B_HEADS, B_ROPE))], axis=-1)
    o_b = causal_attention(jnp.concatenate([q_nope, q_pe], axis=-1), k_b, v_b)

    qc = rms_norm(heads(c_q, C_HEADS), c_qk_g[0])
    qc_rot = apply_rope(qc, cos64, sin64)
    k_cmp = rms_norm(compress_blocks(heads(c_kc, C_KV_HEADS), c_cmp_pe[0], c_cmp_w1[0], c_cmp_w2[0]), c_qk_g[1])
    v_cmp = compress_blocks(heads(c_vc, C_KV_HEADS), c_cmp_pe[1], c_cmp_w1[1], c_cmp_w2[1])
    k_slc = apply_rope(rms_norm(heads(c_ks, C_KV_HEADS), c_qk_g[2]), cos64, sin64)
    k_win = apply_rope(rms_norm(heads(c_kw, C_KV_HEADS), c_qk_g[3]), cos64, sin64)
    o_cmp, o_slc = nsa_compressed_selected(qc, qc_rot, k_cmp, v_cmp, k_slc, heads(c_vs, C_KV_HEADS))
    o_win = banded_attention(qc_rot, k_win, heads(c_vw, C_KV_HEADS), C_WINDOW)
    gates = jax.nn.sigmoid(jax.nn.silu(c_gf) @ c_gate_w + c_gate_b).reshape(b, t, C_HEADS, 3)
    o_c = gates[..., 0:1] * o_cmp + gates[..., 1:2] * o_slc + gates[..., 2:3] * o_win

    o = jnp.concatenate([o_a.reshape(b, t, -1), o_b.reshape(b, t, -1), o_c.reshape(b, t, -1)], axis=-1)
    return o @ w_out

def setup_inputs(seed: int = 0) -> dict:
    key = jax.random.key(seed)
    ks = jax.random.split(key, 25)

    def nrm(k, shape, s):
        return jax.random.normal(k, shape, jnp.float32) * s

    def gain(k, shape):
        return 1.0 + 0.05 * jax.random.normal(k, shape, jnp.float32)

    x = nrm(ks[0], (BATCH, SEQ, D_MODEL), 1.0)
    c = nrm(ks[1], (BATCH, D_MODEL), 1.0)
    offsets = jax.random.randint(ks[2], (BATCH, 1), 0, 1024, dtype=jnp.int32)
    positions = (offsets + jnp.arange(SEQ, dtype=jnp.int32)[None, :]).astype(jnp.int32)
    return {
        'x': x,
        'c': c,
        'positions': positions,
        'ada_w': nrm(ks[3], (DEPTH, D_MODEL, N_MOD * D_MODEL), 0.5 * D_MODEL ** -0.5),
        'ada_b': nrm(ks[4], (DEPTH, N_MOD * D_MODEL), 0.02),
        'norm_g': gain(ks[5], (DEPTH, 3, D_MODEL)),
        'ffn_w_in': nrm(ks[6], (DEPTH, 2, D_MODEL, 2 * D_FF), D_MODEL ** -0.5),
        'ffn_w_out': nrm(ks[7], (DEPTH, 2, D_FF, D_MODEL), D_FF ** -0.5),
        'w_in': nrm(ks[8], (DEPTH, D_MODEL, D_IN), D_MODEL ** -0.5),
        'w_out': nrm(ks[9], (DEPTH, D_MIX, D_MODEL), D_MIX ** -0.5),
        'a_sinks': nrm(ks[10], (DEPTH, A_HEADS), 0.5),
        'a_qk_g': gain(ks[11], (DEPTH, 2, HEAD_DIM)),
        'b_q_lat_g': gain(ks[12], (DEPTH, B_Q_LORA)),
        'b_kv_lat_g': gain(ks[13], (DEPTH, B_KV_LORA)),
        'b_w_uq': nrm(ks[14], (DEPTH, B_Q_LORA, B_HEADS * (B_NOPE + B_ROPE)), B_Q_LORA ** -0.5),
        'b_w_ukv': nrm(ks[15], (DEPTH, B_KV_LORA, B_HEADS * (B_NOPE + B_V)), B_KV_LORA ** -0.5),
        'b_qk_nope_g': gain(ks[16], (DEPTH, 2, B_NOPE)),
        'b_qk_rope_g': gain(ks[17], (DEPTH, 2, B_ROPE)),
        'c_qk_g': gain(ks[18], (DEPTH, 4, HEAD_DIM)),
        'c_cmp_pe': nrm(ks[19], (DEPTH, 2, C_CMP_BLOCK, HEAD_DIM), 0.2),
        'c_cmp_w1': nrm(ks[20], (DEPTH, 2, C_CMP_BLOCK * HEAD_DIM, C_CMP_HID), (C_CMP_BLOCK * HEAD_DIM) ** -0.5),
        'c_cmp_w2': nrm(ks[21], (DEPTH, 2, C_CMP_HID, HEAD_DIM), C_CMP_HID ** -0.5),
        'c_gate_w': nrm(ks[22], (DEPTH, C_GATE_HID, C_HEADS * 3), C_GATE_HID ** -0.5),
        'c_gate_b': nrm(ks[23], (DEPTH, C_HEADS * 3), 0.02),
    }

def reference(x, c, positions, ada_w, ada_b, norm_g, ffn_w_in, ffn_w_out, w_in, w_out,
              a_sinks, a_qk_g, b_q_lat_g, b_kv_lat_g, b_w_uq, b_w_ukv, b_qk_nope_g, b_qk_rope_g,
              c_qk_g, c_cmp_pe, c_cmp_w1, c_cmp_w2, c_gate_w, c_gate_b):
    bsz, _, dm = x.shape
    cos64, sin64 = rope_tables(positions, HEAD_DIM)
    cos32, sin32 = rope_tables(positions, B_ROPE)
    cond = jax.nn.silu(c)
    h = x
    for l in range(DEPTH):
        mod = (cond @ ada_w[l] + ada_b[l]).reshape(bsz, N_MOD, 1, dm)
        sh1, sc1, g1, sh2, sc2, g2, sh3, sc3, g3 = [mod[:, i] for i in range(N_MOD)]
        u = rms_norm(h, norm_g[l, 0]) * (1.0 + sc1) + sh1
        h = h + 0.5 * g1 * swiglu(u, ffn_w_in[l, 0], ffn_w_out[l, 0])
        u = rms_norm(h, norm_g[l, 1]) * (1.0 + sc2) + sh2
        h = h + g2 * hybrid_mixer(u, cos64, sin64, cos32, sin32, w_in[l], w_out[l], a_sinks[l], a_qk_g[l],
                                  b_q_lat_g[l], b_kv_lat_g[l], b_w_uq[l], b_w_ukv[l], b_qk_nope_g[l],
                                  b_qk_rope_g[l], c_qk_g[l], c_cmp_pe[l], c_cmp_w1[l], c_cmp_w2[l],
                                  c_gate_w[l], c_gate_b[l])
        u = rms_norm(h, norm_g[l, 2]) * (1.0 + sc3) + sh3
        h = h + 0.5 * g3 * swiglu(u, ffn_w_in[l, 1], ffn_w_out[l, 1])
    return h


_drawn_inputs = setup_inputs


def setup_inputs(seed=0):
    import zlib

    import numpy as np

    out = dict(_drawn_inputs(seed))
    spreads = {}
    factors = {'ada_b': 2.742,
     'norm_g': 3.287,
     'a_sinks': 60.066,
     'a_qk_g': 8.0,
     'b_q_lat_g': 8.0,
     'b_kv_lat_g': 8.0,
     'b_qk_nope_g': 8.0,
     'b_qk_rope_g': 8.0,
     'c_qk_g': 8.0,
     'c_cmp_pe': 3.068,
     'c_gate_b': 8.0}
    for name, (base, spread) in spreads.items():
        noise = np.random.default_rng([zlib.crc32(name.encode()), seed]).standard_normal(out[name].shape)
        drawn = base * np.exp(spread * noise) if base else spread * noise
        out[name] = jnp.asarray(drawn.astype(out[name].dtype))
    for name, factor in factors.items():
        out[name] = (out[name] * factor).astype(out[name].dtype)
    return out
```

```python
from contextlib import ExitStack

import numpy as np

import concourse.bass as bass
from concourse import mybir

F32 = mybir.dt.float32
BF16 = mybir.dt.bfloat16
I32 = mybir.dt.int32
ALU = mybir.AluOpType
ACT = mybir.ActivationFunctionType
AX = mybir.AxisListType

P = 128
DEPTH = 2
SEQ = 256
NT = SEQ // P
DM = 1024
KD = DM // P
NMOD = 9
DFF = 2816
NPAIR = DFF // (2 * P)
EPS = 1e-6
NEG = -1e30
HD = 64
ROPE_B = 32
A_H, A_KV = 4, 2
B_H = 4
C_H, C_KV = 8, 2
NCMP = SEQ // 16 - 1
CL = 32
SC64 = float(HD) ** -0.5
SC96 = float(HD + ROPE_B) ** -0.5

C_ID, C_CAUSAL, C_BAND, C_INVF, C_NEG, C_VIS = 0, 128, 256, 384, 432, 462
C_END = 492

G_A, G_C, G_BN, G_BR, G_SINK, G_GB, G_END = 0, 128, 384, 512, 576, 580, 604

WIDE_A, WIDE_M, WIDE_B, WIDE = 0, NPAIR, NPAIR + 6, 2 * NPAIR + 6
TALL_A, TALL_M, TALL_B, TALL = 0, NPAIR, NPAIR + 4, 2 * NPAIR + 4
F_LAT, F_CMPIN, F_A, F_CMPW, F_CQ, F_CK = range(6)
CHUNKS = (F_LAT, F_CMPIN, F_A, F_CQ, F_CK)

AUX = [("zk", "dve"), ("zv", "dve"), ("lat", "dve"), ("kvgf", "act"), ("hid", "act"), ("uq0", "act"),
       ("uq1", "act"), ("w2", "act"), ("gate", "dve"), ("ukv0", "act"), ("ukv1", "act"),
       ("qa", "act"), ("ka", "dve"), ("cq0", "act"), ("cq1", "dve"), ("kc", "dve"), ("cmps0", "dve"), ("cmps1", "dve"),
       ("cr0", "act"), ("cr1", "dve"), ("ks", "act"), ("kw", "dve"),
       ("qb0", "act"), ("qb1", "dve"), ("kb0", "act"), ("kb1", "dve"), ("cmpt", "dve")]
AUXN = [n for n, _ in AUX]
AUX_ACT = sum(e == "act" for _, e in AUX)
AUX_DVE = sum(e == "dve" for _, e in AUX)

JOBS = [("a", h) for h in range(A_H)] + [("b", h) for h in range(B_H)]
JOBS += [(br, h) for h in range(C_H) for br in ("slc", "win")]
NJ = len(JOBS)
LAST = [n for n in range(NJ) if JOBS[n][1] % 2 and (n + 1 == NJ or JOBS[n + 1][1] != JOBS[n][1])]

ADA_PRO = KD
ADA_L = 4 * KD
CHAIN_PRO, CHAIN_L = 19, 256


def hybrid_kernel(nc, x, c, positions, ada_w, ada_b, norm_g, ffn_w_in, ffn_w_out, w_in, w_out,
                  a_sinks, a_qk_g, b_q_lat_g, b_kv_lat_g, b_w_uq, b_w_ukv, b_qk_nope_g, b_qk_rope_g,
                  c_qk_g, c_cmp_pe, c_cmp_w1, c_cmp_w2, c_gate_w, c_gate_b, consts, out):
    with ExitStack() as ctx:
        def sb(name, shape, dt=F32):
            return ctx.enter_context(nc.sbuf_tensor(name, shape, dt))

        def sem(name):
            return ctx.enter_context(nc.semaphore(name))

        h = sb("h", [P, KD, SEQ])
        u = sb("u", [P, KD, SEQ])
        sq = sb("sq", [P, KD * SEQ])
        wide = sb("wide", [P, 2, KD * 512])
        tall = sb("tall", [P, 2, 2 * DM])
        ada = sb("ada", [P, 2, 3 * DM])
        acc = sb("acc", [P, 6 * DM])
        fs = sb("fs", [P, 2, SEQ])
        fa = sb("fa", [P, 2, SEQ])
        cst = sb("cst", [P, C_END])
        idb = sb("idb", [P, P], BF16)
        mcausal = sb("mcausal", [P, 3 * P], BF16)
        mband = sb("mband", [P, 3 * P], BF16)
        zb = sb("zb", [P, 512], BF16)
        ones = sb("ones", [P, P])
        rows = sb("rows", [P, 3, P])
        vt = sb("vt", [P, 3, P])
        cond = sb("cond", [P, KD])
        mod = sb("mod", [P, 3, 3, KD])
        posi = sb("posi", [P, NT], I32)
        posf = sb("posf", [P, NT])
        cs64 = sb("cs64", [P, 2, NT, HD])
        cs32 = sb("cs32", [P, 2, NT, ROPE_B])
        small = sb("small", [P, 64])
        newt_i = sb("newt_i", [P, 32], I32)
        newt = sb("newt", [P, 32])
        ssb = sb("ssb", [P, 32])
        rst = sb("rst", [P, 32])
        gn = sb("gn", [P, G_END])
        uq = sb("uq", [P, 2, 384])
        ukv = sb("ukv", [P, 512])
        w2 = sb("w2", [P, 2, HD])
        gw = sb("gw", [HD, 24])
        plat = acc[:, 0:832].rearrange("p (t n) -> p t n", t=NT)
        pz = acc[:, 832:1856].rearrange("p (t a d n) -> p t a d n", t=NT, a=4, d=2)
        pgf = acc[:, 1856:1984].rearrange("p (t n) -> p t n", t=NT)
        pa = acc[:, 1984:3008].rearrange("p (t n) -> p t n", t=NT)
        pq = acc[:, 3008:4032].rearrange("p (t n) -> p t n", t=NT)
        pk = acc[:, 4032:5056].rearrange("p (t n) -> p t n", t=NT)
        zc = acc[:, 5056:6016].rearrange("p (a h m b) -> p a h m b", a=2, h=2, m=CL // 2)
        qa = sb("qa", [P, NT, A_H, HD])
        kad = sb("kad", [P, NT, A_KV, 2, HD])
        qr = sb("qr", [P, NT, C_H, HD])
        krd = sb("krd", [P, NT, 4, 2, HD])
        qb = sb("qb", [P, NT, B_H, 96])
        kvb = sb("kvb", [P, NT, B_H, P])
        kb = sb("kb", [P, NT, B_H, 96])
        latT = sb("latT", [P, 3, SEQ])
        gfT = sb("gfT", [HD, SEQ])
        qaT = sb("qaT", [P, 2, SEQ])
        kaT = sb("kaT", [P, 2, SEQ])
        cqT = sb("cqT", [P, 4, SEQ])
        crT = sb("crT", [P, 4, SEQ])
        ckT = sb("ckT", [P, 4, SEQ])
        qbT = sb("qbT", [96, B_H, SEQ])
        kbT = sb("kbT", [96, B_H, SEQ])
        hidk = sb("hidk", [P, 2, 16])
        hidv = sb("hidv", [P, 2, 4, 32])
        kcn = sb("kcn", [16, 2, HD])
        kcd = sb("kcd", [P, 2, 2, HD])
        kcT = sb("kcT", [P, 2, P])
        vrep = sb("vrep", [P, 2, HD])
        gt = sb("gt", [P, NT, 24])
        latg = sb("latg", [P, 3])
        pe2 = sb("pe2", [P, 32])
        cmpT = sb("cmpT", [P, 2, SEQ])
        stat = sb("stat", [P, 4, 8])
        E = sq[:, 0:1152].rearrange("p (r n) -> p r n", r=3)
        ET = sq[:, 1152:1920].rearrange("p (r n) -> p r n", r=2)
        T1 = sq[:, 0:1024]
        T2 = sq[:, 1024:2048]
        cp = fs[:, :, :].rearrange("p a (h b) -> p a h b", h=C_H)
        csc = fa[:, :, 0:C_H * NCMP].rearrange("p a (h b) -> p a h b", h=C_H)
        trg = cqT[:, 0:2, :].rearrange("p a n -> p (a n)")
        cst16 = sb("cst16", [P, 3, NT * C_H])

        ps = ctx.enter_context(nc.psum_tensor("ps", [P, 8, 512], F32))
        y = ps[:, 4:8, :].rearrange("p b (e n) -> p (b e) n", e=2)

        s_const, s_pos, s_x, s_rows, s_small = (sem(n) for n in ("const", "pos", "xin", "rows", "smallw"))
        wide_in = [sem("wide_in0"), sem("wide_in1")]
        tall_in = [sem("tall_in0"), sem("tall_in1")]
        ada_in = [sem("ada_in0"), sem("ada_in1")]
        wide_used, tall_used, ada_used = sem("wide_used"), sem("tall_used"), sem("ada_used")
        setup, turned, cond_ok, trig, trig_in = (sem(n) for n in ("setup", "turned", "cond", "trig", "trigin"))
        h_ready, sq_ready, ss_ready, diag_ready, r_ready = (
            sem(n) for n in ("h_ready", "sq_ready", "ss_ready", "diag_ready", "r_ready"))
        hn_ready, u_ready = sem("hn_ready"), sem("u_ready")
        gu_ready, silu_ready, mul_ready, y_ready = (
            sem(n) for n in ("gu_ready", "silu_ready", "mul_ready", "y_ready"))
        acc_zero, acc_ready, mod_ps, mod_ready = (
            sem(n) for n in ("acc_zero", "acc_ready", "mod_ps", "mod_ready"))
        proj0, pcopy, aux_ready, aux_act, aux_dve = (
            sem(n) for n in ("proj0", "pcopy", "aux_ready", "aux_act", "aux_dve"))
        prep = sem("prep")
        cmp_shift, cmp_exp = sem("cmp_shift"), sem("cmp_exp")
        gate_exp, mod_lat = sem("gate_exp"), sem("mod_lat")
        s_ready, nm_ready, exp_ready, en_ready, pt_ready, et_ready, pv_ready, o_ready = (
            sem(n) for n in ("s_ready", "nm_ready", "exp_ready", "en_ready", "pt_ready", "et_ready",
                             "pv_ready", "o_ready"))
        out_ps, out_sb, s_out = sem("out_ps"), sem("out_sb"), sem("out")
        chain_s = sem("chain")

        ident = cst[:, C_ID:C_ID + P]

        def wide_wait(eng, l, n):
            eng.wait_ge(wide_in[n % 2], l * (WIDE // 2 * 32) + 32 * (n // 2 + 1))

        def tall_wait(eng, l, n):
            eng.wait_ge(tall_in[n % 2], l * (TALL // 2 * 16) + 16 * (n // 2 + 1))

        PREP = ["lat", "qa", "cq", "kc", "cr", "ck", "qb", "kb", "cmp"]

        def prep_at(l, name):
            return l * len(PREP) + PREP.index(name) + 1

        def aux_bank(name):
            return 4 + AUXN.index(name) % 4

        def aux_done(name, l):
            g = AUXN.index(name)
            who = AUX[g][1]
            count = sum(e == who for _, e in AUX[:g + 1])
            return (aux_act, l * AUX_ACT + count) if who == "act" else (aux_dve, l * AUX_DVE + count)

        def aux_at(l, name):
            names = [m for m in AUXN if m != "hid"]
            return l * len(names) + names.index(name) + 1

        def job(n):
            br, hh = JOBS[n]
            half = slice(64 * (hh % 2), 64 * (hh % 2) + 64)
            if br == "a":
                return (qaT[half, hh // 2, :], kaT[half, hh // 2, :],
                        lambda t: pa[:, t, 384 + hh // 2 * HD:384 + hh // 2 * HD + HD], mband, SC64)
            if br == "b":
                return qbT[:, hh, :], kbT[:, hh, :], lambda t: kvb[:, t, hh, HD:P], mcausal, SC96
            win = int(br == "win")
            kv = hh // 4
            off = 256 + 128 * win + kv * HD
            return (crT[half, hh // 2, :], ckT[half, 2 * win + kv, :],
                    lambda t: pk[:, t, off:off + HD], mcausal, SC64)

        block = ctx.enter_context(nc.Block())

        @block.sync
        def _(sp):
            def fill_wide(l, n, loads):
                sp.wait_ge(wide_used, l * WIDE + n + 1)
                for dst, src in loads:
                    sp.dma_start(dst, src).then_inc(wide_in[n % 2], 16)

            def fill_tall(l, n, src):
                sp.wait_ge(tall_used, l * TALL + n + 1)
                sp.dma_start(tall[:, n % 2, :].rearrange("p (a n) -> p a n", a=2), src)\
                    .then_inc(tall_in[n % 2], 16)

            def fill_ada(count, slot, width, src):
                sp.wait_ge(ada_used, count + 1)
                sp.dma_start(ada[:, slot, 0:width], src).then_inc(ada_in[slot], 16)

            def ffn_pair(l, f, n0, m0, it, parity):
                slot = wide[:, parity[0], :].rearrange("p (e k n) -> p e k n", e=2, k=KD)
                sp.wait_ge(wide_used, l * WIDE + n0 + it + 1)
                for e in range(2):
                    src = ffn_w_in[l, f, :, bass.ds(e * DFF + it * 256, 256)].rearrange(
                        "(k p) n -> p k n", p=P)
                    sp.dma_start(slot[:, e, :, :], src).then_inc(wide_in[parity[0]], 16)
                sp.wait_ge(tall_used, l * TALL + m0 + it + 1)
                src = ffn_w_out[l, f, bass.ds(it * 256, 256), :].rearrange("(a p) n -> p a n", p=P)
                sp.dma_start(tall[:, parity[1], :].rearrange("p (a n) -> p a n", a=2), src)\
                    .then_inc(tall_in[parity[1]], 16)

            def ada_pair(l, f, i):
                for e in range(2):
                    count = l * ADA_L + (ADA_PRO + f * 2 * KD + e) + 2 * i
                    if f == 0:
                        src = ada_w[l, bass.ds(i * P, P), 3 * DM * (e + 1):3 * DM * (e + 2)]
                        fill_ada(count, e, 3 * DM, src)
                    else:
                        src = ada_w[DEPTH - 1, bass.ds(i * P, P), 1536 * e:1536 * (e + 1)]
                        fill_ada(count, e, 1536, src)

            def ffn(l, f):
                n0, m0 = (WIDE_A, TALL_A) if f == 0 else (WIDE_B, TALL_B)
                with sp.Fori(0, KD // 2) as i:
                    for q in range(2):
                        ffn_pair(l, f, n0, m0, 2 * i + q, ((n0 + q) % 2, (m0 + q) % 2))
                        ada_pair(l, f, 2 * i + q)
                for it in range(KD, NPAIR):
                    ffn_pair(l, f, n0, m0, it, ((n0 + it) % 2, (m0 + it) % 2))

            for k in range(ADA_PRO):
                fill_ada(k, k % 2, 3 * DM, ada_w[0, k * P:(k + 1) * P, 0:3 * DM])
            with sp.Fori(0, DEPTH) as l:
                bc = lambda ap: ap.partition_broadcast(P)
                for lo, hi, src in ((G_A, G_C, a_qk_g[l].rearrange("a b -> (a b)")),
                                    (G_C, G_BN, c_qk_g[l].rearrange("a b -> (a b)")),
                                    (G_BN, G_BR, b_qk_nope_g[l].rearrange("a b -> (a b)")),
                                    (G_BR, G_SINK, b_qk_rope_g[l].rearrange("a b -> (a b)")),
                                    (G_SINK, G_GB, a_sinks[l]), (G_GB, G_END, c_gate_b[l])):
                    sp.dma_start(gn[:, lo:hi], bc(src)).then_inc(s_small, 16)
                sp.dma_start(uq[:, :, :], b_w_uq[l].rearrange("(k p) n -> p k n", p=P)).then_inc(s_small, 16)
                sp.dma_start(ukv[:, :], b_w_ukv[l]).then_inc(s_small, 16)
                sp.dma_start(w2[:, :, :], c_cmp_w2[l].rearrange("a p n -> p a n")).then_inc(s_small, 16)
                sp.dma_start(gw[:, :], c_gate_w[l]).then_inc(s_small, 16)
                ffn(l, 0)

                def cols(n, off, lo, hi, rest=None):
                    width = rest or hi - lo
                    slot = wide[:, n % 2, 0:KD * width].rearrange("p (k n) -> p k n", k=KD)
                    return slot[:, :, off:off + hi - lo], w_in[l, :, lo:hi].rearrange("(k p) n -> p k n", p=P)

                n = WIDE_M
                fill_wide(l, n, [cols(n, 0, 512, 720, 416), cols(n, 208, 720, 928, 416)])
                n += 1
                fill_wide(l, n, [cols(n, 0, 1440, 1696, 320), cols(n, 256, 2208, 2272, 320)])
                n += 1
                fill_wide(l, n, [cols(n, 256, 256, 512, 512), cols(n, 0, 0, 256, 512)])
                fill_tall(l, TALL_M, w_out[l, 0:256, :].rearrange("(a p) n -> p a n", p=P))
                n += 1
                w1 = wide[:, n % 2, :].rearrange("p (m n) -> p m n", n=P)
                w1_src = c_cmp_w1[l].rearrange("a (m p) n -> p (a m) n", p=P)
                fill_wide(l, n, [(w1[r:r + 64, :, :], w1_src[r:r + 64, :, :]) for r in (0, 64)])
                n += 1
                fill_wide(l, n, [cols(n, 0, 928, 1184, 512), cols(n, 256, 1184, 1440, 512)])
                n += 1
                fill_wide(l, n, [cols(n, 0, 1696, 1952, 512), cols(n, 256, 1952, 2208, 512)])
                for m in range(1, 4):
                    fill_tall(l, TALL_M + m, w_out[l, m * 256:(m + 1) * 256, :].rearrange("(a p) n -> p a n", p=P))
                ffn(l, 1)
            o = u[:, :, :].rearrange("p (t j) n -> p t (j n)", t=NT)
            for t in range(NT):
                sp.wait_ge(out_sb, 2 * t + 2)
                sp.dma_start(out[0, t * P:(t + 1) * P, :], o[:, t, :]).then_inc(s_out, 16)
            sp.wait_ge(s_out, 16 * NT)

        @block.tensor
        def _(pe):
            mm, tr = nc.tensor.matmul, nc.tensor.transpose
            pe.sem_inc(wide_used, 2)
            pe.sem_inc(tall_used, 2)

            def norm_stats(l, j):
                for k in range(KD):
                    pe.wait_ge(sq_ready, l * 24 + (8 * j + k + 1))
                    for t in range(NT):
                        i = mm(ps[:, 2 + t, 0:1], sq[:, k * SEQ + t * P:k * SEQ + t * P + P], ones[:, 0:1],
                               start=(k == 0), stop=(k == KD - 1))
                i.then_inc(ss_ready, 1)
                pe.wait_ge(diag_ready, l * 3 + (j + 1))
                for t in range(NT):
                    i = mm(ps[:, 2, t * P:(t + 1) * P], ones[:, :], T1[:, t * P:(t + 1) * P], start=True, stop=True)
                i.then_inc(r_ready, 1)

            def open_y(first):
                for b in range(4):
                    i = mm(ps[:, 4 + b, :], zb[:, 0:P], zb[:, :], start=True, stop=False, skip_group_check=True)

            def gate_up(l, f, n0, it, slot, a, first, uj):
                wv = wide[:, slot, :].rearrange("p (e k n) -> p e k n", e=2, k=KD)
                for e in range(2):
                    for k in range(KD):
                        if a == 0 and e == 0:
                            if k == 0:
                                pe.wait_ge(wide_in[slot], l * (WIDE // 2 * 32) + it_landed(n0, it, 32))
                            pe.wait_ge(u_ready, l * 24 + (8 * uj + k + 1))
                        i = mm(ps[:, a, e * SEQ:(e + 1) * SEQ], wv[:, e, k, a * P:(a + 1) * P], u[:, k, :],
                               start=(k == 0), stop=(k == KD - 1))
                i.then_inc(gu_ready, 1)

            def it_landed(n0, it, per):
                return it[1] * per + per * ((n0 + it[0]) // 2 + 1)

            def down(l, f, m0, it, slot, a, last):
                tv = tall[:, slot, :].rearrange("p (a n) -> p a n", a=2)
                if a == 0:
                    pe.wait_ge(tall_in[slot], l * (TALL // 2 * 16) + it_landed(m0, it, 16))
                pe.wait_ge(mul_ready, l * (4 * NPAIR) + (2 * NPAIR * f + 2 * it[0] + a + 1) + 4 * it[1])
                for d in range(KD):
                    i = mm(y[:, d, :], tv[:, a, d * P:(d + 1) * P], fa[:, a, :], start=False, stop=False,
                           skip_group_check=True)
                    if a == 0 and d == 0:
                        i.then_inc(wide_used, 1)
                    if last and a == 1 and d in (1, 3, 5):
                        i.then_inc(y_ready, 1)
                if a == 1:
                    i.then_inc(tall_used, 1)

            def ffn(l, f):
                j = 2 * f
                n0, m0 = (WIDE_A, TALL_A) if f == 0 else (WIDE_B, TALL_B)
                norm_stats(l, j)
                open_y(f == 0)

                def iteration(it, last):
                    q = it[0]
                    for a in range(2):
                        gate_up(l, f, n0, it, (n0 + q) % 2, a, False, j)
                    for a in range(2):
                        down(l, f, m0, it, (m0 + q) % 2, a, last)

                with pe.Fori(0, KD // 2) as i:
                    for q in range(2):
                        iteration((q, i), False)
                iteration((KD, 0), False)
                units = 2 - f
                pe.wait_ge(acc_ready, l * 2 + (f + 2))
                for v in range(24 * units):
                    i = mm(ps[:, 2, v:v + 1], acc[:, v * P:(v + 1) * P], ones[:, 0:1], start=True, stop=True)
                i.then_inc(mod_ps, 1)
                for it in range(KD + 1, NPAIR):
                    iteration((it, 0), it == NPAIR - 1)

            def aux_open(l, name):
                g = AUXN.index(name)
                if g >= 4:
                    pe.wait_ge(*aux_done(AUXN[g - 4], l))
                return ps[:, 4 + g % 4, :]

            def project(l, fill, width, banks):
                n = WIDE_M + fill
                wv = wide[:, n % 2, 0:KD * width].rearrange("p (k n) -> p k n", k=KD)
                wide_wait(pe, l, n)
                c = CHUNKS.index(fill)
                if c >= 2:
                    pe.wait_ge(pcopy, l * 2 * len(CHUNKS) + 2 * (c - 1))
                for t in range(NT):
                    for k in range(KD):
                        if fill == F_LAT and t == 0:
                            pe.wait_ge(u_ready, l * 24 + (8 + k + 1))
                        i = mm(ps[:, banks + t, 0:width], u[:, k, t * P:(t + 1) * P], wv[:, k, :],
                               start=(k == 0), stop=(k == KD - 1))
                    i.then_inc(proj0 if t == 0 else wide_used, 1)

            def turn(l, name, blocks):
                bank = aux_open(l, name)
                for col, src in blocks:
                    rows_, width = src.shape[0], src.shape[-1]
                    i = tr(bank[0:width, col:col + rows_], src, ident[0:rows_, 0:rows_])
                i.then_inc(aux_ready, 1)

            def scores(l, n):
                q, k, _, mask, _ = job(n)
                bank = ps[:, n % 2, 0:3 * P]
                if n >= 2:
                    pe.wait_ge(exp_ready, l * NJ + (n - 1))
                mm(bank, idb[:, :], mask[:, :], start=True, stop=False, skip_group_check=True)
                mm(bank[:, 0:P], q[:, 0:P], k[:, 0:P], start=False, stop=False, skip_group_check=True)
                mm(bank[:, P:3 * P], q[:, P:2 * P], k[:, :], start=False, stop=True,
                   skip_group_check=True).then_inc(s_ready, 1)

            def turn_probs(l, n):
                pe.wait_ge(en_ready, l * NJ + (n + 1))
                if n >= 1:
                    pe.wait_ge(et_ready, l * NJ + n)
                for b in range(3):
                    i = tr(ps[:, 2, b * P:(b + 1) * P], E[:, n % 3, b * P:(b + 1) * P], ident)
                i.then_inc(pt_ready, 1)

            def values(l, n):
                _, _, v, _, _ = job(n)
                br, hh = JOBS[n]
                o = ps[64 * (hh % 2):64 * (hh % 2) + 64, 3, 0:SEQ]
                pair = sum(m < n for m in LAST)
                first = n == 0 or JOBS[n - 1][1] != hh
                if first and hh % 2 == 0 and pair:
                    pe.wait_ge(o_ready, l * 8 + pair)
                pe.wait_ge(et_ready, l * NJ + (n + 1))
                mm(o, v(0), ET[:, n % 2, 0:SEQ], start=first, stop=False, skip_group_check=True)
                i = mm(o[:, P:SEQ], v(1), ET[:, n % 2, SEQ:3 * P], start=False, stop=False, skip_group_check=True)
                if br == "win":
                    r = slice(32 * (hh % 4), 32 * (hh % 4) + 32)
                    if hh == 0:
                        pe.wait_ge(*aux_done("cmpt", l))
                    i = mm(o, vrep[r, hh // 4, :], cmpT[r, hh // 4, :], start=False, stop=True, skip_group_check=True)
                i.then_inc(pv_ready, 1)

            def mix_out(l, m):
                n = TALL_M + m
                tall_wait(pe, l, n)
                tv = tall[:, n % 2, :].rearrange("p (a n) -> p a n", a=2)
                if m == 0:
                    pe.wait_ge(*aux_done("kb0", l))
                    pe.wait_ge(*aux_done("cmpt", l))
                    open_y(False)
                for a in range(2):
                    pe.wait_ge(o_ready, l * 8 + (2 * m + a + 1))
                    for d in range(KD):
                        i = mm(y[:, d, :], tv[:, a, d * P:(d + 1) * P], u[:, 2 * m + a, :], start=False,
                               stop=False, skip_group_check=True)
                        if m == 3 and a == 1 and d in (1, 3, 5):
                            i.then_inc(y_ready, 1)
                i.then_inc(tall_used, 1)

            def mixer(l):
                norm_stats(l, 1)
                project(l, F_LAT, 416, 0)
                project(l, F_CMPIN, 320, 2)
                project(l, F_A, 512, 0)
                pe.wait_ge(pcopy, l * 10 + 4)
                for a, name in enumerate(("zk", "zv")):
                    turn(l, name, [(hh * SEQ + t * P, pz[:, t, 2 * a + hh, :, :].rearrange("p d n -> p (d n)"))
                                   for hh in range(2) for t in range(NT)])
                pe.wait_ge(prep, prep_at(l, "lat"))
                turn(l, "lat", [(b * SEQ + t * P, plat[:, t, b * P:(b + 1) * P]) for b in range(2) for t in range(NT)])
                turn(l, "kvgf", [(t * P, plat[:, t, 256:384]) for t in range(NT)]
                     + [(SEQ + t * P, pgf[:, t, :]) for t in range(NT)])
                n = WIDE_M + F_CMPW
                w1 = wide[:, n % 2, :].rearrange("p (a m n) -> p a m n", a=2, m=CL // 2)
                bank = aux_open(l, "hid")
                pe.wait_ge(*aux_done("zv", l))
                wide_wait(pe, l, n)
                for a in range(2):
                    for m in range(CL // 2):
                        i = mm(bank[:, 32 * a:32 * a + 2 * NCMP], w1[:, a, m, :], zc[:, a, :, m, :],
                               start=(m == 0), stop=(m == CL // 2 - 1))
                i.then_inc(wide_used, 1)
                project(l, F_CQ, 512, 2)
                pe.wait_ge(*aux_done("lat", l))
                pe.wait_ge(*aux_done("kvgf", l))
                pe.wait_ge(s_small, (l + 1) * 160)
                for t in range(NT):
                    bank = aux_open(l, f"uq{t}")
                    for k in range(2):
                        i = mm(bank[:, 0:384], latT[:, k, t * P:(t + 1) * P], uq[:, k, :], start=(k == 0), stop=(k == 1))
                    i.then_inc(aux_ready, 1)
                bank = aux_open(l, "w2")
                pe.wait_ge(*aux_done("hid", l))
                for g in range(2):
                    mm(bank[0:NCMP, g * HD:(g + 1) * HD], hidk[:, g, 0:NCMP], w2[:, 0, :], start=True, stop=True)
                for g in range(2):
                    i = mm(bank[:, (2 + g) * HD:(3 + g) * HD], hidv[:, g, :, :].rearrange("p r b -> p (r b)"),
                           w2[:, 1, :], start=True, stop=True)
                i.then_inc(aux_ready, 1)
                bank = aux_open(l, "gate")
                for t in range(NT):
                    i = mm(bank[:, t * 24:(t + 1) * 24], gfT[:, t * P:(t + 1) * P], gw[:, :], start=True, stop=True)
                i.then_inc(aux_ready, 1)
                project(l, F_CK, 512, 0)
                for t in range(NT):
                    bank = aux_open(l, f"ukv{t}")
                    mm(bank, latT[:, 2, t * P:(t + 1) * P], ukv[:, :], start=True, stop=True).then_inc(aux_ready, 1)

                def pairs(name, src, heads):
                    turn(l, name, [(b * SEQ + t * P, src[:, t, 2 * hp:2 * hp + 2, :].rearrange("p a n -> p (a n)"))
                                   for b, hp in enumerate(heads) for t in range(NT)])

                def doubled(name, src, g0):
                    turn(l, name, [(b * SEQ + t * P, src[:, t, g0 + b, :, :].rearrange("p a n -> p (a n)"))
                                   for b in range(2) for t in range(NT)])

                pe.wait_ge(prep, prep_at(l, "qa"))
                pairs("qa", qa, (0, 1))
                doubled("ka", kad, 0)
                cq = pq[:, :, :].rearrange("p t (a n) -> p t a n", a=C_H)
                pe.wait_ge(prep, prep_at(l, "cq"))
                pairs("cq0", cq, (0, 1))
                pairs("cq1", cq, (2, 3))
                pe.wait_ge(prep, prep_at(l, "kc"))
                turn(l, "kc", [(P * g, kcd[:, g, :, :].rearrange("p a n -> p (a n)")) for g in range(2)])
                pe.wait_ge(*aux_done("cq0", l))
                pe.wait_ge(*aux_done("cq1", l))
                pe.wait_ge(*aux_done("kc", l))
                for odd in range(2):
                    bank = aux_open(l, f"cmps{odd}")
                    half = slice(64 * odd, 64 * odd + 64)
                    for t in range(NT):
                        for hp in range(C_H // 2):
                            col = (t * C_H // 2 + hp) * 16
                            i = mm(bank[:, col:col + NCMP], cqT[half, hp, t * P:(t + 1) * P],
                                   kcT[half, hp // 2, 0:NCMP], start=True, stop=True)
                    i.then_inc(aux_ready, 1)
                pe.wait_ge(prep, prep_at(l, "cr"))
                pairs("cr0", qr, (0, 1))
                pairs("cr1", qr, (2, 3))
                pe.wait_ge(prep, prep_at(l, "ck"))
                doubled("ks", krd, 0)
                doubled("kw", krd, 2)
                for nm, src in (("qb", qb), ("kb", kb)):
                    pe.wait_ge(prep, prep_at(l, nm))
                    for g in range(2):
                        turn(l, f"{nm}{g}", [(b * SEQ + t * P, src[:, t, 2 * g + b, :]) for b in range(2)
                                             for t in range(NT)])
                pe.wait_ge(prep, prep_at(l, "cmp"))
                turn(l, "cmpt", [(g * SEQ + t * P, cp[:, t, 4 * g:4 * g + 4, :].rearrange("p a n -> p (a n)"))
                                 for g in range(2) for t in range(NT)])
                pe.wait_ge(*aux_done("kb0", l))
                pe.wait_ge(*aux_done("kb1", l))
                for n in range(NJ + 3):
                    if n < NJ:
                        scores(l, n)
                    if 0 <= n - 2 < NJ:
                        turn_probs(l, n - 2)
                    if n >= 3:
                        values(l, n - 3)
                    for m in range(4):
                        if n == LAST[2 * m + 1] + 5 or (n == NJ + 2 and LAST[2 * m + 1] + 5 > n):
                            mix_out(l, m)

            pe.wait_ge(setup, 1)
            pe.wait_ge(s_const, 16)
            pe.wait_ge(s_rows, 16 * 7)
            for r in range(3):
                m = (126, 72, 72)[r]
                i = tr(ps[:, 0, r * P:r * P + m], rows[0:m, r, :], ident[0:m, 0:m])
            i.then_inc(turned, 1)
            pe.wait_ge(s_x, 32)
            xs = u[:, :, :].rearrange("p (t j) n -> p t (j n)", t=NT)
            for b in range(4):
                for e in range(2):
                    for t in range(NT):
                        k = 2 * b + e
                        i = tr(y[:, k, t * P:(t + 1) * P], xs[:, t, k * P:(k + 1) * P], ident)
                i.then_inc(turned, 1)
            pe.wait_ge(acc_ready, 1)
            for v in range(24):
                i = mm(ps[:, 1, v:v + 1], acc[:, v * P:(v + 1) * P], ones[:, 0:1], start=True, stop=True)
            i.then_inc(mod_ps, 1)
            with pe.Fori(0, DEPTH) as l:
                ffn(l, 0)
                mixer(l)
                ffn(l, 1)
            pe.wait_ge(h_ready, 8 + 24 * DEPTH)
            for t in range(NT):
                for b in range(2):
                    for k in range(4):
                        i = tr(ps[:, 2 * t + b, k * P:(k + 1) * P], h[:, 4 * b + k, t * P:(t + 1) * P], ident)
                    i.then_inc(out_ps, 1)

        @block.scalar
        def _(act):
            A = nc.scalar.activation
            act.dma_start(cst[:, :], consts[:, :]).then_inc(s_const, 16)
            for r0, src in ((0, norm_g.rearrange("l j (k n) -> (l j k) n", n=P)),
                            (48, c.rearrange("a (k n) -> (a k) n", n=P)),
                            (56, b_q_lat_g.rearrange("l (k n) -> (l k) n", n=P)),
                            (60, b_kv_lat_g[:, :]),
                            (62, c_cmp_pe.rearrange("l a (m e) n -> (l a m) (e n)", e=2))):
                act.dma_start(rows[r0:r0 + src.shape[0], 0, :], src).then_inc(s_rows, 16)
            for l in range(DEPTH):
                act.dma_start(rows[0:72, 1 + l, :], ada_b[l].rearrange("(k n) -> k n", n=P)).then_inc(s_rows, 16)
            xs = u[:, :, :].rearrange("p (t j) n -> p t (j n)", t=NT)
            for t in range(NT):
                act.dma_start(xs[:, t, :], x[0, t * P:(t + 1) * P, :]).then_inc(s_x, 16)
            act.dma_start(posi[:, :], positions.rearrange("a (t p) -> p (a t)", p=P),
                          allow_slow_non_contiguous=True).then_inc(s_pos, 16)

            act.wait_ge(turned, 1)
            A(cond[:, :], ps[:, 0, 48:56], ACT.Silu).then_inc(cond_ok, 1)
            act.wait_ge(trig_in, 1)
            A(trg[:, 0:192], trg[:, 0:192], ACT.Sin).then_inc(trig, 1)

            def squares(l, j):
                for k in range(KD):
                    act.wait_ge(h_ready, l * 24 + (8 * j + k + 1))
                    A(sq[:, k * SEQ:(k + 1) * SEQ], h[:, k, :], ACT.Square).then_inc(sq_ready, 1)

            def shift(l, j):
                act.wait_ge(mod_ready, l * 3 + (j + 1))
                for k in range(KD):
                    act.wait_ge(hn_ready, l * 24 + (8 * j + k + 1))
                    A(u[:, k, :], sq[:, k * SEQ:(k + 1) * SEQ], ACT.Identity, bias=mod[:, j, 0, k:k + 1])\
                        .then_inc(u_ready, 1)

            def ffn(l, f):
                squares(l, 2 * f)
                shift(l, 2 * f)
                act.wait_ge(mod_ps, l * 2 + (1 + f))
                width = (2 - f) * 3 * DM
                nc.scalar.copy(acc[:, 0:width], zb[:, 0:1].broadcast_to([P, width])).then_inc(acc_zero, 1)

                def tile(m, i=0):
                    act.wait_ge(gu_ready, l * (4 * NPAIR) + (2 * NPAIR * f + m + 1) + 4 * i)
                    A(fs[:, m % 2, :], ps[:, m % 2, 0:SEQ], ACT.Silu).then_inc(silu_ready, 1)

                with act.Fori(0, KD // 2) as i:
                    for q in range(4):
                        tile(q, i)
                for m in range(2 * KD, 2 * NPAIR):
                    tile(m)

            def copy_proj(l, chunk):
                base = l * 2 * len(CHUNKS) + 2 * chunk
                fill = CHUNKS[chunk]
                bank = 2 * (chunk % 2)
                for t in range(NT):
                    if t == 0:
                        act.wait_ge(proj0, l * len(CHUNKS) + (chunk + 1))
                    else:
                        act.wait_ge(wide_used, l * WIDE + (WIDE_M + fill + 3))
                    src = ps[:, bank + t, :]
                    if fill == F_LAT:
                        nc.scalar.copy(plat[:, t, :], src[:, 0:416]).then_inc(pcopy, 1)
                    elif fill == F_CMPIN:
                        A(pgf[:, t, :], src[:, 256:320], ACT.Silu)
                        nc.scalar.copy(pz[:, t, :, :, :], src[:, 0:256].rearrange("p (a n) -> p a n", a=4)
                                       .unsqueeze(2).broadcast_to([P, 4, 2, HD])).then_inc(pcopy, 1)
                    elif fill == F_CK:
                        nc.scalar.copy(pk[:, t, :].rearrange("p (b a n) -> p a b n", a=2, b=2),
                                       src.rearrange("p (a b n) -> p a b n", a=2, b=2)).then_inc(pcopy, 1)
                    else:
                        dst = {F_A: pa, F_CQ: pq}[fill]
                        nc.scalar.copy(dst[:, t, :], src).then_inc(pcopy, 1)

            def aux_wait(l, name):
                act.wait_ge(aux_ready, aux_at(l, name))

            def out_of(l, name, dst, width=P):
                aux_wait(l, name)
                src = ps[0:width, aux_bank(name), :].rearrange("p (b n) -> p b n", b=2)
                nc.scalar.copy(dst, src).then_inc(aux_act, 1)

            def mixer(l):
                squares(l, 1)
                shift(l, 1)
                act.wait_ge(mod_ps, l * 2 + 2)
                copy_proj(l, 0)
                copy_proj(l, 1)
                copy_proj(l, 2)
                aux_wait(l, "kvgf")
                b = aux_bank("kvgf")
                act.wait_ge(mod_lat, l + 1)
                A(latT[:, 2, :], ps[:, b, 0:SEQ], ACT.Copy, scale=latg[:, 2:3])
                nc.scalar.copy(gfT[:, :], ps[0:HD, b, SEQ:2 * SEQ]).then_inc(aux_act, 1)
                act.wait_ge(wide_used, l * WIDE + (WIDE_M + F_CMPW + 3))
                b = aux_bank("hid")
                A(hidk[:, :, 0:NCMP], ps[:, b, 0:2 * NCMP].rearrange("p (g b) -> p g b", g=2), ACT.Silu)
                A(hidv[:, :, :, 0:NCMP], ps[:, b, 32:32 + 2 * NCMP].rearrange("p (g b) -> p g b", g=2)
                  .unsqueeze(2).broadcast_to([P, 2, 4, NCMP]), ACT.Silu).then_inc(aux_act, 1)
                copy_proj(l, 3)
                for t in range(NT):
                    aux_wait(l, f"uq{t}")
                    nc.scalar.copy(qb[:, t, :, :].rearrange("p a n -> p (a n)"), ps[:, aux_bank(f"uq{t}"), 0:384])\
                        .then_inc(aux_act, 1)
                aux_wait(l, "w2")
                b = aux_bank("w2")
                nc.scalar.copy(kcn[0:NCMP, :, :], ps[0:NCMP, b, 0:P].rearrange("p (g n) -> p g n", g=2))
                nc.scalar.copy(vrep[:, :, :], ps[:, b, P:2 * P].rearrange("p (g n) -> p g n", g=2)).then_inc(aux_act, 1)
                act.wait_ge(*aux_done("gate", l))
                A(gt[:, :, :], gt[:, :, :], ACT.Exp, scale=-1.0).then_inc(gate_exp, 1)
                copy_proj(l, 4)
                for t in range(NT):
                    aux_wait(l, f"ukv{t}")
                    nc.scalar.copy(kvb[:, t, :, :].rearrange("p a n -> p (a n)"), ps[:, aux_bank(f"ukv{t}"), :])\
                        .then_inc(aux_act, 1)
                out_of(l, "qa", qaT[:, :, :])
                out_of(l, "cq0", cqT[:, 0:2, :])
                out_of(l, "cr0", crT[:, 0:2, :])
                out_of(l, "ks", ckT[:, 0:2, :])
                out_of(l, "qb0", qbT[:, 0:2, :], 96)
                out_of(l, "kb0", kbT[:, 0:2, :], 96)
                act.wait_ge(cmp_shift, l + 1)
                A(csc, csc, ACT.Exp, scale=SC64).then_inc(cmp_exp, 1)
                for n in range(NJ + 2):
                    if n < NJ:
                        act.wait_ge(nm_ready, l * NJ + (n + 1))
                        st = stat[:, n % 4, :]
                        scale = job(n)[4]
                        bank = ps[:, n % 2, :]
                        if JOBS[n][0] == "a":
                            hh = JOBS[n][1]
                            A(st[:, 6:8], st[:, 2:4], ACT.Exp, bias=gn[:, G_SINK + hh:G_SINK + hh + 1])
                        A(E[:, n % 3, 0:P], bank[:, 0:P], ACT.Exp, bias=st[:, 2:3], scale=scale,
                          accum_out=st[:, 4:5])
                        A(E[:, n % 3, P:3 * P], bank[:, P:3 * P], ACT.Exp, bias=st[:, 3:4], scale=scale,
                          accum_out=st[:, 5:6]).then_inc(exp_ready, 1)
                    if n >= 2:
                        m = n - 2
                        act.wait_ge(pt_ready, l * NJ + (m + 1))
                        if m >= 2:
                            act.wait_ge(pv_ready, l * NJ + (m - 1))
                        nc.scalar.copy(ET[:, m % 2, :], ps[:, 2, 0:3 * P]).then_inc(et_ready, 1)

            with act.Fori(0, DEPTH) as l:
                ffn(l, 0)
                mixer(l)
                ffn(l, 1)
            o = u[:, :, :].rearrange("p (b j) n -> p b (j n)", b=4)
            for b in range(4):
                act.wait_ge(out_ps, b + 1)
                nc.scalar.copy(o[:, b, :], ps[:, b, :]).then_inc(out_sb, 1)

        @block.vector
        def _(dve):
            V = nc.vector
            tt, ts, stt = V.tensor_tensor, V.tensor_scalar, V.scalar_tensor_tensor
            chain = {"base": 0, "n": 0}

            def link(ins):
                chain["n"] += 1
                ins.then_inc(chain_s, 1)
                dve.wait_ge(chain_s, chain["base"] + chain["n"])

            def rsqrt(n, p=P):
                s, t, r = ssb[0:p, 0:n], newt[0:p, 0:n], rst[0:p, 0:n]
                link(ts(newt_i[0:p, 0:n], s.bitcast(I32), 1, None, ALU.logical_shift_right))
                link(ts(r.bitcast(I32), newt_i[0:p, 0:n], -1.0, float(0x5F3759DF), ALU.mult, ALU.add))
                for _ in range(3):
                    link(tt(t, r, r, ALU.mult))
                    link(stt(t, t, -0.5, s, ALU.mult, ALU.mult))
                    link(stt(r, t, 1.5, r, ALU.add, ALU.mult))

            def heads_rstd(src, dim):
                p, a, n, d = src.shape
                tmp = T1[0:p, 0:a * n * d].rearrange("p (a n d) -> p a n d", a=a, n=n)
                link(tt(tmp, src, src, ALU.mult))
                link(V.tensor_reduce(ssb[0:p, 0:a * n].rearrange("p (a n) -> p a n", a=a), tmp, AX.X, ALU.add))
                link(ts(ssb[0:p, 0:a * n], ssb[0:p, 0:a * n], 1.0 / dim, EPS, ALU.mult, ALU.add))
                rsqrt(a * n, p)

            def by_rstd(src, dst):
                p, a, n, d = src.shape
                r = rst[0:p, 0:a * n].rearrange("p (a n) -> p a n", a=a).unsqueeze(3).broadcast_to([p, a, n, d])
                link(tt(dst, src, r, ALU.mult))

            def gain(ap, lo, dst=None):
                p, a, n, d = ap.shape
                g = gn[0:p, lo:lo + d].unsqueeze(1).unsqueeze(1).broadcast_to([p, a, n, d])
                return tt(ap if dst is None else dst, ap, g, ALU.mult)

            def rope(src, cs, outs):
                p, a, n, d = src.shape
                hf = d // 2
                t1 = T1[:, 0:a * n * d].rearrange("p (a n d) -> p a n d", a=a, n=n)
                t2 = T2[:, 0:a * n * d].rearrange("p (a n d) -> p a n d", a=a, n=n)
                wide_ = lambda ap: ap.unsqueeze(2).broadcast_to([p, a, n, ap.shape[-1]])
                tt(t1, src, wide_(cs[:, 0, :, :]), ALU.mult)
                tt(t2[:, :, :, 0:hf], src[:, :, :, hf:d], wide_(cs[:, 1, :, 0:hf]), ALU.mult)
                link(tt(t2[:, :, :, hf:d], src[:, :, :, 0:hf], wide_(cs[:, 1, :, hf:d]), ALU.mult))
                for o in outs[:-1]:
                    tt(o, t1, t2, ALU.add)
                return tt(outs[-1], t1, t2, ALU.add)

            def unit(sums, adab, ng, slot, half):
                m = mod[:, slot, :, :].rearrange("p v k -> p (v k)")
                link(tt(m, sums, adab, ALU.add))
                if half:
                    ts(mod[:, slot, 2, :], mod[:, slot, 2, :], 0.5, None, ALU.mult)
                return stt(mod[:, slot, 1, :], mod[:, slot, 1, :], 1.0, ng, ALU.add, ALU.mult)

            dve.sem_inc(ada_used, 2)
            V.memset(ones[:, :], 1.0)
            V.memset(zb[:, :], 0.0)
            V.memset(hidk[:, :, :], 0.0)
            V.memset(kcd[:, :, :, :], 0.0)
            V.memset(hidv[:, :, :, :], 0.0)
            link(V.memset(mband[:, :], 0.0))
            link(V.memset(mcausal[:, :], 0.0))
            dve.wait_ge(s_const, 16)
            V.tensor_copy(idb[:, :], ident)
            for m in (mcausal, mband):
                V.tensor_copy(m[:, 0:P], cst[:, C_CAUSAL:C_CAUSAL + P])
                V.tensor_copy(m[:, 2 * P:3 * P], cst[:, C_CAUSAL:C_CAUSAL + P])
            V.tensor_copy(mband[:, P:2 * P], cst[:, C_BAND:C_BAND + P]).then_inc(setup, 1)
            dve.wait_ge(turned, 1)
            dve.wait_ge(cond_ok, 1)
            for r in range(3):
                m = (126, 72, 72)[r]
                i = V.tensor_copy(vt[:, r, 0:m], ps[:, 0, r * P:r * P + m])
            link(i)
            for b in range(4):
                dve.wait_ge(turned, b + 2)
                for e in range(2):
                    V.tensor_copy(h[:, 2 * b + e, :], y[:, 2 * b + e, :]).then_inc(h_ready, 1)

            two_pi = 2.0 * np.pi
            c1 = 6.28125
            c2 = float(np.float32(two_pi - c1))
            c3 = float(np.float32(two_pi - c1 - np.float64(np.float32(two_pi - c1))))
            magic = 12582912.0
            angf = trg[:, 192:288]
            ang = angf.rearrange("p (t n) -> p t n", t=NT)
            kk = trg[:, 288:480].rearrange("p (e n) -> p e n", e=2)
            rr = trg[:, 0:192].rearrange("p (e n) -> p e n", e=2)
            dve.wait_ge(s_pos, 16)
            link(V.tensor_copy(posf[:, :], posi[:, :]))
            link(tt(ang, cst[:, C_INVF:C_INVF + 48].unsqueeze(1).broadcast_to([P, NT, 48]),
                    posf[:, :].unsqueeze(2).broadcast_to([P, NT, 48]), ALU.mult))
            ts(kk[:, 0, :], angf, 1.0 / two_pi, 0.25, ALU.mult, ALU.add)
            link(ts(kk[:, 1, :], angf, 1.0 / two_pi, None, ALU.mult))
            link(ts(kk, kk, magic, None, ALU.add))
            link(ts(kk, kk, -magic, None, ALU.add))
            link(stt(rr, kk, -c1, ang.rearrange("p t n -> p (t n)").unsqueeze(1).broadcast_to([P, 2, 96]),
                     ALU.mult, ALU.add))
            link(stt(rr, kk, -c2, rr, ALU.mult, ALU.add))
            link(stt(rr, kk, -c3, rr, ALU.mult, ALU.add))
            link(ts(rr[:, 0, :], rr[:, 0, :], two_pi / 4, None, ALU.add))
            for cmp, turn_ in ((ALU.is_gt, -two_pi), (ALU.is_lt, two_pi)):
                link(ts(kk, rr, float(np.float32(-turn_ / 2)), turn_, cmp, ALU.mult))
                link(tt(rr, rr, kk, ALU.add))
            link(ts(rr, rr, 3.1415925, -3.1415925, ALU.min, ALU.max))
            V.memset(small[:, 1:2], 0.0).then_inc(trig_in, 1)
            dve.wait_ge(trig, 1)
            tv = rr.rearrange("p e (t n) -> p e t n", t=NT)
            for cs, lo, hf in ((cs64, 0, 32), (cs32, 32, 16)):
                V.tensor_copy(cs[:, 0, :, 0:hf], tv[:, 0, :, lo:lo + hf])
                V.tensor_copy(cs[:, 0, :, hf:2 * hf], tv[:, 0, :, lo:lo + hf])
                ts(cs[:, 1, :, 0:hf], tv[:, 1, :, lo:lo + hf], -1.0, None, ALU.mult)
                i = V.tensor_copy(cs[:, 1, :, hf:2 * hf], tv[:, 1, :, lo:lo + hf])
            link(i)
            for k in range(ADA_PRO):
                dve.wait_ge(ada_in[k % 2], 16 * (k // 2 + 1))
                if k == 0:
                    i = ts(acc[:, 0:3 * DM], ada[:, 0, :], cond[:, 0:1], None, ALU.mult)
                else:
                    i = stt(acc[:, 0:3 * DM], ada[:, k % 2, :], cond[:, k:k + 1], acc[:, 0:3 * DM], ALU.mult, ALU.add)
                i.then_inc(ada_used, 1)
                dve.wait_ge(ada_used, 3 + k)
            V.memset(small[:, 0:1], 0.0).then_inc(acc_ready, 1)

            dve.wait_ge(mod_ps, 1)
            unit(ps[:, 1, 0:24], vt[:, 1, 0:24], vt[:, 0, 0:8], 0, True).then_inc(mod_ready, 1)
            dve.wait_ge(mod_ready, 1)
            assert chain["n"] == CHAIN_PRO, chain

            def norm(l, j):
                dve.wait_ge(ss_ready, l * 3 + (j + 1))
                for t in range(NT):
                    i = ts(ssb[:, t:t + 1], ps[:, 2 + t, 0:1], 1.0 / DM, EPS, ALU.mult, ALU.add)
                link(i)
                rsqrt(NT)
                for t in range(NT):
                    i = ts(T1[:, t * P:(t + 1) * P], ident, rst[:, t:t + 1], None, ALU.mult)
                i.then_inc(diag_ready, 1)
                dve.wait_ge(r_ready, l * 3 + (j + 1))
                for k in range(KD):
                    stt(sq[:, k * SEQ:(k + 1) * SEQ], h[:, k, :], mod[:, j, 1, k:k + 1], ps[:, 2, 0:SEQ],
                        ALU.mult, ALU.mult).then_inc(hn_ready, 1)

            def residual(l, j, n):
                for k in range(KD):
                    if k % 2 == 0 and k < 6:
                        dve.wait_ge(y_ready, l * 9 + (3 * j + k // 2 + 1))
                    elif k == 6:
                        dve.wait_ge(tall_used, l * TALL + n + 3)
                    stt(h[:, k, :], y[:, k, :], mod[:, j, 2, k:k + 1], h[:, k, :], ALU.mult, ALU.add)\
                        .then_inc(h_ready, 1)

            def ffn(l, f):
                j = 2 * f
                norm(l, j)
                width = 3 * DM if f == 0 else 1536

                def tile(m, i=0):
                    dve.wait_ge(silu_ready, l * (4 * NPAIR) + (2 * NPAIR * f + m + 1) + 4 * i)
                    tt(fa[:, m % 2, :], fs[:, m % 2, :], ps[:, m % 2, SEQ:2 * SEQ], ALU.mult).then_inc(mul_ready, 1)

                def ada_step(q, i):
                    for e in range(2):
                        count = l * ADA_L + (ADA_PRO + f * 2 * KD + 2 * q + e) + 4 * i
                        dve.wait_ge(ada_in[e], l * (ADA_L * 8) + (ADA_PRO * 8 + f * KD * 16 + 16 * (q + 1)) + 32 * i)
                        a = acc[:, e * width:(e + 1) * width]
                        dve.wait_ge(ada_used, count + 1)
                        stt(a, ada[:, e, 0:width], cond[:, bass.ds(2 * i + q, 1)], a, ALU.mult, ALU.add)\
                            .then_inc(ada_used, 1)

                with dve.Fori(0, KD // 2) as i:
                    for q in range(2):
                        if q == 0:
                            dve.wait_ge(acc_zero, l * 2 + (f + 1))
                        for a in range(2):
                            tile(2 * q + a, i)
                        ada_step(q, i)
                dve.wait_ge(ada_used, l * ADA_L + (ADA_PRO + (f + 1) * 2 * KD + 2))
                V.memset(small[:, 0:1], 0.0).then_inc(acc_ready, 1)
                for m in range(2 * KD, 2 * NPAIR):
                    tile(m)
                    if m == 2 * KD + 3:
                        dve.wait_ge(mod_ps, l * 2 + (f + 2))
                        for s in ((1, 2) if f == 0 else (0,)):
                            if f == 0:
                                adab = vt[:, bass.ds(l + 1, 1), 24 * s:24 * s + 24].rearrange("p a n -> p (a n)")
                                ng = vt[:, 0, bass.ds(l * 24 + 8 * s, 8)]
                                i = unit(ps[:, 2, 24 * (s - 1):24 * s], adab, ng, s, s == 2)
                            else:
                                i = unit(ps[:, 2, 0:24], vt[:, DEPTH, 0:24],
                                         vt[:, 0, 24 * (DEPTH - 1):24 * (DEPTH - 1) + 8], 0, True)
                            i.then_inc(mod_ready, 1)
                        if f == 0:
                            V.tensor_copy(latg[:, 0:2], vt[:, 0, bass.ds(l * 2 + 56, 2)])
                            V.tensor_copy(pe2[:, :], vt[:, 0, bass.ds(l * 32 + 62, 32)])
                            V.tensor_copy(latg[:, 2:3], vt[:, 0, bass.ds(l + 60, 1)]).then_inc(mod_lat, 1)
                            dve.wait_ge(mod_lat, l + 1)
                dve.wait_ge(mod_ready, l * 3 + (3 if f == 0 else 4))
                residual(l, j, (TALL_A if f == 0 else TALL_B) + NPAIR - 1)

            def aux_wait(l, name):
                dve.wait_ge(aux_ready, aux_at(l, name))

            def copied(l, chunk):
                dve.wait_ge(pcopy, l * 2 * len(CHUNKS) + 2 * (chunk + 1))

            def out_of(l, name, dst, width=P):
                aux_wait(l, name)
                src = ps[0:width, aux_bank(name), :].rearrange("p (b n) -> p b n", b=2)
                V.tensor_copy(dst, src).then_inc(aux_dve, 1)

            def v4(ap, n):
                return ap.rearrange("p t (n d) -> p t n d", n=n)

            def mixer(l):
                norm(l, 1)
                dve.wait_ge(s_small, (l + 1) * 160)
                dve.wait_ge(u_ready, l * 24 + 16)
                copied(l, 0)
                for lo, hi, part in ((0, 256, 0), (256, 384, 2), (384, 416, 4)):
                    s = plat[:, :, lo:hi].unsqueeze(2)
                    tmp = T1[:, 0:2 * (hi - lo)].rearrange("p (a n d) -> p a n d", a=2, n=1)
                    link(tt(tmp, s, s, ALU.mult))
                    link(V.tensor_reduce(ssb[:, part:part + 2].unsqueeze(2), tmp, AX.X, ALU.add))
                    link(ts(ssb[:, part:part + 2], ssb[:, part:part + 2], 1.0 / (hi - lo), EPS, ALU.mult, ALU.add))
                rsqrt(6)
                for lo, hi, part in ((0, 256, 0), (256, 384, 2), (384, 416, 4)):
                    s = plat[:, :, lo:hi]
                    r = rst[:, part:part + 2].unsqueeze(2).broadcast_to([P, NT, hi - lo])
                    i = tt(s, s, r, ALU.mult)
                i.then_inc(prep, 1)
                dve.wait_ge(prep, prep_at(l, "lat"))
                kr = plat[:, :, 384:416].unsqueeze(2)
                link(gain(kr, G_BR + 32))
                link(rope(kr, cs32, [kb[:, :, hh:hh + 1, HD:96] for hh in range(B_H)]))
                for a, name in enumerate(("zk", "zv")):
                    aux_wait(l, name)
                    for hh in range(2):
                        for par in range(2):
                            half = slice(64 * par, 64 * par + 64)
                            src = ps[half, aux_bank(name), hh * SEQ:(hh + 1) * SEQ].rearrange("p (b r) -> p b r", r=16)
                            for late in range(2):
                                z = src[:, late:late + NCMP, par:16:2].rearrange("p b m -> p m b")
                                dst = zc[half, a, hh, 8 * late:8 * late + 8, :]
                                o = pe2[half, a * 16 + 8 * late:a * 16 + 8 * late + 8].unsqueeze(2)\
                                    .broadcast_to([64, 8, NCMP])
                                i = tt(dst, z, o, ALU.add)
                    i.then_inc(aux_dve, 1)
                aux_wait(l, "lat")
                for b in range(2):
                    i = ts(latT[:, b, :], ps[:, aux_bank("lat"), b * SEQ:(b + 1) * SEQ], latg[:, b:b + 1], None, ALU.mult)
                i.then_inc(aux_dve, 1)
                copied(l, 2)
                qk = v4(pa[:, :, 0:384], 6)
                heads_rstd(qk, HD)
                by_rstd(qk, qk)
                gain(qk[:, :, 0:A_H, :], G_A)
                link(gain(qk[:, :, A_H:6, :], G_A + HD))
                link(rope(qk[:, :, 0:A_H, :], cs64, [qa[:, :, :, :]]))
                rope(qk[:, :, A_H:6, :], cs64, [kad[:, :, :, 0, :], kad[:, :, :, 1, :]]).then_inc(prep, 1)
                dve.wait_ge(prep, prep_at(l, "qa"))
                copied(l, 3)
                cq = v4(pq, C_H)
                heads_rstd(cq, HD)
                by_rstd(cq, cq)
                gain(cq, G_C).then_inc(prep, 1)
                dve.wait_ge(prep, prep_at(l, "cq"))
                aux_wait(l, "gate")
                tt(gt[:, :, :], ps[:, aux_bank("gate"), 0:48].rearrange("p (t n) -> p t n", t=NT),
                   gn[:, G_GB:G_END].unsqueeze(1).broadcast_to([P, NT, 24]), ALU.add).then_inc(aux_dve, 1)
                dve.wait_ge(aux_done("gate", l)[0], aux_done("gate", l)[1])
                dve.wait_ge(*aux_done("w2", l))
                kc = kcn[0:NCMP, :, :].unsqueeze(2)
                heads_rstd(kc, HD)
                by_rstd(kc, kc)
                for dup in range(2):
                    i = gain(kc, G_C + HD, kcd[0:NCMP, :, dup, :].unsqueeze(2))
                i.then_inc(prep, 1)
                dve.wait_ge(gate_exp, l + 1)
                link(ts(gt[:, :, :], gt[:, :, :], 1.0, None, ALU.add))
                link(V.reciprocal(gt[:, :, :], gt[:, :, :]))
                rope(cq, cs64, [qr[:, :, :, :]]).then_inc(prep, 1)
                dve.wait_ge(prep, prep_at(l, "cr"))
                copied(l, 4)
                ck = v4(pk[:, :, 0:256], 4)
                heads_rstd(ck, HD)
                by_rstd(ck, ck)
                gain(ck[:, :, 0:2, :], G_C + 2 * HD)
                link(gain(ck[:, :, 2:4, :], G_C + 3 * HD))
                rope(ck, cs64, [krd[:, :, :, 0, :], krd[:, :, :, 1, :]]).then_inc(prep, 1)
                dve.wait_ge(prep, prep_at(l, "ck"))
                dve.wait_ge(*aux_done("uq1", l))
                qn, qp = qb[:, :, :, 0:HD], qb[:, :, :, HD:96]
                heads_rstd(qn, HD)
                by_rstd(qn, qn)
                gain(qn, G_BN)
                heads_rstd(qp, ROPE_B)
                by_rstd(qp, qp)
                link(gain(qp, G_BR))
                rope(qp, cs32, [qp]).then_inc(prep, 1)
                dve.wait_ge(prep, prep_at(l, "qb"))
                dve.wait_ge(*aux_done("ukv1", l))
                kn = kvb[:, :, :, 0:HD]
                heads_rstd(kn, HD)
                by_rstd(kn, kb[:, :, :, 0:HD])
                gain(kb[:, :, :, 0:HD], G_BN + HD).then_inc(prep, 1)
                out_of(l, "ka", kaT[:, :, :])
                out_of(l, "cq1", cqT[:, 2:4, :])
                aux_wait(l, "kc")
                V.tensor_copy(kcT[:, :, 0:NCMP], ps[:, aux_bank("kc"), 0:2 * P].rearrange("p (g b) -> p g b", g=2)
                              [:, :, 0:NCMP]).then_inc(aux_dve, 1)
                spread = lambda ap, n=C_H: ap.rearrange("p (t b) -> p t b", t=NT).unsqueeze(2)\
                    .broadcast_to([P, NT, n, NCMP])
                over = lambda r: cst16[:, r, :].rearrange("p (t n) -> p t n", t=NT)
                for odd in range(2):
                    aux_wait(l, f"cmps{odd}")
                    sv = ps[:, aux_bank(f"cmps{odd}"), 0:128].rearrange("p (t n b) -> p t n b", t=NT, b=16)
                    tt(csc[:, :, odd:C_H:2, :], sv[:, :, :, 0:NCMP], spread(cst[:, C_NEG:C_NEG + 30], C_H // 2),
                       ALU.add).then_inc(aux_dve, 1)
                dve.wait_ge(*aux_done("cmps1", l))
                link(V.tensor_reduce(over(0), csc, AX.X, ALU.max))
                tt(csc, csc, over(0).unsqueeze(3).broadcast_to([P, NT, C_H, NCMP]), ALU.subtract)\
                    .then_inc(cmp_shift, 1)
                out_of(l, "cr1", crT[:, 2:4, :])
                out_of(l, "kw", ckT[:, 2:4, :])
                out_of(l, "qb1", qbT[:, 2:4, :], 96)
                out_of(l, "kb1", kbT[:, 2:4, :], 96)
                dve.wait_ge(cmp_exp, l + 1)
                link(V.memset(cp, 0.0))
                link(V.tensor_reduce(over(1), csc, AX.X, ALU.add))
                link(V.reciprocal(over(1), over(1)))
                gates = gt[:, :, :].rearrange("p t (n g) -> p t n g", g=3)
                link(tt(over(2), over(1), gates[:, :, :, 0], ALU.mult))
                link(tt(csc, csc, spread(cst[:, C_VIS:C_VIS + 30]), ALU.mult))
                tt(cp[:, :, :, 0:NCMP], csc, over(2).unsqueeze(3).broadcast_to([P, NT, C_H, NCMP]), ALU.mult)\
                    .then_inc(prep, 1)
                aux_wait(l, "cmpt")
                V.tensor_copy(cmpT[:, :, :], ps[:, aux_bank("cmpt"), :].rearrange("p (b n) -> p b n", b=2))\
                    .then_inc(aux_dve, 1)
                for n in range(NJ + 4):
                    if n < NJ:
                        br, hh = JOBS[n]
                        st = stat[:, n % 4, :]
                        scale = job(n)[4]
                        bank = ps[:, n % 2, :]
                        dve.wait_ge(s_ready, l * NJ + (n + 1))
                        V.tensor_reduce(st[:, 0:1], bank[:, 0:P], AX.X, ALU.max)
                        link(V.tensor_reduce(st[:, 1:2], bank[:, P:3 * P], AX.X, ALU.max))
                        if br == "a":
                            sink = gn[:, G_SINK + hh:G_SINK + hh + 1].broadcast_to([P, 2])
                            link(stt(st[:, 0:2], st[:, 0:2], scale, sink, ALU.mult, ALU.max))
                            ts(st[:, 2:4], st[:, 0:2], -1.0, None, ALU.mult).then_inc(nm_ready, 1)
                        else:
                            ts(st[:, 2:4], st[:, 0:2], -scale, None, ALU.mult).then_inc(nm_ready, 1)
                    if 1 <= n <= NJ:
                        m = n - 1
                        br, hh = JOBS[m]
                        st = stat[:, m % 4, :]
                        dve.wait_ge(exp_ready, l * NJ + (m + 1))
                        if br == "a":
                            link(tt(st[:, 4:6], st[:, 4:6], st[:, 6:8], ALU.add))
                        link(V.reciprocal(st[:, 4:6], st[:, 4:6]))
                        if br in ("slc", "win"):
                            g = gates[:, :, hh, 1 if br == "slc" else 2]
                            link(tt(st[:, 4:6], st[:, 4:6], g, ALU.mult))
                        ts(E[:, m % 3, 0:P], E[:, m % 3, 0:P], st[:, 4:5], None, ALU.mult)
                        ts(E[:, m % 3, P:3 * P], E[:, m % 3, P:3 * P], st[:, 5:6], None, ALU.mult)\
                            .then_inc(en_ready, 1)
                    if n - 4 in LAST:
                        pair = LAST.index(n - 4)
                        dve.wait_ge(pv_ready, l * NJ + (n - 3))
                        V.tensor_copy(u[:, pair, :], ps[:, 3, 0:SEQ]).then_inc(o_ready, 1)
                residual(l, 1, TALL_M + 3)

            with dve.Fori(0, DEPTH) as l:
                chain["base"], chain["n"] = l * CHAIN_L + CHAIN_PRO, 0
                ffn(l, 0)
                mixer(l)
                ffn(l, 1)
                assert chain["n"] == CHAIN_L, chain


_INS = ["x", "c", "positions", "ada_w", "ada_b", "norm_g", "ffn_w_in", "ffn_w_out", "w_in", "w_out",
        "a_sinks", "a_qk_g", "b_q_lat_g", "b_kv_lat_g", "b_w_uq", "b_w_ukv", "b_qk_nope_g", "b_qk_rope_g",
        "c_qk_g", "c_cmp_pe", "c_cmp_w1", "c_cmp_w2", "c_gate_w", "c_gate_b"]


def shape_constants():
    t = np.zeros((P, C_END), np.float32)
    q, k = np.arange(P)[:, None], np.arange(P)[None, :]
    t[:, C_ID:C_ID + P] = q == k
    t[:, C_CAUSAL:C_CAUSAL + P] = np.where(k > q, NEG, 0.0)
    t[:, C_BAND:C_BAND + P] = np.where(k <= q, NEG, 0.0)
    for lo, dim in ((0, HD), (HD // 2, ROPE_B)):
        power = np.arange(0, dim, 2, dtype=np.float32) / np.float32(dim)
        t[:, C_INVF + lo:C_INVF + lo + dim // 2] = np.float32(1.0) / np.power(np.float32(10000.0), power)
    for i in range(NT):
        seen = np.arange(NCMP)[None, :] * 16 + CL - 1 <= i * P + q
        t[:, C_NEG + i * NCMP:C_NEG + (i + 1) * NCMP] = np.where(seen, 0.0, NEG)
        t[:, C_VIS + i * NCMP:C_VIS + (i + 1) * NCMP] = seen
    return t


def kernel(**inputs):
    import concourse.bacc as _bacc
    from concourse.bass_utils import run_bass_kernel_spmd as _run

    nc = _bacc.Bacc("TRN2", target_bir_lowering=False, num_devices=1)
    arrays, args = {}, []
    for name in _INS + ["consts"]:
        a = np.ascontiguousarray(inputs[name] if name != "consts" else shape_constants())
        arrays[f"in_{name}_dram"] = a
        args.append(nc.dram_tensor(f"in_{name}_dram", a.shape, mybir.dt.from_np(a.dtype), kind="ExternalInput").ap())
    out = nc.dram_tensor("out_0_dram", (1, SEQ, DM), F32, kind="ExternalOutput").ap()
    hybrid_kernel(nc, *args, out)
    r = _run(nc, [arrays], core_ids=[0])
    return r.results[0]["out_0_dram"]
```

```python
from contextlib import ExitStack

import numpy as np

import concourse.bass as bass
from concourse import mybir

F32 = mybir.dt.float32
F32R = mybir.dt.float32r
BF16 = mybir.dt.bfloat16
I32 = mybir.dt.int32
ALU = mybir.AluOpType
ACT = mybir.ActivationFunctionType
AX = mybir.AxisListType

P = 128
DEPTH = 2
SEQ = 256
NT = SEQ // P
DM = 1024
KD = DM // P
NMOD = 9
DFF = 2816
NPAIR = DFF // (2 * P)
EPS = 1e-6
NEG = -1e30
HD = 64
ROPE_B = 32
A_H, A_KV = 4, 2
B_H = 4
C_H, C_KV = 8, 2
NCMP = SEQ // 16 - 1
CL = 32
SC64 = float(HD) ** -0.5
SC96 = float(HD + ROPE_B) ** -0.5

C_ID, C_CAUSAL, C_BAND, C_INVF, C_NEG, C_VIS = 0, 128, 256, 384, 432, 462
C_END = 492

G_A, G_C, G_BN, G_BR, G_SINK, G_GB, G_END = 0, 128, 384, 512, 576, 580, 604

WIDE_A, WIDE_M, WIDE_B, WIDE = 0, NPAIR, NPAIR + 6, 2 * NPAIR + 6
TALL_A, TALL_M, TALL_B, TALL = 0, NPAIR, NPAIR + 4, 2 * NPAIR + 4
F_LAT, F_CMPIN, F_A, F_CMPW, F_CQ, F_CK = range(6)
CHUNKS = (F_LAT, F_CMPIN, F_A, F_CQ, F_CK)

AUX = [("zk", "dve"), ("zv", "dve"), ("lat", "dve"), ("kvgf", "act"), ("hid", "act"), ("uq0", "act"),
       ("uq1", "act"), ("w2", "act"), ("gate", "dve"), ("ukv0", "act"), ("ukv1", "act"),
       ("qa", "act"), ("ka", "dve"), ("cq0", "act"), ("cq1", "dve"), ("kc", "dve"), ("cmps0", "dve"), ("cmps1", "dve"),
       ("cr0", "act"), ("cr1", "dve"), ("ks", "act"), ("kw", "dve"),
       ("qb0", "act"), ("qb1", "dve"), ("kb0", "act"), ("kb1", "dve"), ("cmpt", "dve")]
AUXN = [n for n, _ in AUX]
AUX_ACT = sum(e == "act" for _, e in AUX)
AUX_DVE = sum(e == "dve" for _, e in AUX)

JOBS = [("a", h) for h in range(A_H)] + [("b", h) for h in range(B_H)]
JOBS += [(br, h) for h in range(C_H) for br in ("slc", "win")]
NJ = len(JOBS)
LAST = [n for n in range(NJ) if JOBS[n][1] % 2 and (n + 1 == NJ or JOBS[n + 1][1] != JOBS[n][1])]

ADA_PRO = KD
ADA_L = 4 * KD
PRO_BANKS = (0, 1, 4, 5, 6, 7)


def hybrid_kernel(nc, x, c, positions, ada_w, ada_b, norm_g, ffn_w_in, ffn_w_out, w_in, w_out,
                  a_sinks, a_qk_g, b_q_lat_g, b_kv_lat_g, b_w_uq, b_w_ukv, b_qk_nope_g, b_qk_rope_g,
                  c_qk_g, c_cmp_pe, c_cmp_w1, c_cmp_w2, c_gate_w, c_gate_b, consts, out):
    with ExitStack() as ctx:
        def sb(name, shape, dt=F32):
            return ctx.enter_context(nc.sbuf_tensor(name, shape, dt))

        def sem(name):
            return ctx.enter_context(nc.semaphore(name))

        h = sb("h", [P, KD, SEQ])
        wide = sb("wide", [P, 2, KD * 512])
        tall = sb("tall", [P, 2, 2 * DM])
        ada = sb("ada", [P, 2, 3 * DM])
        fs = sb("fs", [P, 2, SEQ])
        fa = sb("fa", [P, 2, SEQ])
        ARENA = 13440
        SHARED0 = nc.sbuf_base
        A_U, A_SQ, A_ACC, A_MIX = 0, 2048, 4096, 4096 + 6 * DM
        shared = sb("shared", [P, A_MIX + ARENA])

        def at(name, shape, off, dt=F32):
            return nc.alloc_sbuf_tensor_at(name, shape, dt, offset=SHARED0 + 4 * off)

        u = at("u", [P, KD, SEQ], A_U)
        uh = at("uh", [P, KD, SEQ], A_U, F32R)
        sq = at("sq", [P, KD * SEQ], A_SQ)
        ul = at("ul", [P, KD, SEQ], A_SQ, F32R)
        acc = at("acc", [P, 6 * DM], A_ACC)
        ol = at("ol", [P, KD, SEQ], A_ACC, F32R)
        th = at("th", [P, 2, DM], A_MIX, F32R)
        tl = at("tl", [P, 2, DM], A_MIX + 2048, F32R)
        wh = at("wh", [P, 2, 2, KD, P], A_MIX + 4096, F32R)
        wl = at("wl", [P, 2, 2, KD, P], A_MIX + 8192, F32R)
        fh = at("fh", [P, 2, SEQ], A_MIX + 12288, F32R)
        fl = at("fl", [P, 2, SEQ], A_MIX + 12800, F32R)
        cst = sb("cst", [P, C_END])
        idb = sb("idb", [P, P], BF16)
        mcausal = sb("mcausal", [P, 3 * P], BF16)
        mband = sb("mband", [P, 3 * P], BF16)
        zb = sb("zb", [P, 512], BF16)
        ones = sb("ones", [P, P])
        rows = sb("rows", [P, 3, P])
        vt = sb("vt", [P, 3, P])
        cond = sb("cond", [P, KD])
        mod = sb("mod", [P, 3, 3, KD])
        posi = sb("posi", [P, NT], I32)
        posf = sb("posf", [P, NT])
        cs64 = sb("cs64", [P, 2, NT, HD])
        cs32 = sb("cs32", [P, 2, NT, ROPE_B])
        small = sb("small", [P, 64])
        newt_i = sb("newt_i", [P, 32], I32)
        newt = sb("newt", [P, 32])
        ssb = sb("ssb", [P, 32])
        rst = sb("rst", [P, 32])
        gn = sb("gn", [P, G_END])
        uq = sb("uq", [P, 2, 384])
        ukv = sb("ukv", [P, 512])
        w2 = sb("w2", [P, 2, HD])
        gw = sb("gw", [HD, 24])
        plat = acc[:, 0:832].rearrange("p (t n) -> p t n", t=NT)
        pz = acc[:, 832:1856].rearrange("p (t a d n) -> p t a d n", t=NT, a=4, d=2)
        pgf = acc[:, 1856:1984].rearrange("p (t n) -> p t n", t=NT)
        pq = acc[:, 1984:3008].rearrange("p (t n) -> p t n", t=NT)
        pa = acc[:, 3008:4032].rearrange("p (t n) -> p t n", t=NT)
        pk = acc[:, 4032:5056].rearrange("p (t n) -> p t n", t=NT)
        zc = acc[:, 5056:6016].rearrange("p (a h m b) -> p a h m b", a=2, h=2, m=CL // 2)
        qa = at("qa", [P, NT, A_H, HD], A_MIX + 0)
        kad = at("kad", [P, NT, A_KV, 2, HD], A_MIX + 512)
        qr = at("qr", [P, NT, C_H, HD], A_MIX + 1024)
        krd = at("krd", [P, NT, 4, 2, HD], A_MIX + 2048)
        qb = at("qb", [P, NT, B_H, 96], A_MIX + 3072)
        kvb = at("kvb", [P, NT, B_H, P], A_MIX + 6656)
        kb = at("kb", [P, NT, B_H, 96], A_MIX + 3840)
        latT = at("latT", [P, 3, SEQ], A_MIX + 4608)
        gfT = at("gfT", [HD, SEQ], A_MIX + 5376)
        qaT = at("qaT", [P, 2, SEQ], A_MIX + 7680)
        kaT = at("kaT", [P, 2, SEQ], A_MIX + 8192)
        cqT = at("cqT", [P, 4, SEQ], A_MIX + 5632)
        crT = at("crT", [P, 4, SEQ], A_MIX + 8704)
        ckT = at("ckT", [P, 4, SEQ], A_MIX + 9728)
        qbT = at("qbT", [96, B_H, SEQ], A_MIX + 10752)
        kbT = at("kbT", [96, B_H, SEQ], A_MIX + 11776)
        hidk = sb("hidk", [P, 2, 16])
        hidv = sb("hidv", [P, 2, 4, 32])
        kcn = sb("kcn", [16, 2, HD])
        kcd = sb("kcd", [P, 2, 2, HD])
        kcT = sb("kcT", [P, 2, P])
        vrep = at("vrep", [P, 2, HD], A_MIX + 13312)
        gt = sb("gt", [P, NT, 24])
        latg = sb("latg", [P, 3])
        pe2 = sb("pe2", [P, 32])
        cmpT = at("cmpT", [P, 2, SEQ], A_MIX + 12800)
        msum = sb("msum", [P, 48])
        stat = sb("stat", [P, 4, 8])
        E = sq[:, 0:1152].rearrange("p (r n) -> p r n", r=3)
        ET = sq[:, 1152:1920].rearrange("p (r n) -> p r n", r=2)
        T1 = sq[:, 0:1024]
        T2 = sq[:, 1024:2048]
        cp = fs[:, :, :].rearrange("p a (h b) -> p a h b", h=C_H)
        csc = fa[:, :, 0:C_H * NCMP].rearrange("p a (h b) -> p a h b", h=C_H)
        trg = cqT[:, 0:2, :].rearrange("p a n -> p (a n)")
        cst16 = sb("cst16", [P, 3, NT * C_H])

        ps = ctx.enter_context(nc.psum_tensor("ps", [P, 8, 512], F32))
        y = ps[:, 4:8, :].rearrange("p b (e n) -> p (b e) n", e=2)

        s_const, s_pos, s_x, s_rows, s_small = (sem(n) for n in ("const", "pos", "xin", "rows", "smallw"))
        wide_in = [sem("wide_in0"), sem("wide_in1")]
        tall_in = [sem("tall_in0"), sem("tall_in1")]
        ada_in = [sem("ada_in0"), sem("ada_in1")]
        wide_used, tall_used, ada_used = sem("wide_used"), sem("tall_used"), sem("ada_used")
        setup, turned, cond_ok, trig, trig_in = (sem(n) for n in ("setup", "turned", "cond", "trig", "trigin"))
        h_ready, sq_ready, ss_ready, diag_ready, r_ready = (
            sem(n) for n in ("h_ready", "sq_ready", "ss_ready", "diag_ready", "r_ready"))
        hn_ready, u_ready = sem("hn_ready"), sem("u_ready")
        gu_ready, silu_ready, mul_ready, y_ready = (
            sem(n) for n in ("gu_ready", "silu_ready", "mul_ready", "y_ready"))
        ul_ready, wh_ready, wl_ready, th_ready, tl_ready, mix_done = (
            sem(n) for n in ("ul_ready", "wh_ready", "wl_ready", "th_ready", "tl_ready", "mix_done"))
        acc_zero, acc_ready, mod_ps, mod_red, mod_ready = (
            sem(n) for n in ("acc_zero", "acc_ready", "mod_ps", "mod_red", "mod_ready"))
        proj, pcopy, aux_ready, aux_act, aux_dve = (
            sem(n) for n in ("proj", "pcopy", "aux_ready", "aux_act", "aux_dve"))
        prep, fa_s, fh_s, oh_s = sem("prep"), sem("fa"), sem("fh"), sem("oh")
        cmp_shift, cmp_exp = sem("cmp_shift"), sem("cmp_exp")
        gate_exp, mod_lat = sem("gate_exp"), sem("mod_lat")
        s_ready, nm_ready, exp_ready, en_ready, pt_ready, et_ready, pv_ready, o_ready = (
            sem(n) for n in ("s_ready", "nm_ready", "exp_ready", "en_ready", "pt_ready", "et_ready",
                             "pv_ready", "o_ready"))
        out_ps, out_sb, s_out = sem("out_ps"), sem("out_sb"), sem("out")
        chain_s = sem("chain")

        ident = cst[:, C_ID:C_ID + P]

        def wide_wait(eng, l, n):
            eng.wait_ge(wide_in[n % 2], l * (WIDE // 2 * 32) + 32 * (n // 2 + 1))

        def tall_wait(eng, l, n):
            eng.wait_ge(tall_in[n % 2], l * (TALL // 2 * 16) + 16 * (n // 2 + 1))

        PREP = ["lat", "qa", "cq", "kc", "cr", "ck", "qb", "kb", "cmp"]

        def landed(l, it, n0, per_layer, loads):
            return l * (per_layer // 2 * loads) + loads * ((n0 + it[0]) // 2 + 1) + loads * it[1]

        def tile_at(l, f, m, i=0):
            return l * (4 * NPAIR) + (2 * NPAIR * f + m + 1) + 4 * i

        def rows_at(l, j, m, i=0):
            return l * (4 * NPAIR + KD) + ((0, 2 * NPAIR, 2 * NPAIR + KD)[j] + m + 1) + 4 * i

        def prep_at(l, name):
            return l * len(PREP) + PREP.index(name) + 1

        def aux_bank(name):
            return 4 + AUXN.index(name) % 4

        def aux_done(name, l):
            g = AUXN.index(name)
            who = AUX[g][1]
            count = sum(e == who for _, e in AUX[:g + 1])
            return (aux_act, l * AUX_ACT + count) if who == "act" else (aux_dve, l * AUX_DVE + count)

        def aux_at(l, name):
            return l * len(AUX) + AUXN.index(name) + 1

        def job(n):
            br, hh = JOBS[n]
            half = slice(64 * (hh % 2), 64 * (hh % 2) + 64)
            if br == "a":
                return (qaT[half, hh // 2, :], kaT[half, hh // 2, :],
                        lambda t: pa[:, t, 384 + hh // 2 * HD:384 + hh // 2 * HD + HD], mband, SC64)
            if br == "b":
                return qbT[:, hh, :], kbT[:, hh, :], lambda t: kvb[:, t, hh, HD:P], mcausal, SC96
            win = int(br == "win")
            kv = hh // 4
            off = 256 + 128 * win + kv * HD
            return (crT[half, hh // 2, :], ckT[half, 2 * win + kv, :],
                    lambda t: pk[:, t, off:off + HD], mcausal, SC64)

        block = ctx.enter_context(nc.Block())

        @block.sync
        def _(sp):
            def fill_wide(l, n, loads):
                sp.wait_ge(wide_used, l * WIDE + n + 1)
                for dst, src in loads:
                    sp.dma_start(dst, src).then_inc(wide_in[n % 2], 16)

            def fill_tall(l, n, src):
                sp.wait_ge(tall_used, l * TALL + n + 1)
                sp.dma_start(tall[:, n % 2, :].rearrange("p (a n) -> p a n", a=2), src)\
                    .then_inc(tall_in[n % 2], 16)

            def fill_ada(count, slot, width, src):
                sp.wait_ge(ada_used, count + 1)
                sp.dma_start(ada[:, slot, 0:width], src).then_inc(ada_in[slot], 16)

            def ffn_pair(l, f, it, q, ada_row=None):
                n0, m0 = (WIDE_A, TALL_A) if f == 0 else (WIDE_B, TALL_B)
                ws, ts = (n0 + q) % 2, (m0 + q) % 2
                slot = wide[:, ws, :].rearrange("p (e k n) -> p e k n", e=2, k=KD)
                sp.wait_ge(wide_used, l * WIDE + n0 + it + 1)
                for e in range(2):
                    src = ffn_w_in[l, f, :, bass.ds(e * DFF + it * 256, 256)].rearrange(
                        "(k p) n -> p k n", p=P)
                    sp.dma_start(slot[:, e, :, :], src).then_inc(wide_in[ws], 16)
                if ada_row is not None:
                    ada_piece(l, f, ada_row, 0)
                sp.wait_ge(tall_used, l * TALL + m0 + it + 1)
                src = ffn_w_out[l, f, bass.ds(it * 256, 256), :].rearrange("(a p) n -> p a n", p=P)
                sp.dma_start(tall[:, ts, :].rearrange("p (a n) -> p a n", a=2), src).then_inc(tall_in[ts], 16)
                if ada_row is not None:
                    ada_piece(l, f, ada_row, 1)

            def ada_piece(l, f, i, e):
                count = l * ADA_L + (ADA_PRO + f * 2 * KD + e) + 2 * i
                if f == 0:
                    src = ada_w[l, bass.ds(i * P, P), 3 * DM * (e + 1):3 * DM * (e + 2)]
                    fill_ada(count, e, 3 * DM, src)
                else:
                    src = ada_w[DEPTH - 1, bass.ds(i * P, P), 1536 * e:1536 * (e + 1)]
                    fill_ada(count, e, 1536, src)

            def ffn(l, f):
                ffn_pair(l, f, 0, 0)
                with sp.Fori(0, KD // 2) as i:
                    for q in range(2):
                        ffn_pair(l, f, 2 * i + q + 1, (q + 1) % 2, 2 * i + q)
                for it in range(KD + 1, NPAIR):
                    ffn_pair(l, f, it, it % 2)

            for k in range(ADA_PRO):
                fill_ada(k, k % 2, 3 * DM, ada_w[0, k * P:(k + 1) * P, 0:3 * DM])
            with sp.Fori(0, DEPTH) as l:
                bc = lambda ap: ap.partition_broadcast(P)
                for lo, hi, src in ((G_A, G_C, a_qk_g[l].rearrange("a b -> (a b)")),
                                    (G_C, G_BN, c_qk_g[l].rearrange("a b -> (a b)")),
                                    (G_BN, G_BR, b_qk_nope_g[l].rearrange("a b -> (a b)")),
                                    (G_BR, G_SINK, b_qk_rope_g[l].rearrange("a b -> (a b)")),
                                    (G_SINK, G_GB, a_sinks[l]), (G_GB, G_END, c_gate_b[l])):
                    sp.dma_start(gn[:, lo:hi], bc(src)).then_inc(s_small, 16)
                sp.dma_start(uq[:, :, :], b_w_uq[l].rearrange("(k p) n -> p k n", p=P)).then_inc(s_small, 16)
                sp.dma_start(ukv[:, :], b_w_ukv[l]).then_inc(s_small, 16)
                sp.dma_start(w2[:, :, :], c_cmp_w2[l].rearrange("a p n -> p a n")).then_inc(s_small, 16)
                sp.dma_start(gw[:, :], c_gate_w[l]).then_inc(s_small, 16)
                ffn(l, 0)

                def cols(n, off, lo, hi, rest=None):
                    width = rest or hi - lo
                    slot = wide[:, n % 2, 0:KD * width].rearrange("p (k n) -> p k n", k=KD)
                    return slot[:, :, off:off + hi - lo], w_in[l, :, lo:hi].rearrange("(k p) n -> p k n", p=P)

                n = WIDE_M
                fill_wide(l, n, [cols(n, 0, 512, 720, 416), cols(n, 208, 720, 928, 416)])
                n += 1
                fill_wide(l, n, [cols(n, 0, 1440, 1696, 320), cols(n, 256, 2208, 2272, 320)])
                n += 1
                fill_wide(l, n, [cols(n, 256, 256, 512, 512), cols(n, 0, 0, 256, 512)])
                fill_tall(l, TALL_M, w_out[l, 0:256, :].rearrange("(a p) n -> p a n", p=P))
                n += 1
                w1 = wide[:, n % 2, :].rearrange("p (m n) -> p m n", n=P)
                w1_src = c_cmp_w1[l].rearrange("a (m p) n -> p (a m) n", p=P)
                fill_wide(l, n, [(w1[r:r + 64, :, :], w1_src[r:r + 64, :, :]) for r in (0, 64)])
                n += 1
                fill_wide(l, n, [cols(n, 0, 928, 1184, 512), cols(n, 256, 1184, 1440, 512)])
                n += 1
                fill_wide(l, n, [cols(n, 0, 1696, 1952, 512), cols(n, 256, 1952, 2208, 512)])
                for m in range(1, 4):
                    fill_tall(l, TALL_M + m, w_out[l, m * 256:(m + 1) * 256, :].rearrange("(a p) n -> p a n", p=P))
                ffn(l, 1)
            o = u[:, :, :].rearrange("p (t j) n -> p t (j n)", t=NT)
            for t in range(NT):
                sp.wait_ge(out_sb, 2 * t + 2)
                sp.dma_start(out[0, t * P:(t + 1) * P, :], o[:, t, :]).then_inc(s_out, 16)
            sp.wait_ge(s_out, 16 * NT)

        @block.tensor
        def _(pe):
            mm, tr = nc.tensor.matmul, nc.tensor.transpose

            def norm_stats(l, j):
                for k in range(KD):
                    pe.wait_ge(sq_ready, l * 24 + (8 * j + k + 1))
                    for t in range(NT):
                        i = mm(ps[:, 2 + t, 0:1], sq[:, k * SEQ + t * P:k * SEQ + t * P + P], ones[:, 0:1],
                               start=(k == 0), stop=(k == KD - 1))
                i.then_inc(ss_ready, 1)
                pe.wait_ge(diag_ready, l * 3 + (j + 1))
                for t in range(NT):
                    i = mm(ps[:, 2, t * P:(t + 1) * P], ones[:, :], T1[:, t * P:(t + 1) * P], start=True, stop=True)
                i.then_inc(r_ready, 1)

            def open_y():
                for b in range(4):
                    i = mm(ps[:, 4 + b, :], zb[:, 0:P], zb[:, :], start=True, stop=False, skip_group_check=True)

            def gate_up(l, f, m, i=0):
                a = m % 2
                for e in range(2):
                    o = ps[:, a, e * SEQ:(e + 1) * SEQ]
                    for part in range(3):
                        w, v = (wl if part == 2 else wh), (ul if part == 1 else uh)
                        for k in range(KD):
                            if m == 0 and e == 0:
                                if part == 0 and k == 0:
                                    pe.wait_ge(wh_ready, tile_at(l, f, 0))
                                if part == 0:
                                    pe.wait_ge(u_ready, l * 24 + (16 * f + k + 1))
                                if part == 1:
                                    pe.wait_ge(ul_ready, l * 16 + (8 * f + k + 1))
                                if part == 2 and k == 0:
                                    pe.wait_ge(wl_ready, tile_at(l, f, 0))
                            elif e == 0 and part == 0 and k == 0:
                                pe.wait_ge(wl_ready, tile_at(l, f, m, i))
                            q = mm(o, w[:, a, e, k, :], v[:, k, :], start=(part == 0 and k == 0),
                                   stop=(part == 2 and k == KD - 1))
                q.then_inc(gu_ready, 1)

            def add_rows(a, hi, lo, last, done=None):
                for d in range(KD):
                    cols = slice(d * P, (d + 1) * P)
                    mm(y[:, d, :], th[:, a, cols], hi, start=False, stop=False, skip_group_check=True)
                    mm(y[:, d, :], th[:, a, cols], lo, start=False, stop=False, skip_group_check=True)
                    i = mm(y[:, d, :], tl[:, a, cols], hi, start=False, stop=False, skip_group_check=True)
                    if last and d % 2:
                        i.then_inc(y_ready, 1)
                    elif done is not None and d == KD - 1:
                        i.then_inc(done, 1)

            def down(l, f, m, i=0):
                a = m % 2
                pe.wait_ge(tl_ready, rows_at(l, 2 * f, m, i))
                pe.wait_ge(mul_ready, tile_at(l, f, m, i))
                add_rows(a, fh[:, a, :], fl[:, a, :], m == 2 * NPAIR - 1)

            def sum_parts(l, f, r):
                if r == 0:
                    pe.wait_ge(acc_ready, l * 2 + (f + 2))
                if r >= 2:
                    pe.wait_ge(mod_red, l * 18 + (12 * f + r - 1))
                for v in range(4):
                    i = tr(ps[:, 2 + r % 2, v * P:(v + 1) * P], acc[:, (4 * r + v) * P:(4 * r + v + 1) * P], ident)
                i.then_inc(mod_ps, 1)

            def ffn(l, f):
                norm_stats(l, 2 * f)
                open_y()
                gate_up(l, f, 0)
                with pe.Fori(0, KD // 2) as i:
                    for q in range(4):
                        gate_up(l, f, q + 1, i)
                        down(l, f, q, i)
                for m in range(2 * KD, 2 * NPAIR):
                    if m + 1 < 2 * NPAIR:
                        gate_up(l, f, m + 1)
                    for r in range(2 * (m - 2 * KD), 2 * (m - 2 * KD) + 2):
                        if r < 12 - 6 * f:
                            sum_parts(l, f, r)
                    down(l, f, m)

            def aux_open(l, name):
                g = AUXN.index(name)
                if g >= 4:
                    pe.wait_ge(*aux_done(AUXN[g - 4], l))
                return ps[:, 4 + g % 4, :]

            def project(l, fill, width, banks):
                n = WIDE_M + fill
                wv = wide[:, n % 2, 0:KD * width].rearrange("p (k n) -> p k n", k=KD)
                wide_wait(pe, l, n)
                c = CHUNKS.index(fill)
                if c >= 2:
                    pe.wait_ge(pcopy, l * 2 * len(CHUNKS) + 2 * (c - 1))
                for t in range(NT):
                    for k in range(KD):
                        if fill == F_LAT and t == 0:
                            pe.wait_ge(u_ready, l * 24 + (8 + k + 1))
                        i = mm(ps[:, banks + t, 0:width], u[:, k, t * P:(t + 1) * P], wv[:, k, :],
                               start=(k == 0), stop=(k == KD - 1))
                    i.then_inc(proj, 1)

            def turn(l, name, blocks):
                bank = aux_open(l, name)
                for col, src in blocks:
                    rows_, width = src.shape[0], src.shape[-1]
                    i = tr(bank[0:width, col:col + rows_], src, ident[0:rows_, 0:rows_])
                i.then_inc(aux_ready, 1)

            def scores(l, n):
                q, k, _, mask, _ = job(n)
                bank = ps[:, n % 2, 0:3 * P]
                if n >= 2:
                    pe.wait_ge(exp_ready, l * NJ + (n - 1))
                mm(bank, idb[:, :], mask[:, :], start=True, stop=False, skip_group_check=True)
                mm(bank[:, 0:P], q[:, 0:P], k[:, 0:P], start=False, stop=False, skip_group_check=True)
                mm(bank[:, P:3 * P], q[:, P:2 * P], k[:, :], start=False, stop=True,
                   skip_group_check=True).then_inc(s_ready, 1)

            def turn_probs(l, n):
                pe.wait_ge(en_ready, l * NJ + (n + 1))
                if n >= 1:
                    pe.wait_ge(et_ready, l * NJ + n)
                for b in range(3):
                    i = tr(ps[:, 2, b * P:(b + 1) * P], E[:, n % 3, b * P:(b + 1) * P], ident)
                i.then_inc(pt_ready, 1)

            def values(l, n):
                _, _, v, _, _ = job(n)
                br, hh = JOBS[n]
                o = ps[64 * (hh % 2):64 * (hh % 2) + 64, 3, 0:SEQ]
                pair = sum(m < n for m in LAST)
                first = n == 0 or JOBS[n - 1][1] != hh
                if first and hh % 2 == 0 and pair:
                    pe.wait_ge(o_ready, l * 8 + pair)
                pe.wait_ge(et_ready, l * NJ + (n + 1))
                mm(o, v(0), ET[:, n % 2, 0:SEQ], start=first, stop=False, skip_group_check=True)
                i = mm(o[:, P:SEQ], v(1), ET[:, n % 2, SEQ:3 * P], start=False, stop=False, skip_group_check=True)
                if br == "win":
                    r = slice(32 * (hh % 4), 32 * (hh % 4) + 32)
                    if hh == 0:
                        pe.wait_ge(*aux_done("cmpt", l))
                    i = mm(o, vrep[r, hh // 4, :], cmpT[r, hh // 4, :], start=False, stop=True, skip_group_check=True)
                i.then_inc(pv_ready, 1)

            def mix_out(l, k):
                if k == 0:
                    pe.wait_ge(*aux_done("kb0", l))
                    pe.wait_ge(*aux_done("cmpt", l))
                    open_y()
                pe.wait_ge(tl_ready, rows_at(l, 1, k))
                pe.wait_ge(o_ready, l * 8 + (k + 1))
                add_rows(k % 2, uh[:, k, :], ol[:, k, :], k == KD - 1, mix_done)

            def mixer(l):
                norm_stats(l, 1)
                project(l, F_LAT, 416, 0)
                project(l, F_CMPIN, 320, 2)
                project(l, F_A, 512, 0)
                pe.wait_ge(pcopy, l * 10 + 4)
                for a, name in enumerate(("zk", "zv")):
                    turn(l, name, [(hh * SEQ + t * P, pz[:, t, 2 * a + hh, :, :].rearrange("p d n -> p (d n)"))
                                   for hh in range(2) for t in range(NT)])
                pe.wait_ge(prep, prep_at(l, "lat"))
                turn(l, "lat", [(b * SEQ + t * P, plat[:, t, b * P:(b + 1) * P]) for b in range(2) for t in range(NT)])
                turn(l, "kvgf", [(t * P, plat[:, t, 256:384]) for t in range(NT)]
                     + [(SEQ + t * P, pgf[:, t, :]) for t in range(NT)])
                n = WIDE_M + F_CMPW
                w1 = wide[:, n % 2, :].rearrange("p (a m n) -> p a m n", a=2, m=CL // 2)
                bank = aux_open(l, "hid")
                pe.wait_ge(*aux_done("zv", l))
                wide_wait(pe, l, n)
                for a in range(2):
                    for m in range(CL // 2):
                        i = mm(bank[:, 32 * a:32 * a + 2 * NCMP], w1[:, a, m, :], zc[:, a, :, m, :],
                               start=(m == 0), stop=(m == CL // 2 - 1))
                i.then_inc(aux_ready, 1)
                project(l, F_CQ, 512, 2)
                pe.wait_ge(*aux_done("lat", l))
                pe.wait_ge(*aux_done("kvgf", l))
                pe.wait_ge(s_small, (l + 1) * 160)
                for t in range(NT):
                    bank = aux_open(l, f"uq{t}")
                    for k in range(2):
                        i = mm(bank[:, 0:384], latT[:, k, t * P:(t + 1) * P], uq[:, k, :], start=(k == 0), stop=(k == 1))
                    i.then_inc(aux_ready, 1)
                bank = aux_open(l, "w2")
                pe.wait_ge(*aux_done("hid", l))
                for g in range(2):
                    mm(bank[0:NCMP, g * HD:(g + 1) * HD], hidk[:, g, 0:NCMP], w2[:, 0, :], start=True, stop=True)
                for g in range(2):
                    i = mm(bank[:, (2 + g) * HD:(3 + g) * HD], hidv[:, g, :, :].rearrange("p r b -> p (r b)"),
                           w2[:, 1, :], start=True, stop=True)
                i.then_inc(aux_ready, 1)
                bank = aux_open(l, "gate")
                for t in range(NT):
                    i = mm(bank[:, t * 24:(t + 1) * 24], gfT[:, t * P:(t + 1) * P], gw[:, :], start=True, stop=True)
                i.then_inc(aux_ready, 1)
                project(l, F_CK, 512, 0)
                for t in range(NT):
                    bank = aux_open(l, f"ukv{t}")
                    mm(bank, latT[:, 2, t * P:(t + 1) * P], ukv[:, :], start=True, stop=True).then_inc(aux_ready, 1)

                def pairs(name, src, heads):
                    turn(l, name, [(b * SEQ + t * P, src[:, t, 2 * hp:2 * hp + 2, :].rearrange("p a n -> p (a n)"))
                                   for b, hp in enumerate(heads) for t in range(NT)])

                def doubled(name, src, g0):
                    turn(l, name, [(b * SEQ + t * P, src[:, t, g0 + b, :, :].rearrange("p a n -> p (a n)"))
                                   for b in range(2) for t in range(NT)])

                pe.wait_ge(prep, prep_at(l, "qa"))
                pairs("qa", qa, (0, 1))
                doubled("ka", kad, 0)
                cq = pq[:, :, :].rearrange("p t (a n) -> p t a n", a=C_H)
                pe.wait_ge(prep, prep_at(l, "cq"))
                pairs("cq0", cq, (0, 1))
                pairs("cq1", cq, (2, 3))
                pe.wait_ge(prep, prep_at(l, "kc"))
                turn(l, "kc", [(P * g, kcd[:, g, :, :].rearrange("p a n -> p (a n)")) for g in range(2)])
                pe.wait_ge(*aux_done("cq0", l))
                pe.wait_ge(*aux_done("cq1", l))
                pe.wait_ge(*aux_done("kc", l))
                for odd in range(2):
                    bank = aux_open(l, f"cmps{odd}")
                    half = slice(64 * odd, 64 * odd + 64)
                    for t in range(NT):
                        for hp in range(C_H // 2):
                            col = (t * C_H // 2 + hp) * 16
                            i = mm(bank[:, col:col + NCMP], cqT[half, hp, t * P:(t + 1) * P],
                                   kcT[half, hp // 2, 0:NCMP], start=True, stop=True)
                    i.then_inc(aux_ready, 1)
                pe.wait_ge(prep, prep_at(l, "cr"))
                pairs("cr0", qr, (0, 1))
                pairs("cr1", qr, (2, 3))
                pe.wait_ge(prep, prep_at(l, "ck"))
                doubled("ks", krd, 0)
                doubled("kw", krd, 2)
                for nm, src in (("qb", qb), ("kb", kb)):
                    pe.wait_ge(prep, prep_at(l, nm))
                    for g in range(2):
                        turn(l, f"{nm}{g}", [(b * SEQ + t * P, src[:, t, 2 * g + b, :]) for b in range(2)
                                             for t in range(NT)])
                pe.wait_ge(prep, prep_at(l, "cmp"))
                turn(l, "cmpt", [(g * SEQ + t * P, cp[:, t, 4 * g:4 * g + 4, :].rearrange("p a n -> p (a n)"))
                                 for g in range(2) for t in range(NT)])
                pe.wait_ge(*aux_done("kb0", l))
                pe.wait_ge(*aux_done("kb1", l))
                for n in range(NJ + 3):
                    if n < NJ:
                        scores(l, n)
                    if 0 <= n - 2 < NJ:
                        turn_probs(l, n - 2)
                    if n >= 3:
                        values(l, n - 3)
                    for k in range(KD):
                        if n == min(LAST[k] + 5, NJ + 2):
                            mix_out(l, k)

            pe.wait_ge(setup, 1)
            pe.wait_ge(s_const, 16)
            pe.wait_ge(s_rows, 16 * 7)
            for r in range(3):
                m = (126, 72, 72)[r]
                i = tr(ps[:, 0, r * P:r * P + m], rows[0:m, r, :], ident[0:m, 0:m])
            i.then_inc(turned, 1)
            pe.wait_ge(s_x, 32)
            xs = u[:, :, :].rearrange("p (t j) n -> p t (j n)", t=NT)
            for b in range(4):
                for e in range(2):
                    for t in range(NT):
                        k = 2 * b + e
                        i = tr(y[:, k, t * P:(t + 1) * P], xs[:, t, k * P:(k + 1) * P], ident)
                i.then_inc(turned, 1)
            pe.wait_ge(acc_ready, 1)
            pe.wait_ge(h_ready, KD)
            for r in range(6):
                for v in range(4):
                    i = tr(ps[:, PRO_BANKS[r], v * P:(v + 1) * P], acc[:, (4 * r + v) * P:(4 * r + v + 1) * P], ident)
                i.then_inc(mod_ps, 1)
            with pe.Fori(0, DEPTH) as l:
                ffn(l, 0)
                mixer(l)
                ffn(l, 1)
            pe.wait_ge(h_ready, 8 + 24 * DEPTH)
            for t in range(NT):
                for b in range(2):
                    for k in range(4):
                        i = tr(ps[:, 2 * t + b, k * P:(k + 1) * P], h[:, 4 * b + k, t * P:(t + 1) * P], ident)
                    i.then_inc(out_ps, 1)

        @block.scalar
        def _(act):
            A = nc.scalar.activation
            act.dma_start(cst[:, :], consts[:, :]).then_inc(s_const, 16)
            for r0, src in ((0, norm_g.rearrange("l j (k n) -> (l j k) n", n=P)),
                            (48, c.rearrange("a (k n) -> (a k) n", n=P)),
                            (56, b_q_lat_g.rearrange("l (k n) -> (l k) n", n=P)),
                            (60, b_kv_lat_g[:, :]),
                            (62, c_cmp_pe.rearrange("l a (m e) n -> (l a m) (e n)", e=2))):
                act.dma_start(rows[r0:r0 + src.shape[0], 0, :], src).then_inc(s_rows, 16)
            for l in range(DEPTH):
                act.dma_start(rows[0:72, 1 + l, :], ada_b[l].rearrange("(k n) -> k n", n=P)).then_inc(s_rows, 16)
            xs = u[:, :, :].rearrange("p (t j) n -> p t (j n)", t=NT)
            for t in range(NT):
                act.dma_start(xs[:, t, :], x[0, t * P:(t + 1) * P, :]).then_inc(s_x, 16)
            act.dma_start(posi[:, :], positions.rearrange("a (t p) -> p (a t)", p=P),
                          allow_slow_non_contiguous=True).then_inc(s_pos, 16)

            act.wait_ge(turned, 1)
            A(cond[:, :], ps[:, 0, 48:56], ACT.Silu).then_inc(cond_ok, 1)
            act.wait_ge(trig_in, 1)
            A(trg[:, 0:192], trg[:, 0:192], ACT.Sin).then_inc(trig, 1)

            def squares(l, j):
                for k in range(KD):
                    act.wait_ge(h_ready, l * 24 + (8 * j + k + 1))
                    A(sq[:, k * SEQ:(k + 1) * SEQ], h[:, k, :], ACT.Square).then_inc(sq_ready, 1)

            def shift(l, j, dst):
                act.wait_ge(mod_ready, l * 3 + (j + 1))
                for k in range(KD):
                    act.wait_ge(hn_ready, l * 24 + (8 * j + k + 1))
                    A(dst[:, k, :], sq[:, k * SEQ:(k + 1) * SEQ], ACT.Identity, bias=mod[:, j, 0, k:k + 1])\
                        .then_inc(u_ready, 1)

            def round_wide(l, f, n0, m, i=0):
                it, a = m // 2, m % 2
                slot = (n0 + it) % 2
                if a == 0:
                    act.wait_ge(wide_in[slot], landed(l, (it, i), n0, WIDE, 32))
                raw = wide[:, slot, :].rearrange("p (g n) -> p g n", n=2 * P)[:, :, a * P:(a + 1) * P]
                nc.scalar.copy(wh[:, a, :, :, :].rearrange("p e k n -> p (e k) n"), raw).then_inc(wh_ready, 1)

            def round_tall(l, j, m0, m, i=0):
                it, a = m // 2, m % 2
                slot = (m0 + it) % 2
                if a == 0:
                    act.wait_ge(tall_in[slot], landed(l, (it, i), m0, TALL, 16))
                nc.scalar.copy(th[:, a, :], tall[:, slot, a * DM:(a + 1) * DM]).then_inc(th_ready, 1)

            def ffn(l, f):
                n0, m0 = (WIDE_A, TALL_A) if f == 0 else (WIDE_B, TALL_B)
                squares(l, 2 * f)
                round_wide(l, f, n0, 0)
                round_wide(l, f, n0, 1)
                shift(l, 2 * f, uh)
                width = (2 - f) * 3 * DM
                nc.scalar.copy(acc[:, 0:width], zb[:, 0:1].broadcast_to([P, width])).then_inc(acc_zero, 1)

                def tile(m, i=0):
                    act.wait_ge(gu_ready, tile_at(l, f, m, i))
                    A(fs[:, m % 2, :], ps[:, m % 2, 0:SEQ], ACT.Silu).then_inc(silu_ready, 1)
                    round_tall(l, 2 * f, m0, m, i)
                    if m + 2 < 2 * NPAIR:
                        round_wide(l, f, n0, m + 2, i)

                with act.Fori(0, KD // 2) as i:
                    for q in range(4):
                        tile(q, i)
                for m in range(2 * KD, 2 * NPAIR):
                    tile(m)

            def copy_proj(l, chunk):
                fill = CHUNKS[chunk]
                bank = 2 * (chunk % 2)
                for t in range(NT):
                    act.wait_ge(proj, l * 2 * len(CHUNKS) + (2 * chunk + t + 1))
                    src = ps[:, bank + t, :]
                    if fill == F_LAT:
                        nc.scalar.copy(plat[:, t, :], src[:, 0:416]).then_inc(pcopy, 1)
                    elif fill == F_CMPIN:
                        A(pgf[:, t, :], src[:, 256:320], ACT.Silu)
                        nc.scalar.copy(pz[:, t, :, :, :], src[:, 0:256].rearrange("p (a n) -> p a n", a=4)
                                       .unsqueeze(2).broadcast_to([P, 4, 2, HD])).then_inc(pcopy, 1)
                    elif fill == F_CK:
                        nc.scalar.copy(pk[:, t, :].rearrange("p (b a n) -> p a b n", a=2, b=2),
                                       src.rearrange("p (a b n) -> p a b n", a=2, b=2)).then_inc(pcopy, 1)
                    else:
                        dst = {F_A: pa, F_CQ: pq}[fill]
                        nc.scalar.copy(dst[:, t, :], src).then_inc(pcopy, 1)

            def aux_wait(l, name):
                act.wait_ge(aux_ready, aux_at(l, name))

            def out_of(l, name, dst, width=P):
                aux_wait(l, name)
                src = ps[0:width, aux_bank(name), :].rearrange("p (b n) -> p b n", b=2)
                nc.scalar.copy(dst, src).then_inc(aux_act, 1)

            def mixer(l):
                squares(l, 1)
                shift(l, 1, u)
                copy_proj(l, 0)
                copy_proj(l, 1)
                copy_proj(l, 2)
                aux_wait(l, "kvgf")
                b = aux_bank("kvgf")
                act.wait_ge(mod_lat, l + 1)
                A(latT[:, 2, :], ps[:, b, 0:SEQ], ACT.Copy, scale=latg[:, 2:3])
                nc.scalar.copy(gfT[:, :], ps[0:HD, b, SEQ:2 * SEQ]).then_inc(aux_act, 1)
                aux_wait(l, "hid")
                b = aux_bank("hid")
                A(hidk[:, :, 0:NCMP], ps[:, b, 0:2 * NCMP].rearrange("p (g b) -> p g b", g=2), ACT.Silu)
                A(hidv[:, :, :, 0:NCMP], ps[:, b, 32:32 + 2 * NCMP].rearrange("p (g b) -> p g b", g=2)
                  .unsqueeze(2).broadcast_to([P, 2, 4, NCMP]), ACT.Silu).then_inc(aux_act, 1)
                copy_proj(l, 3)
                for t in range(NT):
                    aux_wait(l, f"uq{t}")
                    nc.scalar.copy(qb[:, t, :, :].rearrange("p a n -> p (a n)"), ps[:, aux_bank(f"uq{t}"), 0:384])\
                        .then_inc(aux_act, 1)
                aux_wait(l, "w2")
                b = aux_bank("w2")
                nc.scalar.copy(kcn[0:NCMP, :, :], ps[0:NCMP, b, 0:P].rearrange("p (g n) -> p g n", g=2))
                nc.scalar.copy(vrep[:, :, :], ps[:, b, P:2 * P].rearrange("p (g n) -> p g n", g=2)).then_inc(aux_act, 1)
                act.wait_ge(*aux_done("gate", l))
                A(gt[:, :, :], gt[:, :, :], ACT.Exp, scale=-1.0).then_inc(gate_exp, 1)
                copy_proj(l, 4)
                for t in range(NT):
                    aux_wait(l, f"ukv{t}")
                    nc.scalar.copy(kvb[:, t, :, :].rearrange("p a n -> p (a n)"), ps[:, aux_bank(f"ukv{t}"), :])\
                        .then_inc(aux_act, 1)
                out_of(l, "qa", qaT[:, :, :])
                out_of(l, "cq0", cqT[:, 0:2, :])
                out_of(l, "cr0", crT[:, 0:2, :])
                out_of(l, "ks", ckT[:, 0:2, :])
                out_of(l, "qb0", qbT[:, 0:2, :], 96)
                out_of(l, "kb0", kbT[:, 0:2, :], 96)
                act.wait_ge(cmp_shift, l + 1)
                A(csc, csc, ACT.Exp, scale=SC64).then_inc(cmp_exp, 1)
                for n in range(NJ + 2):
                    if n < NJ:
                        act.wait_ge(nm_ready, l * NJ + (n + 1))
                        st = stat[:, n % 4, :]
                        scale = job(n)[4]
                        bank = ps[:, n % 2, :]
                        if JOBS[n][0] == "a":
                            hh = JOBS[n][1]
                            A(st[:, 6:8], st[:, 2:4], ACT.Exp, bias=gn[:, G_SINK + hh:G_SINK + hh + 1])
                        A(E[:, n % 3, 0:P], bank[:, 0:P], ACT.Exp, bias=st[:, 2:3], scale=scale,
                          accum_out=st[:, 4:5])
                        A(E[:, n % 3, P:3 * P], bank[:, P:3 * P], ACT.Exp, bias=st[:, 3:4], scale=scale,
                          accum_out=st[:, 5:6]).then_inc(exp_ready, 1)
                    if n >= 2:
                        m = n - 2
                        act.wait_ge(pt_ready, l * NJ + (m + 1))
                        if m >= 2:
                            act.wait_ge(pv_ready, l * NJ + (m - 1))
                        nc.scalar.copy(ET[:, m % 2, :], ps[:, 2, 0:3 * P]).then_inc(et_ready, 1)
                    for k in range(KD):
                        if n == min(LAST[k] + 3, NJ + 1):
                            if k >= 2:
                                act.wait_ge(mix_done, l * (KD - 1) + (k - 1))
                            round_tall(l, 1, TALL_M, k)

            with act.Fori(0, DEPTH) as l:
                ffn(l, 0)
                mixer(l)
                ffn(l, 1)
            o = u[:, :, :].rearrange("p (b j) n -> p b (j n)", b=4)
            for b in range(4):
                act.wait_ge(out_ps, b + 1)
                nc.scalar.copy(o[:, b, :], ps[:, b, :]).then_inc(out_sb, 1)

        @block.vector
        def _(dve):
            V = nc.vector
            tt, ts, stt = V.tensor_tensor, V.tensor_scalar, V.scalar_tensor_tensor
            chain = {"n": 0}

            def link(ins):
                chain["n"] += 1
                ins.then_inc(chain_s, 1)
                dve.wait_ge(chain_s, chain["n"])

            def rsqrt(n, p=P):
                s, t, r = ssb[0:p, 0:n], newt[0:p, 0:n], rst[0:p, 0:n]
                link(ts(newt_i[0:p, 0:n], s.bitcast(I32), 1, None, ALU.logical_shift_right))
                link(ts(r.bitcast(I32), newt_i[0:p, 0:n], -1.0, float(0x5F3759DF), ALU.mult, ALU.add))
                for _ in range(3):
                    link(tt(t, r, r, ALU.mult))
                    link(stt(t, t, -0.5, s, ALU.mult, ALU.mult))
                    link(stt(r, t, 1.5, r, ALU.add, ALU.mult))

            def heads_rstd(src, dim):
                p, a, n, d = src.shape
                tmp = T1[0:p, 0:a * n * d].rearrange("p (a n d) -> p a n d", a=a, n=n)
                link(tt(tmp, src, src, ALU.mult))
                link(V.tensor_reduce(ssb[0:p, 0:a * n].rearrange("p (a n) -> p a n", a=a), tmp, AX.X, ALU.add))
                link(ts(ssb[0:p, 0:a * n], ssb[0:p, 0:a * n], 1.0 / dim, EPS, ALU.mult, ALU.add))
                rsqrt(a * n, p)

            def by_rstd(src, dst):
                p, a, n, d = src.shape
                r = rst[0:p, 0:a * n].rearrange("p (a n) -> p a n", a=a).unsqueeze(3).broadcast_to([p, a, n, d])
                link(tt(dst, src, r, ALU.mult))

            def gain(ap, lo, dst=None):
                p, a, n, d = ap.shape
                g = gn[0:p, lo:lo + d].unsqueeze(1).unsqueeze(1).broadcast_to([p, a, n, d])
                return tt(ap if dst is None else dst, ap, g, ALU.mult)

            def rope(src, cs, outs):
                p, a, n, d = src.shape
                hf = d // 2
                t1 = T1[:, 0:a * n * d].rearrange("p (a n d) -> p a n d", a=a, n=n)
                t2 = T2[:, 0:a * n * d].rearrange("p (a n d) -> p a n d", a=a, n=n)
                wide_ = lambda ap: ap.unsqueeze(2).broadcast_to([p, a, n, ap.shape[-1]])
                tt(t1, src, wide_(cs[:, 0, :, :]), ALU.mult)
                tt(t2[:, :, :, 0:hf], src[:, :, :, hf:d], wide_(cs[:, 1, :, 0:hf]), ALU.mult)
                link(tt(t2[:, :, :, hf:d], src[:, :, :, 0:hf], wide_(cs[:, 1, :, hf:d]), ALU.mult))
                for o in outs[:-1]:
                    tt(o, t1, t2, ALU.add)
                return tt(outs[-1], t1, t2, ALU.add)

            def sum_parts(r, bank, dst):
                return V.tensor_reduce(dst[:, 4 * r:4 * r + 4], ps[:, bank, :].rearrange("p (a n) -> p a n", a=4),
                                       AX.X, ALU.add)

            def unit(sums, adab, ng, slot, half):
                m = mod[:, slot, :, :].rearrange("p v k -> p (v k)")
                link(tt(m, sums, adab, ALU.add))
                if half:
                    ts(mod[:, slot, 2, :], mod[:, slot, 2, :], 0.5, None, ALU.mult)
                return stt(mod[:, slot, 1, :], mod[:, slot, 1, :], 1.0, ng, ALU.add, ALU.mult)

            dve.sem_inc(ada_used, 2)
            dve.sem_inc(wide_used, 2)
            dve.sem_inc(tall_used, 2)
            V.memset(ones[:, :], 1.0)
            V.memset(zb[:, :], 0.0)
            V.memset(hidk[:, :, :], 0.0)
            V.memset(kcd[:, :, :, :], 0.0)
            V.memset(hidv[:, :, :, :], 0.0)
            link(V.memset(mband[:, :], 0.0))
            link(V.memset(mcausal[:, :], 0.0))
            dve.wait_ge(s_const, 16)
            V.tensor_copy(idb[:, :], ident)
            for m in (mcausal, mband):
                V.tensor_copy(m[:, 0:P], cst[:, C_CAUSAL:C_CAUSAL + P])
                V.tensor_copy(m[:, 2 * P:3 * P], cst[:, C_CAUSAL:C_CAUSAL + P])
            V.tensor_copy(mband[:, P:2 * P], cst[:, C_BAND:C_BAND + P]).then_inc(setup, 1)
            dve.wait_ge(turned, 1)
            dve.wait_ge(cond_ok, 1)
            for r in range(3):
                m = (126, 72, 72)[r]
                i = V.tensor_copy(vt[:, r, 0:m], ps[:, 0, r * P:r * P + m])
            link(i)
            for b in range(4):
                dve.wait_ge(turned, b + 2)
                for e in range(2):
                    V.tensor_copy(h[:, 2 * b + e, :], y[:, 2 * b + e, :]).then_inc(h_ready, 1)

            two_pi = 2.0 * np.pi
            c1 = 6.28125
            c2 = float(np.float32(two_pi - c1))
            c3 = float(np.float32(two_pi - c1 - np.float64(np.float32(two_pi - c1))))
            magic = 12582912.0
            angf = trg[:, 192:288]
            ang = angf.rearrange("p (t n) -> p t n", t=NT)
            kk = trg[:, 288:480].rearrange("p (e n) -> p e n", e=2)
            rr = trg[:, 0:192].rearrange("p (e n) -> p e n", e=2)
            dve.wait_ge(s_pos, 16)
            link(V.tensor_copy(posf[:, :], posi[:, :]))
            link(tt(ang, cst[:, C_INVF:C_INVF + 48].unsqueeze(1).broadcast_to([P, NT, 48]),
                    posf[:, :].unsqueeze(2).broadcast_to([P, NT, 48]), ALU.mult))
            ts(kk[:, 0, :], angf, 1.0 / two_pi, 0.25, ALU.mult, ALU.add)
            link(ts(kk[:, 1, :], angf, 1.0 / two_pi, None, ALU.mult))
            link(ts(kk, kk, magic, None, ALU.add))
            link(ts(kk, kk, -magic, None, ALU.add))
            link(stt(rr, kk, -c1, ang.rearrange("p t n -> p (t n)").unsqueeze(1).broadcast_to([P, 2, 96]),
                     ALU.mult, ALU.add))
            link(stt(rr, kk, -c2, rr, ALU.mult, ALU.add))
            link(stt(rr, kk, -c3, rr, ALU.mult, ALU.add))
            link(ts(rr[:, 0, :], rr[:, 0, :], two_pi / 4, None, ALU.add))
            for cmp, turn_ in ((ALU.is_gt, -two_pi), (ALU.is_lt, two_pi)):
                link(ts(kk, rr, float(np.float32(-turn_ / 2)), turn_, cmp, ALU.mult))
                link(tt(rr, rr, kk, ALU.add))
            link(ts(rr, rr, 3.1415925, -3.1415925, ALU.min, ALU.max))
            V.memset(small[:, 1:2], 0.0).then_inc(trig_in, 1)
            dve.wait_ge(trig, 1)
            tv = rr.rearrange("p e (t n) -> p e t n", t=NT)
            for cs, lo, hf in ((cs64, 0, 32), (cs32, 32, 16)):
                V.tensor_copy(cs[:, 0, :, 0:hf], tv[:, 0, :, lo:lo + hf])
                V.tensor_copy(cs[:, 0, :, hf:2 * hf], tv[:, 0, :, lo:lo + hf])
                ts(cs[:, 1, :, 0:hf], tv[:, 1, :, lo:lo + hf], -1.0, None, ALU.mult)
                i = V.tensor_copy(cs[:, 1, :, hf:2 * hf], tv[:, 1, :, lo:lo + hf])
            link(i)
            for k in range(ADA_PRO):
                dve.wait_ge(ada_in[k % 2], 16 * (k // 2 + 1))
                if k == 0:
                    i = ts(acc[:, 0:3 * DM], ada[:, 0, :], cond[:, 0:1], None, ALU.mult)
                else:
                    i = stt(acc[:, 0:3 * DM], ada[:, k % 2, :], cond[:, k:k + 1], acc[:, 0:3 * DM], ALU.mult, ALU.add)
                i.then_inc(ada_used, 1)
                dve.wait_ge(ada_used, 3 + k)
            V.memset(small[:, 0:1], 0.0).then_inc(acc_ready, 1)

            for r in range(6):
                dve.wait_ge(mod_ps, r + 1)
                i = sum_parts(r, PRO_BANKS[r], msum)
            link(i)
            unit(msum[:, 0:24], vt[:, 1, 0:24], vt[:, 0, 0:8], 0, True).then_inc(mod_ready, 1)
            dve.wait_ge(mod_ready, 1)

            def norm(l, j):
                dve.wait_ge(ss_ready, l * 3 + (j + 1))
                for t in range(NT):
                    i = ts(ssb[:, t:t + 1], ps[:, 2 + t, 0:1], 1.0 / DM, EPS, ALU.mult, ALU.add)
                link(i)
                rsqrt(NT)
                for t in range(NT):
                    i = ts(T1[:, t * P:(t + 1) * P], ident, rst[:, t:t + 1], None, ALU.mult)
                i.then_inc(diag_ready, 1)
                dve.wait_ge(r_ready, l * 3 + (j + 1))
                for k in range(KD):
                    stt(sq[:, k * SEQ:(k + 1) * SEQ], h[:, k, :], mod[:, j, 1, k:k + 1], ps[:, 2, 0:SEQ],
                        ALU.mult, ALU.mult).then_inc(hn_ready, 1)

            def residual(l, j):
                for k in range(KD):
                    if k % 2 == 0:
                        dve.wait_ge(y_ready, l * 12 + (4 * j + k // 2 + 1))
                    stt(h[:, k, :], y[:, k, :], mod[:, j, 2, k:k + 1], h[:, k, :], ALU.mult, ALU.add)\
                        .then_inc(h_ready, 1)

            def rest_tall(l, j, m0, m, i=0):
                it, a = m // 2, m % 2
                dve.wait_ge(th_ready, rows_at(l, j, m, i))
                tt(tl[:, a, :], tall[:, (m0 + it) % 2, a * DM:(a + 1) * DM], th[:, a, :].bitcast(F32),
                   ALU.subtract).then_inc(tl_ready, 1)

            def ffn(l, f):
                j = 2 * f
                n0, m0 = (WIDE_A, TALL_A) if f == 0 else (WIDE_B, TALL_B)
                norm(l, j)
                for k in range(KD):
                    dve.wait_ge(u_ready, l * 24 + (8 * j + k + 1))
                    stt(ul[:, k, :], sq[:, k * SEQ:(k + 1) * SEQ], mod[:, j, 0, k:k + 1], uh[:, k, :].bitcast(F32),
                        ALU.add, ALU.subtract).then_inc(ul_ready, 1)
                width = 3 * DM if f == 0 else 1536

                def rest_wide(m, i=0):
                    it, a = m // 2, m % 2
                    raw = wide[:, (n0 + it) % 2, :].rearrange("p (g n) -> p g n", n=2 * P)[:, :, a * P:(a + 1) * P]
                    dve.wait_ge(wh_ready, tile_at(l, f, m, i))
                    tt(wl[:, a, :, :, :].rearrange("p e k n -> p (e k) n"), raw,
                       wh[:, a, :, :, :].rearrange("p e k n -> p (e k) n").bitcast(F32), ALU.subtract)\
                        .then_inc(wl_ready, 1)

                def tile(m, i=0):
                    a = m % 2
                    dve.wait_ge(silu_ready, tile_at(l, f, m, i))
                    tt(fa[:, a, :], fs[:, a, :], ps[:, a, SEQ:2 * SEQ], ALU.mult).then_inc(fa_s, 1)
                    dve.wait_ge(fa_s, tile_at(l, f, m, i))
                    V.tensor_copy(fh[:, a, :], fa[:, a, :]).then_inc(fh_s, 1)
                    rest_tall(l, 2 * f, m0, m, i)
                    dve.wait_ge(fh_s, tile_at(l, f, m, i))
                    tt(fl[:, a, :], fa[:, a, :], fh[:, a, :].bitcast(F32), ALU.subtract).then_inc(mul_ready, 1)
                    if a == 1:
                        dve.wait_ge(tl_ready, rows_at(l, 2 * f, m, i))
                        dve.sem_inc(tall_used, 1)
                    if m + 2 < 2 * NPAIR:
                        rest_wide(m + 2, i)

                def free_wide(m, i=0):
                    dve.wait_ge(wl_ready, tile_at(l, f, m, i))
                    dve.sem_inc(wide_used, 1)

                def ada_step(q, e, i):
                    count = l * ADA_L + (ADA_PRO + f * 2 * KD + 2 * q + e) + 4 * i
                    dve.wait_ge(ada_in[e], l * (ADA_L * 8) + (ADA_PRO * 8 + f * KD * 16 + 16 * (q + 1)) + 32 * i)
                    a = acc[:, e * width:(e + 1) * width]
                    dve.wait_ge(ada_used, count + 1)
                    stt(a, ada[:, e, 0:width], cond[:, bass.ds(2 * i + q, 1)], a, ALU.mult, ALU.add)\
                        .then_inc(ada_used, 1)

                rest_wide(0)
                rest_wide(1)
                free_wide(1)
                with dve.Fori(0, KD // 2) as i:
                    for q in range(4):
                        tile(q, i)
                        if q == 0:
                            dve.wait_ge(acc_zero, l * 2 + (f + 1))
                        ada_step(q // 2, q % 2, i)
                        if q % 2:
                            free_wide(q + 2, i)
                dve.wait_ge(ada_used, l * ADA_L + (ADA_PRO + (f + 1) * 2 * KD + 2))
                V.memset(small[:, 0:1], 0.0).then_inc(acc_ready, 1)
                rounds = 12 - 6 * f
                for m in range(2 * KD, 2 * NPAIR):
                    tile(m)
                    if m % 2 and m + 2 < 2 * NPAIR:
                        free_wide(m + 2)
                    for r in range(2 * (m - 2 * KD), 2 * (m - 2 * KD) + 2):
                        if r < rounds:
                            dve.wait_ge(mod_ps, l * 18 + (6 + 12 * f + r + 1))
                            sum_parts(r, 2 + r % 2, msum).then_inc(mod_red, 1)
                residual(l, j)
                dve.wait_ge(mod_red, l * 18 + (12 * f + rounds))
                for s in ((1, 2) if f == 0 else (0,)):
                    if f == 0:
                        adab = vt[:, bass.ds(l + 1, 1), 24 * s:24 * s + 24].rearrange("p a n -> p (a n)")
                        ng = vt[:, 0, bass.ds(l * 24 + 8 * s, 8)]
                        i = unit(msum[:, 24 * (s - 1):24 * s], adab, ng, s, s == 2)
                    else:
                        i = unit(msum[:, 0:24], vt[:, DEPTH, 0:24],
                                 vt[:, 0, 24 * (DEPTH - 1):24 * (DEPTH - 1) + 8], 0, True)
                    i.then_inc(mod_ready, 1)
                if f == 0:
                    V.tensor_copy(latg[:, 0:2], vt[:, 0, bass.ds(l * 2 + 56, 2)])
                    V.tensor_copy(pe2[:, :], vt[:, 0, bass.ds(l * 32 + 62, 32)])
                    V.tensor_copy(latg[:, 2:3], vt[:, 0, bass.ds(l + 60, 1)]).then_inc(mod_lat, 1)
                    dve.wait_ge(mod_lat, l + 1)
                dve.wait_ge(mod_ready, l * 3 + (3 if f == 0 else 4))

            def aux_wait(l, name):
                dve.wait_ge(aux_ready, aux_at(l, name))

            def copied(l, chunk):
                dve.wait_ge(pcopy, l * 2 * len(CHUNKS) + 2 * (chunk + 1))

            def out_of(l, name, dst, width=P):
                aux_wait(l, name)
                src = ps[0:width, aux_bank(name), :].rearrange("p (b n) -> p b n", b=2)
                V.tensor_copy(dst, src).then_inc(aux_dve, 1)

            def v4(ap, n):
                return ap.rearrange("p t (n d) -> p t n d", n=n)

            def mixer(l):
                norm(l, 1)
                dve.wait_ge(s_small, (l + 1) * 160)
                dve.wait_ge(u_ready, l * 24 + 16)
                copied(l, 0)
                dve.sem_inc(wide_used, 1)
                for lo, hi, part in ((0, 256, 0), (256, 384, 2), (384, 416, 4)):
                    s = plat[:, :, lo:hi].unsqueeze(2)
                    tmp = T1[:, 0:2 * (hi - lo)].rearrange("p (a n d) -> p a n d", a=2, n=1)
                    link(tt(tmp, s, s, ALU.mult))
                    link(V.tensor_reduce(ssb[:, part:part + 2].unsqueeze(2), tmp, AX.X, ALU.add))
                    link(ts(ssb[:, part:part + 2], ssb[:, part:part + 2], 1.0 / (hi - lo), EPS, ALU.mult, ALU.add))
                rsqrt(6)
                for lo, hi, part in ((0, 256, 0), (256, 384, 2), (384, 416, 4)):
                    s = plat[:, :, lo:hi]
                    r = rst[:, part:part + 2].unsqueeze(2).broadcast_to([P, NT, hi - lo])
                    i = tt(s, s, r, ALU.mult)
                i.then_inc(prep, 1)
                dve.wait_ge(prep, prep_at(l, "lat"))
                kr = plat[:, :, 384:416].unsqueeze(2)
                link(gain(kr, G_BR + 32))
                link(rope(kr, cs32, [kb[:, :, hh:hh + 1, HD:96] for hh in range(B_H)]))
                for a, name in enumerate(("zk", "zv")):
                    aux_wait(l, name)
                    for hh in range(2):
                        for par in range(2):
                            half = slice(64 * par, 64 * par + 64)
                            src = ps[half, aux_bank(name), hh * SEQ:(hh + 1) * SEQ].rearrange("p (b r) -> p b r", r=16)
                            for late in range(2):
                                z = src[:, late:late + NCMP, par:16:2].rearrange("p b m -> p m b")
                                dst = zc[half, a, hh, 8 * late:8 * late + 8, :]
                                o = pe2[half, a * 16 + 8 * late:a * 16 + 8 * late + 8].unsqueeze(2)\
                                    .broadcast_to([64, 8, NCMP])
                                i = tt(dst, z, o, ALU.add)
                    i.then_inc(aux_dve, 1)
                aux_wait(l, "lat")
                for b in range(2):
                    i = ts(latT[:, b, :], ps[:, aux_bank("lat"), b * SEQ:(b + 1) * SEQ], latg[:, b:b + 1], None, ALU.mult)
                i.then_inc(aux_dve, 1)
                dve.sem_inc(wide_used, 1)
                copied(l, 2)
                dve.sem_inc(wide_used, 1)
                qk = v4(pa[:, :, 0:384], 6)
                heads_rstd(qk, HD)
                by_rstd(qk, qk)
                gain(qk[:, :, 0:A_H, :], G_A)
                link(gain(qk[:, :, A_H:6, :], G_A + HD))
                link(rope(qk[:, :, 0:A_H, :], cs64, [qa[:, :, :, :]]))
                rope(qk[:, :, A_H:6, :], cs64, [kad[:, :, :, 0, :], kad[:, :, :, 1, :]]).then_inc(prep, 1)
                dve.wait_ge(prep, prep_at(l, "qa"))
                copied(l, 3)
                dve.sem_inc(wide_used, 2)
                cq = v4(pq, C_H)
                heads_rstd(cq, HD)
                by_rstd(cq, cq)
                gain(cq, G_C).then_inc(prep, 1)
                dve.wait_ge(prep, prep_at(l, "cq"))
                aux_wait(l, "gate")
                tt(gt[:, :, :], ps[:, aux_bank("gate"), 0:48].rearrange("p (t n) -> p t n", t=NT),
                   gn[:, G_GB:G_END].unsqueeze(1).broadcast_to([P, NT, 24]), ALU.add).then_inc(aux_dve, 1)
                dve.wait_ge(aux_done("gate", l)[0], aux_done("gate", l)[1])
                dve.wait_ge(*aux_done("w2", l))
                kc = kcn[0:NCMP, :, :].unsqueeze(2)
                heads_rstd(kc, HD)
                by_rstd(kc, kc)
                for dup in range(2):
                    i = gain(kc, G_C + HD, kcd[0:NCMP, :, dup, :].unsqueeze(2))
                i.then_inc(prep, 1)
                dve.wait_ge(gate_exp, l + 1)
                link(ts(gt[:, :, :], gt[:, :, :], 1.0, None, ALU.add))
                link(V.reciprocal(gt[:, :, :], gt[:, :, :]))
                rope(cq, cs64, [qr[:, :, :, :]]).then_inc(prep, 1)
                dve.wait_ge(prep, prep_at(l, "cr"))
                copied(l, 4)
                dve.sem_inc(wide_used, 1)
                ck = v4(pk[:, :, 0:256], 4)
                heads_rstd(ck, HD)
                by_rstd(ck, ck)
                gain(ck[:, :, 0:2, :], G_C + 2 * HD)
                link(gain(ck[:, :, 2:4, :], G_C + 3 * HD))
                rope(ck, cs64, [krd[:, :, :, 0, :], krd[:, :, :, 1, :]]).then_inc(prep, 1)
                dve.wait_ge(prep, prep_at(l, "ck"))
                dve.wait_ge(*aux_done("uq1", l))
                qn, qp = qb[:, :, :, 0:HD], qb[:, :, :, HD:96]
                heads_rstd(qn, HD)
                by_rstd(qn, qn)
                gain(qn, G_BN)
                heads_rstd(qp, ROPE_B)
                by_rstd(qp, qp)
                link(gain(qp, G_BR))
                rope(qp, cs32, [qp]).then_inc(prep, 1)
                dve.wait_ge(prep, prep_at(l, "qb"))
                dve.wait_ge(*aux_done("ukv1", l))
                kn = kvb[:, :, :, 0:HD]
                heads_rstd(kn, HD)
                by_rstd(kn, kb[:, :, :, 0:HD])
                gain(kb[:, :, :, 0:HD], G_BN + HD).then_inc(prep, 1)
                out_of(l, "ka", kaT[:, :, :])
                out_of(l, "cq1", cqT[:, 2:4, :])
                aux_wait(l, "kc")
                V.tensor_copy(kcT[:, :, 0:NCMP], ps[:, aux_bank("kc"), 0:2 * P].rearrange("p (g b) -> p g b", g=2)
                              [:, :, 0:NCMP]).then_inc(aux_dve, 1)
                spread = lambda ap, n=C_H: ap.rearrange("p (t b) -> p t b", t=NT).unsqueeze(2)\
                    .broadcast_to([P, NT, n, NCMP])
                over = lambda r: cst16[:, r, :].rearrange("p (t n) -> p t n", t=NT)
                for odd in range(2):
                    aux_wait(l, f"cmps{odd}")
                    sv = ps[:, aux_bank(f"cmps{odd}"), 0:128].rearrange("p (t n b) -> p t n b", t=NT, b=16)
                    tt(csc[:, :, odd:C_H:2, :], sv[:, :, :, 0:NCMP], spread(cst[:, C_NEG:C_NEG + 30], C_H // 2),
                       ALU.add).then_inc(aux_dve, 1)
                dve.wait_ge(*aux_done("cmps1", l))
                link(V.tensor_reduce(over(0), csc, AX.X, ALU.max))
                tt(csc, csc, over(0).unsqueeze(3).broadcast_to([P, NT, C_H, NCMP]), ALU.subtract)\
                    .then_inc(cmp_shift, 1)
                out_of(l, "cr1", crT[:, 2:4, :])
                out_of(l, "kw", ckT[:, 2:4, :])
                out_of(l, "qb1", qbT[:, 2:4, :], 96)
                out_of(l, "kb1", kbT[:, 2:4, :], 96)
                dve.wait_ge(cmp_exp, l + 1)
                link(V.memset(cp, 0.0))
                link(V.tensor_reduce(over(1), csc, AX.X, ALU.add))
                link(V.reciprocal(over(1), over(1)))
                gates = gt[:, :, :].rearrange("p t (n g) -> p t n g", g=3)
                link(tt(over(2), over(1), gates[:, :, :, 0], ALU.mult))
                link(tt(csc, csc, spread(cst[:, C_VIS:C_VIS + 30]), ALU.mult))
                tt(cp[:, :, :, 0:NCMP], csc, over(2).unsqueeze(3).broadcast_to([P, NT, C_H, NCMP]), ALU.mult)\
                    .then_inc(prep, 1)
                aux_wait(l, "cmpt")
                V.tensor_copy(cmpT[:, :, :], ps[:, aux_bank("cmpt"), :].rearrange("p (b n) -> p b n", b=2))\
                    .then_inc(aux_dve, 1)
                for n in range(NJ + 4):
                    if n - 4 in LAST:
                        pair = LAST.index(n - 4)
                        dve.wait_ge(pv_ready, l * NJ + (n - 3))
                        V.tensor_copy(uh[:, pair, :], ps[:, 3, 0:SEQ]).then_inc(oh_s, 1)
                        dve.wait_ge(oh_s, l * KD + (pair + 1))
                        tt(ol[:, pair, :], ps[:, 3, 0:SEQ], uh[:, pair, :].bitcast(F32), ALU.subtract)\
                            .then_inc(o_ready, 1)
                    if n < NJ:
                        br, hh = JOBS[n]
                        st = stat[:, n % 4, :]
                        scale = job(n)[4]
                        bank = ps[:, n % 2, :]
                        dve.wait_ge(s_ready, l * NJ + (n + 1))
                        V.tensor_reduce(st[:, 0:1], bank[:, 0:P], AX.X, ALU.max)
                        link(V.tensor_reduce(st[:, 1:2], bank[:, P:3 * P], AX.X, ALU.max))
                        if br == "a":
                            sink = gn[:, G_SINK + hh:G_SINK + hh + 1].broadcast_to([P, 2])
                            link(stt(st[:, 0:2], st[:, 0:2], scale, sink, ALU.mult, ALU.max))
                            ts(st[:, 2:4], st[:, 0:2], -1.0, None, ALU.mult).then_inc(nm_ready, 1)
                        else:
                            ts(st[:, 2:4], st[:, 0:2], -scale, None, ALU.mult).then_inc(nm_ready, 1)
                    if 1 <= n <= NJ:
                        m = n - 1
                        br, hh = JOBS[m]
                        st = stat[:, m % 4, :]
                        dve.wait_ge(exp_ready, l * NJ + (m + 1))
                        if br == "a":
                            link(tt(st[:, 4:6], st[:, 4:6], st[:, 6:8], ALU.add))
                        link(V.reciprocal(st[:, 4:6], st[:, 4:6]))
                        if br in ("slc", "win"):
                            g = gates[:, :, hh, 1 if br == "slc" else 2]
                            link(tt(st[:, 4:6], st[:, 4:6], g, ALU.mult))
                        ts(E[:, m % 3, 0:P], E[:, m % 3, 0:P], st[:, 4:5], None, ALU.mult)
                        ts(E[:, m % 3, P:3 * P], E[:, m % 3, P:3 * P], st[:, 5:6], None, ALU.mult)\
                            .then_inc(en_ready, 1)
                    for k in range(KD):
                        if n == min(LAST[k] + 4, NJ + 2):
                            rest_tall(l, 1, TALL_M, k)
                            if k % 2:
                                dve.wait_ge(tl_ready, rows_at(l, 1, k))
                                dve.sem_inc(tall_used, 1)
                residual(l, 1)

            with dve.Fori(0, DEPTH) as l:
                dve.sem_clear(chain_s)
                chain["n"] = 0
                ffn(l, 0)
                mixer(l)
                ffn(l, 1)


_INS = ["x", "c", "positions", "ada_w", "ada_b", "norm_g", "ffn_w_in", "ffn_w_out", "w_in", "w_out",
        "a_sinks", "a_qk_g", "b_q_lat_g", "b_kv_lat_g", "b_w_uq", "b_w_ukv", "b_qk_nope_g", "b_qk_rope_g",
        "c_qk_g", "c_cmp_pe", "c_cmp_w1", "c_cmp_w2", "c_gate_w", "c_gate_b"]


def shape_constants():
    t = np.zeros((P, C_END), np.float32)
    q, k = np.arange(P)[:, None], np.arange(P)[None, :]
    t[:, C_ID:C_ID + P] = q == k
    t[:, C_CAUSAL:C_CAUSAL + P] = np.where(k > q, NEG, 0.0)
    t[:, C_BAND:C_BAND + P] = np.where(k <= q, NEG, 0.0)
    for lo, dim in ((0, HD), (HD // 2, ROPE_B)):
        power = np.arange(0, dim, 2, dtype=np.float32) / np.float32(dim)
        t[:, C_INVF + lo:C_INVF + lo + dim // 2] = np.float32(1.0) / np.power(np.float32(10000.0), power)
    for i in range(NT):
        seen = np.arange(NCMP)[None, :] * 16 + CL - 1 <= i * P + q
        t[:, C_NEG + i * NCMP:C_NEG + (i + 1) * NCMP] = np.where(seen, 0.0, NEG)
        t[:, C_VIS + i * NCMP:C_VIS + (i + 1) * NCMP] = seen
    return t


def kernel(**inputs):
    import concourse.bacc as _bacc
    from concourse.bass_utils import run_bass_kernel_spmd as _run

    nc = _bacc.Bacc("TRN2", target_bir_lowering=False, num_devices=1)
    arrays, args = {}, []
    for name in _INS + ["consts"]:
        a = np.ascontiguousarray(inputs[name] if name != "consts" else shape_constants())
        arrays[f"in_{name}_dram"] = a
        args.append(nc.dram_tensor(f"in_{name}_dram", a.shape, mybir.dt.from_np(a.dtype), kind="ExternalInput").ap())
    out = nc.dram_tensor("out_0_dram", (1, SEQ, DM), F32, kind="ExternalOutput").ap()
    hybrid_kernel(nc, *args, out)
    r = _run(nc, [arrays], core_ids=[0])
    return r.results[0]["out_0_dram"]
```

```python
from contextlib import ExitStack

import numpy as np

import concourse.bass as bass
from concourse import mybir

F32 = mybir.dt.float32
F32R = mybir.dt.float32r
BF16 = mybir.dt.bfloat16
I32 = mybir.dt.int32
ALU = mybir.AluOpType
ACT = mybir.ActivationFunctionType
AX = mybir.AxisListType

P = 128
DEPTH = 2
SEQ = 256
NT = SEQ // P
DM = 1024
KD = DM // P
NMOD = 9
DFF = 2816
NPAIR = DFF // (2 * P)
EPS = 1e-6
NEG = -1e30
HD = 64
ROPE_B = 32
A_H, A_KV = 4, 2
B_H = 4
C_H, C_KV = 8, 2
NCMP = SEQ // 16 - 1
CL = 32
SC64 = float(HD) ** -0.5
SC96 = float(HD + ROPE_B) ** -0.5

C_ID, C_CAUSAL, C_BAND, C_INVF, C_NEG, C_VIS = 0, 128, 256, 384, 432, 462
C_END = 492

G_A, G_C, G_BN, G_BR, G_SINK, G_GB, G_END = 0, 128, 384, 512, 576, 580, 604

WIDE_A, WIDE_M, WIDE_B, WIDE = 0, NPAIR, NPAIR + 6, 2 * NPAIR + 6
TALL_A, TALL_M, TALL_B, TALL = 0, NPAIR, NPAIR + 4, 2 * NPAIR + 4
F_LAT, F_CMPIN, F_A, F_CMPW, F_CQ, F_CK = range(6)
CHUNKS = (F_LAT, F_CMPIN, F_A, F_CQ, F_CK)

AUX = [("zk", "dve"), ("zv", "dve"), ("lat", "dve"), ("kvgf", "act"), ("uq0", "act"), ("uq1", "act"),
       ("ukv0", "act"), ("ukv1", "act"), ("gate", "dve"), ("hid", "act"), ("qa", "act"), ("ka", "act"),
       ("w2", "act"), ("qb0", "act"), ("qb1", "act"), ("kb0", "act"), ("kb1", "act"), ("kc", "act"),
       ("cq0", "act"), ("cq1", "act"), ("cmps0", "dve"), ("cmps1", "dve"), ("cr0", "act"), ("cr1", "act"),
       ("ks", "act"), ("kw", "act"), ("cmpt", "dve")]
AUXN = [n for n, _ in AUX]
AUX_ACT = sum(e == "act" for _, e in AUX)
AUX_DVE = sum(e == "dve" for _, e in AUX)

JOBS = [("a", h) for h in range(A_H)] + [("b", h) for h in range(B_H)]
JOBS += [(br, h) for h in range(C_H) for br in ("slc", "win")]
NJ = len(JOBS)
LAST = [n for n in range(NJ) if JOBS[n][1] % 2 and (n + 1 == NJ or JOBS[n + 1][1] != JOBS[n][1])]

ADA_PRO = KD - 2
ADA_L = 4 * KD
PRO_BANKS = (0, 1, 4, 5, 6, 7)


def hybrid_kernel(nc, x, c, positions, ada_w, ada_b, norm_g, ffn_w_in, ffn_w_out, w_in, w_out,
                  a_sinks, a_qk_g, b_q_lat_g, b_kv_lat_g, b_w_uq, b_w_ukv, b_qk_nope_g, b_qk_rope_g,
                  c_qk_g, c_cmp_pe, c_cmp_w1, c_cmp_w2, c_gate_w, c_gate_b, consts, out):
    with ExitStack() as ctx:
        def sb(name, shape, dt=F32):
            return ctx.enter_context(nc.sbuf_tensor(name, shape, dt))

        def sem(name):
            return ctx.enter_context(nc.semaphore(name))

        h = sb("h", [P, KD, SEQ])
        wide = sb("wide", [P, 2, KD * 512])
        tall = sb("tall", [P, 2, 2 * DM])
        ada = sb("ada", [P, 2, 3 * DM])
        fs = sb("fs", [P, 2, SEQ])
        fa = sb("fa", [P, 2, SEQ])
        ARENA = 13440
        SHARED0 = nc.sbuf_base
        A_U, A_SQ, A_ACC, A_MIX = 0, 2048, 4096, 4096 + 6 * DM
        shared = sb("shared", [P, A_MIX + ARENA])

        def at(name, shape, off, dt=F32):
            return nc.alloc_sbuf_tensor_at(name, shape, dt, offset=SHARED0 + 4 * off)

        u = at("u", [P, KD, SEQ], A_U)
        uh = at("uh", [P, KD, SEQ], A_U, F32R)
        sq = at("sq", [P, KD * SEQ], A_SQ)
        ul = at("ul", [P, KD, SEQ], A_SQ, F32R)
        acc = at("acc", [P, 6 * DM], A_ACC)
        ol = at("ol", [P, KD, SEQ], A_ACC, F32R)
        th = at("th", [P, 2, DM], A_MIX, F32R)
        tl = at("tl", [P, 2, DM], A_MIX + 2048, F32R)
        wh = at("wh", [P, 2, 2, KD, P], A_MIX + 4096, F32R)
        wl = at("wl", [P, 2, 2, KD, P], A_MIX + 8192, F32R)
        fh = at("fh", [P, 2, SEQ], A_MIX + 12288, F32R)
        fl = at("fl", [P, 2, SEQ], A_MIX + 12800, F32R)
        cst = sb("cst", [P, C_END])
        idb = sb("idb", [P, P], BF16)
        mcausal = sb("mcausal", [P, 3 * P], BF16)
        mband = sb("mband", [P, 3 * P], BF16)
        zb = sb("zb", [P, 512], BF16)
        ones = sb("ones", [P, P])
        rows = sb("rows", [P, 3, P])
        vt = sb("vt", [P, 3, P])
        cond = sb("cond", [P, KD])
        mod = sb("mod", [P, 3, 3, KD])
        posi = sb("posi", [P, NT], I32)
        posf = sb("posf", [P, NT])
        cs64 = sb("cs64", [P, 2, NT, HD])
        cs32 = sb("cs32", [P, 2, NT, ROPE_B])
        small = sb("small", [P, 64])
        newt_i = sb("newt_i", [P, 32], I32)
        newt = sb("newt", [P, 32])
        ssb = sb("ssb", [P, 32])
        rst = sb("rst", [P, 32])
        gn = sb("gn", [P, G_END])
        uq = sb("uq", [P, 2, 384])
        ukv = sb("ukv", [P, 512])
        w2 = sb("w2", [P, 2, HD])
        gw = sb("gw", [HD, 24])
        plat = acc[:, 0:832].rearrange("p (t n) -> p t n", t=NT)
        pz = acc[:, 832:1856].rearrange("p (t a d n) -> p t a d n", t=NT, a=4, d=2)
        pgf = acc[:, 1856:1984].rearrange("p (t n) -> p t n", t=NT)
        pq = acc[:, 1984:3008].rearrange("p (t n) -> p t n", t=NT)
        pa = acc[:, 3008:4032].rearrange("p (t n) -> p t n", t=NT)
        pk = acc[:, 4032:5056].rearrange("p (t n) -> p t n", t=NT)
        zc = acc[:, 5056:6016].rearrange("p (a h m b) -> p a h m b", a=2, h=2, m=CL // 2)
        qa = at("qa", [P, NT, A_H, HD], A_MIX + 0)
        kad = at("kad", [P, NT, A_KV, 2, HD], A_MIX + 512)
        qr = at("qr", [P, NT, C_H, HD], A_MIX + 1024)
        krd = at("krd", [P, NT, 4, 2, HD], A_MIX + 2048)
        qb = at("qb", [P, NT, B_H, 96], A_MIX + 3072)
        kvb = at("kvb", [P, NT, B_H, P], A_MIX + 6656)
        kb = at("kb", [P, NT, B_H, 96], A_MIX + 3840)
        latT = at("latT", [P, 3, SEQ], A_MIX + 4608)
        gfT = at("gfT", [HD, SEQ], A_MIX + 5376)
        qaT = at("qaT", [P, 2, SEQ], A_MIX + 7680)
        kaT = at("kaT", [P, 2, SEQ], A_MIX + 8192)
        cqT = at("cqT", [P, 4, SEQ], A_MIX + 5632)
        crT = at("crT", [P, 4, SEQ], A_MIX + 8704)
        ckT = at("ckT", [P, 4, SEQ], A_MIX + 9728)
        qbT = at("qbT", [96, B_H, SEQ], A_MIX + 10752)
        kbT = at("kbT", [96, B_H, SEQ], A_MIX + 11776)
        hidk = sb("hidk", [P, 2, 16])
        hidv = sb("hidv", [P, 2, 4, 32])
        kcn = sb("kcn", [16, 2, HD])
        kcd = sb("kcd", [P, 2, 2, HD])
        kcT = sb("kcT", [P, 2, P])
        vrep = at("vrep", [P, 2, HD], A_MIX + 13312)
        gt = sb("gt", [P, NT, 24])
        latg = sb("latg", [P, 3])
        pe2 = sb("pe2", [P, 32])
        cmpT = at("cmpT", [P, 2, SEQ], A_MIX + 12800)
        msum = sb("msum", [P, 48])
        stat = sb("stat", [P, 4, 8])
        E = sq[:, 0:1152].rearrange("p (r n) -> p r n", r=3)
        ET = sq[:, 1152:1920].rearrange("p (r n) -> p r n", r=2)
        T1 = sq[:, 0:1024]
        T2 = sq[:, 1024:2048]
        cp = fs[:, :, :].rearrange("p a (h b) -> p a h b", h=C_H)
        csc = fa[:, :, 0:C_H * NCMP].rearrange("p a (h b) -> p a h b", h=C_H)
        trg = cqT[:, 0:3, :].rearrange("p a n -> p (a n)")
        cst16 = sb("cst16", [P, 3, NT * C_H])

        ps = ctx.enter_context(nc.psum_tensor("ps", [P, 8, 512], F32))
        y = ps[:, 4:8, :].rearrange("p b (e n) -> p (b e) n", e=2)

        s_const, s_pos, s_x, s_rows, s_small = (sem(n) for n in ("const", "pos", "xin", "rows", "smallw"))
        wide_in = [sem("wide_in0"), sem("wide_in1")]
        tall_in = [sem("tall_in0"), sem("tall_in1")]
        ada_in = [sem("ada_in0"), sem("ada_in1")]
        first_in = [sem("first_in0"), sem("first_in1")]
        h_in, tables, pool_s = sem("h_in"), sem("tables"), sem("pool_chain")
        wide_used, tall_used, ada_used = sem("wide_used"), sem("tall_used"), sem("ada_used")
        setup, turned, cond_ok, trig, trig_in = (sem(n) for n in ("setup", "turned", "cond", "trig", "trigin"))
        h_ready, sq_ready, ss_ready, diag_ready, r_ready = (
            sem(n) for n in ("h_ready", "sq_ready", "ss_ready", "diag_ready", "r_ready"))
        hn_ready, u_ready = sem("hn_ready"), sem("u_ready")
        gu_ready, silu_ready, mul_ready, y_ready = (
            sem(n) for n in ("gu_ready", "silu_ready", "mul_ready", "y_ready"))
        ul_ready, wh_ready, wl_ready, th_ready, tl_ready, mix_done = (
            sem(n) for n in ("ul_ready", "wh_ready", "wl_ready", "th_ready", "tl_ready", "mix_done"))
        acc_zero, acc_ready, mod_ps, mod_red, mod_ready = (
            sem(n) for n in ("acc_zero", "acc_ready", "mod_ps", "mod_red", "mod_ready"))
        proj, pcopy, aux_ready, aux_act, aux_dve = (
            sem(n) for n in ("proj", "pcopy", "aux_ready", "aux_act", "aux_dve"))
        prep, fa_s, fh_s, oh_s = sem("prep"), sem("fa"), sem("fh"), sem("oh")
        cmp_shift, cmp_exp = sem("cmp_shift"), sem("cmp_exp")
        gate_exp, mod_lat = sem("gate_exp"), sem("mod_lat")
        s_ready, nm_ready, exp_ready, en_ready, pt_ready, et_ready, pv_ready, o_ready = (
            sem(n) for n in ("s_ready", "nm_ready", "exp_ready", "en_ready", "pt_ready", "et_ready",
                             "pv_ready", "o_ready"))
        out_ps, out_sb, s_out = sem("out_ps"), sem("out_sb"), sem("out")
        chain_s = sem("chain")

        ident = cst[:, C_ID:C_ID + P]

        def wide_wait(eng, l, n):
            eng.wait_ge(wide_in[n % 2], l * (WIDE // 2 * 32) + 32 * (n // 2 + 1))

        PREP = ["lat", "qa", "qb", "kb", "kc", "cq", "cr", "ck", "cmp"]

        def landed(l, it, n0, per_layer, loads):
            return l * (per_layer // 2 * loads) + loads * ((n0 + it[0]) // 2 + 1) + loads * it[1]

        def tile_at(l, f, m, i=0):
            return l * (4 * NPAIR) + (2 * NPAIR * f + m + 1) + 4 * i

        def rows_at(l, j, m, i=0):
            return l * (4 * NPAIR + KD) + ((0, 2 * NPAIR, 2 * NPAIR + KD)[j] + m + 1) + 4 * i

        def projected(l, fill):
            return l * 2 * len(CHUNKS) + 2 * (CHUNKS.index(fill) + 1)

        def prep_at(l, name):
            return l * len(PREP) + PREP.index(name) + 1

        def aux_bank(name):
            return 4 + AUXN.index(name) % 4

        def aux_done(name, l):
            g = AUXN.index(name)
            who = AUX[g][1]
            count = sum(e == who for _, e in AUX[:g + 1])
            return (aux_act, l * AUX_ACT + count) if who == "act" else (aux_dve, l * AUX_DVE + count)

        def aux_at(l, name):
            return l * len(AUX) + AUXN.index(name) + 1

        def job(n):
            br, hh = JOBS[n]
            half = slice(64 * (hh % 2), 64 * (hh % 2) + 64)
            if br == "a":
                return (qaT[half, hh // 2, :], kaT[half, hh // 2, :],
                        lambda t: pa[:, t, 384 + hh // 2 * HD:384 + hh // 2 * HD + HD], mband, SC64)
            if br == "b":
                return qbT[:, hh, :], kbT[:, hh, :], lambda t: kvb[:, t, hh, HD:P], mcausal, SC96
            win = int(br == "win")
            kv = hh // 4
            off = 256 + 128 * win + kv * HD
            return (crT[half, hh // 2, :], ckT[half, 2 * win + kv, :],
                    lambda t: pk[:, t, off:off + HD], mcausal, SC64)

        block = ctx.enter_context(nc.Block())

        @block.sync
        def _(sp):
            def fill_wide(l, n, loads, free):
                sp.wait_ge(*free)
                for dst, src in loads:
                    sp.dma_start(dst, src).then_inc(wide_in[n % 2], 16)

            def fill_tall(l, n, src):
                sp.wait_ge(tall_used, l * TALL + n + 1)
                sp.dma_start(tall[:, n % 2, :].rearrange("p (a n) -> p a n", a=2), src)\
                    .then_inc(tall_in[n % 2], 16)

            def fill_ada(count, slot, width, src):
                sp.wait_ge(ada_used, count + 1)
                sp.dma_start(ada[:, slot, 0:width], src).then_inc(ada_in[slot], 16)

            def ffn_pair(l, f, it, q, ada_row=None, first=False):
                n0, m0 = (WIDE_A, TALL_A) if f == 0 else (WIDE_B, TALL_B)
                ws, ts = (n0 + q) % 2, (m0 + q) % 2
                slot = wide[:, ws, :].rearrange("p (e k n) -> p e k n", e=2, k=KD)
                if first and f == 1:
                    sp.wait_ge(proj, projected(l, F_CQ))
                else:
                    sp.wait_ge(wide_used, (2 * l + f) * NPAIR + it + 1)
                for e in range(2):
                    if first and f == 1 and e == 1:
                        sp.wait_ge(proj, projected(l, F_CK))
                    src = ffn_w_in[l, f, :, bass.ds(e * DFF + it * 256, 256)].rearrange(
                        "(k p) n -> p k n", p=P)
                    sp.dma_start(slot[:, e, :, :], src).then_inc(wide_in[ws], 16)
                if ada_row is not None:
                    ada_piece(l, f, ada_row, 0)
                sp.wait_ge(tall_used, l * TALL + m0 + it + 1)
                src = ffn_w_out[l, f, bass.ds(it * 256, 256), :].rearrange("(a p) n -> p a n", p=P)
                sp.dma_start(tall[:, ts, :].rearrange("p (a n) -> p a n", a=2), src).then_inc(tall_in[ts], 16)
                if ada_row is not None:
                    ada_piece(l, f, ada_row, 1)

            def ada_piece(l, f, i, e):
                count = l * ADA_L + (ADA_PRO + f * 2 * KD + e) + 2 * i
                if f == 0:
                    src = ada_w[l, bass.ds(i * P, P), 3 * DM * (e + 1):3 * DM * (e + 2)]
                    fill_ada(count, e, 3 * DM, src)
                else:
                    src = ada_w[l + 1, bass.ds(i * P, P), 1536 * e:1536 * (e + 1)]
                    fill_ada(count, e, 1536, src)

            def ffn(l, f, last=False):
                ffn_pair(l, f, 0, 0, None, True)
                with sp.Fori(0, KD // 2) as i:
                    for q in range(2):
                        ffn_pair(l, f, 2 * i + q + 1, (q + 1) % 2, None if last else 2 * i + q)
                for it in range(KD + 1, NPAIR):
                    ffn_pair(l, f, it, it % 2)

            for r0, src in ((0, norm_g.rearrange("l j (k n) -> (l j k) n", n=P)),
                            (48, c.rearrange("a (k n) -> (a k) n", n=P)),
                            (56, b_q_lat_g.rearrange("l (k n) -> (l k) n", n=P)),
                            (60, b_kv_lat_g[:, :]),
                            (62, c_cmp_pe.rearrange("l a (m e) n -> (l a m) (e n)", e=2))):
                sp.dma_start(rows[r0:r0 + src.shape[0], 0, :], src).then_inc(s_rows, 16)
            for l in range(DEPTH):
                sp.dma_start(rows[0:72, 1 + l, :], ada_b[l].rearrange("(k n) -> k n", n=P)).then_inc(s_rows, 16)
            n = 0
            for k in range(KD):
                src = ada_w[0, k * P:(k + 1) * P, 0:3 * DM]
                if k in (2, 3):
                    sp.dma_start(wide[:, k - 2, 0:3 * DM], src).then_inc(first_in[k - 2], 16)
                else:
                    fill_ada(n, n % 2, 3 * DM, src)
                    n += 1
            def layer(l, last=False):
                bc = lambda ap: ap.partition_broadcast(P)
                for lo, hi, src in ((G_A, G_C, a_qk_g[l].rearrange("a b -> (a b)")),
                                    (G_C, G_BN, c_qk_g[l].rearrange("a b -> (a b)")),
                                    (G_BN, G_BR, b_qk_nope_g[l].rearrange("a b -> (a b)")),
                                    (G_BR, G_SINK, b_qk_rope_g[l].rearrange("a b -> (a b)")),
                                    (G_SINK, G_GB, a_sinks[l]), (G_GB, G_END, c_gate_b[l])):
                    sp.dma_start(gn[:, lo:hi], bc(src)).then_inc(s_small, 16)
                sp.dma_start(uq[:, :, :], b_w_uq[l].rearrange("(k p) n -> p k n", p=P)).then_inc(s_small, 16)
                sp.dma_start(ukv[:, :], b_w_ukv[l]).then_inc(s_small, 16)
                sp.dma_start(w2[:, :, :], c_cmp_w2[l].rearrange("a p n -> p a n")).then_inc(s_small, 16)
                sp.dma_start(gw[:, :], c_gate_w[l]).then_inc(s_small, 16)
                ffn(l, 0)

                def cols(n, off, lo, hi, rest=None):
                    width = rest or hi - lo
                    slot = wide[:, n % 2, 0:KD * width].rearrange("p (k n) -> p k n", k=KD)
                    return slot[:, :, off:off + hi - lo], w_in[l, :, lo:hi].rearrange("(k p) n -> p k n", p=P)

                n = WIDE_M
                fill_wide(l, n, [cols(n, 0, 512, 720, 416), cols(n, 208, 720, 928, 416)],
                          (wide_used, (2 * l + 1) * NPAIR + 1))
                n += 1
                fill_wide(l, n, [cols(n, 0, 1440, 1696, 320), cols(n, 256, 2208, 2272, 320)],
                          (wide_used, (2 * l + 1) * NPAIR + 2))
                n += 1
                fill_wide(l, n, [cols(n, 256, 256, 512, 512), cols(n, 0, 0, 256, 512)],
                          (proj, projected(l, F_LAT)))
                fill_tall(l, TALL_M, w_out[l, 0:256, :].rearrange("(a p) n -> p a n", p=P))
                n += 1
                w1 = wide[:, n % 2, :].rearrange("p (m n) -> p m n", n=P)
                w1_src = c_cmp_w1[l].rearrange("a (m p) n -> p (a m) n", p=P)
                fill_wide(l, n, [(w1[r:r + 64, :, :], w1_src[r:r + 64, :, :]) for r in (0, 64)],
                          (proj, projected(l, F_CMPIN)))
                n += 1
                fill_wide(l, n, [cols(n, 0, 928, 1184, 512), cols(n, 256, 1184, 1440, 512)],
                          (proj, projected(l, F_A)))
                n += 1
                fill_wide(l, n, [cols(n, 0, 1696, 1952, 512), cols(n, 256, 1952, 2208, 512)],
                          (aux_ready, aux_at(l, "hid")))
                for m in range(1, 4):
                    fill_tall(l, TALL_M + m, w_out[l, m * 256:(m + 1) * 256, :].rearrange("(a p) n -> p a n", p=P))
                ffn(l, 1, last)

            with sp.Fori(0, DEPTH - 1) as l:
                layer(l)
            layer(DEPTH - 1, True)
            o = u[:, :, :].rearrange("p (t j) n -> p t (j n)", t=NT)
            for t in range(NT):
                sp.wait_ge(out_sb, 2 * t + 2)
                sp.dma_start(out[0, t * P:(t + 1) * P, :], o[:, t, :]).then_inc(s_out, 16)
            sp.wait_ge(s_out, 16 * NT)

        @block.tensor
        def _(pe):
            mm, tr = nc.tensor.matmul, nc.tensor.transpose

            def keep_warm(n):
                for _ in range(n):
                    mm(ps[:, 0, :], zb[:, 0:P], zb[:, :], start=True, stop=True)

            def norm_stats(l, j):
                for k in range(KD):
                    pe.wait_ge(sq_ready, l * 24 + (8 * j + k + 1))
                    for t in range(NT):
                        i = mm(ps[:, 2 + t, 0:1], sq[:, k * SEQ + t * P:k * SEQ + t * P + P], ones[:, 0:1],
                               start=(k == 0), stop=(k == KD - 1))
                i.then_inc(ss_ready, 1)
                if j == 0:
                    pe.wait_ge(mod_ready, 1)
                keep_warm(10)
                pe.wait_ge(diag_ready, l * 3 + (j + 1))
                for t in range(NT):
                    i = mm(ps[:, 2, t * P:(t + 1) * P], ones[:, :], T1[:, t * P:(t + 1) * P], start=True, stop=True)
                i.then_inc(r_ready, 1)

            def open_y():
                for b in range(4):
                    i = mm(ps[:, 4 + b, :], zb[:, 0:P], zb[:, :], start=True, stop=False, skip_group_check=True)

            def gate_up(l, f, m, i=0):
                a = m % 2
                for e in range(2):
                    o = ps[:, a, e * SEQ:(e + 1) * SEQ]
                    for part in range(3):
                        w, v = (wl if part == 2 else wh), (ul if part == 1 else uh)
                        for k in range(KD):
                            if e == 0 and part == 0 and k == 0:
                                pe.wait_ge(wl_ready, tile_at(l, f, m, i))
                            q = mm(o, w[:, a, e, k, :], v[:, k, :], start=(part == 0 and k == 0),
                                   stop=(part == 2 and k == KD - 1))
                q.then_inc(gu_ready, 1)

            def gate_up_first(l, f):
                mm(ps[:, 0, :], zb[:, 0:P], zb[:, :], start=True, stop=False, skip_group_check=True)
                for w, v in ((wh, uh), (wl, uh), (wh, ul)):
                    for k in range(KD):
                        if w is wh and v is uh:
                            if k == 0:
                                pe.wait_ge(wh_ready, tile_at(l, f, 0))
                            pe.wait_ge(u_ready, l * 24 + (16 * f + k + 1))
                        elif w is wl and k == 0:
                            pe.wait_ge(wl_ready, tile_at(l, f, 0))
                        elif v is ul:
                            pe.wait_ge(ul_ready, l * 16 + (8 * f + k + 1))
                        for e in range(2):
                            i = mm(ps[:, 0, e * SEQ:(e + 1) * SEQ], w[:, 0, e, k, :], v[:, k, :], start=False,
                                   stop=False, skip_group_check=True)
                i.then_inc(gu_ready, 1)

            def add_rows(a, hi, lo, last, done=None, tiles=range(KD)):
                for d in tiles:
                    cols = slice(d * P, (d + 1) * P)
                    mm(y[:, d, :], th[:, a, cols], hi, start=False, stop=False, skip_group_check=True)
                    mm(y[:, d, :], th[:, a, cols], lo, start=False, stop=False, skip_group_check=True)
                    i = mm(y[:, d, :], tl[:, a, cols], hi, start=False, stop=False, skip_group_check=True)
                    if last and d % 2:
                        i.then_inc(y_ready, 1)
                    elif done is not None and d == KD - 1:
                        i.then_inc(done, 1)

            def down(l, f, m, i=0):
                a = m % 2
                pe.wait_ge(tl_ready, rows_at(l, 2 * f, m, i))
                pe.wait_ge(mul_ready, tile_at(l, f, m, i))
                add_rows(a, fh[:, a, :], fl[:, a, :], m == 2 * NPAIR - 1)

            def sum_parts(l, f, r):
                if r == 0:
                    pe.wait_ge(acc_ready, l * 2 + (f + 2))
                if r >= 2:
                    pe.wait_ge(mod_red, l * 18 + (12 * f + r - 1))
                for v in range(4):
                    i = tr(ps[:, 2 + r % 2, v * P:(v + 1) * P], acc[:, (4 * r + v) * P:(4 * r + v + 1) * P], ident)
                i.then_inc(mod_ps, 1)

            def ffn(l, f, last=False):
                norm_stats(l, 2 * f)
                open_y()
                gate_up_first(l, f)
                with pe.Fori(0, KD // 2) as i:
                    for q in range(4):
                        gate_up(l, f, q + 1, i)
                        down(l, f, q, i)
                for m in range(2 * KD, 2 * NPAIR):
                    if m + 1 < 2 * NPAIR:
                        gate_up(l, f, m + 1)
                    for r in range(2 * (m - 2 * KD), 2 * (m - 2 * KD) + 2):
                        if r < 12 - 6 * f and not last:
                            sum_parts(l, f, r)
                    down(l, f, m)

            def aux_open(l, name):
                g = AUXN.index(name)
                if g >= 4:
                    pe.wait_ge(*aux_done(AUXN[g - 4], l))
                return ps[:, 4 + g % 4, :]

            def project(l, fill, width, banks):
                n = WIDE_M + fill
                wv = wide[:, n % 2, 0:KD * width].rearrange("p (k n) -> p k n", k=KD)
                wide_wait(pe, l, n)
                c = CHUNKS.index(fill)
                if c >= 2:
                    pe.wait_ge(pcopy, l * 2 * len(CHUNKS) + 2 * (c - 1))
                for t in range(NT):
                    for k in range(KD):
                        if fill == F_LAT and t == 0:
                            pe.wait_ge(u_ready, l * 24 + (8 + k + 1))
                        i = mm(ps[:, banks + t, 0:width], u[:, k, t * P:(t + 1) * P], wv[:, k, :],
                               start=(k == 0), stop=(k == KD - 1))
                    i.then_inc(proj, 1)

            def turn(l, name, blocks):
                bank = aux_open(l, name)
                for col, src in blocks:
                    rows_, width = src.shape[0], src.shape[-1]
                    i = tr(bank[0:width, col:col + rows_], src, ident[0:rows_, 0:rows_])
                i.then_inc(aux_ready, 1)

            def scores(l, n):
                q, k, _, mask, _ = job(n)
                bank = ps[:, n % 2, 0:3 * P]
                if n >= 2:
                    pe.wait_ge(exp_ready, l * NJ + (n - 1))
                mm(bank, idb[:, :], mask[:, :], start=True, stop=False, skip_group_check=True)
                mm(bank[:, 0:P], q[:, 0:P], k[:, 0:P], start=False, stop=False, skip_group_check=True)
                mm(bank[:, P:3 * P], q[:, P:2 * P], k[:, :], start=False, stop=True,
                   skip_group_check=True).then_inc(s_ready, 1)

            def turn_probs(l, n):
                pe.wait_ge(en_ready, l * NJ + (n + 1))
                if n >= 1:
                    pe.wait_ge(et_ready, l * NJ + n)
                for b in range(3):
                    i = tr(ps[:, 2, b * P:(b + 1) * P], E[:, n % 3, b * P:(b + 1) * P], ident)
                i.then_inc(pt_ready, 1)

            def values(l, n):
                _, _, v, _, _ = job(n)
                br, hh = JOBS[n]
                o = ps[64 * (hh % 2):64 * (hh % 2) + 64, 3, 0:SEQ]
                pair = sum(m < n for m in LAST)
                first = n == 0 or JOBS[n - 1][1] != hh
                if first and hh % 2 == 0 and pair:
                    pe.wait_ge(o_ready, l * 8 + pair)
                pe.wait_ge(et_ready, l * NJ + (n + 1))
                mm(o, v(0), ET[:, n % 2, 0:SEQ], start=first, stop=False, skip_group_check=True)
                i = mm(o[:, P:SEQ], v(1), ET[:, n % 2, SEQ:3 * P], start=False, stop=False, skip_group_check=True)
                if br == "win":
                    r = slice(32 * (hh % 4), 32 * (hh % 4) + 32)
                    if hh == 0:
                        pe.wait_ge(*aux_done("cmpt", l))
                    i = mm(o, vrep[r, hh // 4, :], cmpT[r, hh // 4, :], start=False, stop=True, skip_group_check=True)
                i.then_inc(pv_ready, 1)

            def mix_out(l, k, part, parts):
                if k == 0 and part == 0:
                    pe.wait_ge(*aux_done("kw", l))
                    pe.wait_ge(*aux_done("cmpt", l))
                    open_y()
                if part == 0:
                    pe.wait_ge(tl_ready, rows_at(l, 1, k))
                    pe.wait_ge(o_ready, l * 8 + (k + 1))
                add_rows(k % 2, uh[:, k, :], ol[:, k, :], k == KD - 1, mix_done,
                         range(part * KD // parts, (part + 1) * KD // parts))

            def mixer(l):
                norm_stats(l, 1)
                project(l, F_LAT, 416, 0)
                project(l, F_CMPIN, 320, 2)
                pe.wait_ge(pcopy, l * 10 + 4)
                for a, name in enumerate(("zk", "zv")):
                    turn(l, name, [(hh * SEQ + t * P, pz[:, t, 2 * a + hh, :, :].rearrange("p d n -> p (d n)"))
                                   for hh in range(2) for t in range(NT)])
                pe.wait_ge(prep, prep_at(l, "lat"))
                turn(l, "lat", [(b * SEQ + t * P, plat[:, t, b * P:(b + 1) * P]) for b in range(2) for t in range(NT)])
                turn(l, "kvgf", [(t * P, plat[:, t, 256:384]) for t in range(NT)]
                     + [(SEQ + t * P, pgf[:, t, :]) for t in range(NT)])
                project(l, F_A, 512, 0)
                pe.wait_ge(*aux_done("lat", l))
                pe.wait_ge(*aux_done("kvgf", l))
                pe.wait_ge(s_small, (l + 1) * 160)
                for t in range(NT):
                    bank = aux_open(l, f"uq{t}")
                    for k in range(2):
                        i = mm(bank[:, 0:384], latT[:, k, t * P:(t + 1) * P], uq[:, k, :], start=(k == 0), stop=(k == 1))
                    i.then_inc(aux_ready, 1)
                for t in range(NT):
                    bank = aux_open(l, f"ukv{t}")
                    mm(bank, latT[:, 2, t * P:(t + 1) * P], ukv[:, :], start=True, stop=True).then_inc(aux_ready, 1)
                bank = aux_open(l, "gate")
                for t in range(NT):
                    i = mm(bank[:, t * 24:(t + 1) * 24], gfT[:, t * P:(t + 1) * P], gw[:, :], start=True, stop=True)
                i.then_inc(aux_ready, 1)
                n = WIDE_M + F_CMPW
                w1 = wide[:, n % 2, :].rearrange("p (a m n) -> p a m n", a=2, m=CL // 2)
                bank = aux_open(l, "hid")
                pe.wait_ge(*aux_done("zv", l))
                wide_wait(pe, l, n)
                for a in range(2):
                    for m in range(CL // 2):
                        i = mm(bank[:, 32 * a:32 * a + 2 * NCMP], w1[:, a, m, :], zc[:, a, :, m, :],
                               start=(m == 0), stop=(m == CL // 2 - 1))
                i.then_inc(aux_ready, 1)

                def pairs(name, src, heads):
                    turn(l, name, [(b * SEQ + t * P, src[:, t, 2 * hp:2 * hp + 2, :].rearrange("p a n -> p (a n)"))
                                   for b, hp in enumerate(heads) for t in range(NT)])

                def doubled(name, src, g0):
                    turn(l, name, [(b * SEQ + t * P, src[:, t, g0 + b, :, :].rearrange("p a n -> p (a n)"))
                                   for b in range(2) for t in range(NT)])

                pe.wait_ge(prep, prep_at(l, "qa"))
                pairs("qa", qa, (0, 1))
                doubled("ka", kad, 0)
                bank = aux_open(l, "w2")
                pe.wait_ge(*aux_done("hid", l))
                for g in range(2):
                    mm(bank[0:NCMP, g * HD:(g + 1) * HD], hidk[:, g, 0:NCMP], w2[:, 0, :], start=True, stop=True)
                for g in range(2):
                    i = mm(bank[:, (2 + g) * HD:(3 + g) * HD], hidv[:, g, :, :].rearrange("p r b -> p (r b)"),
                           w2[:, 1, :], start=True, stop=True)
                i.then_inc(aux_ready, 1)
                project(l, F_CQ, 512, 2)
                for nm, src in (("qb", qb), ("kb", kb)):
                    pe.wait_ge(prep, prep_at(l, nm))
                    for g in range(2):
                        turn(l, f"{nm}{g}", [(b * SEQ + t * P, src[:, t, 2 * g + b, :]) for b in range(2)
                                             for t in range(NT)])
                pe.wait_ge(prep, prep_at(l, "kc"))
                turn(l, "kc", [(P * g, kcd[:, g, :, :].rearrange("p a n -> p (a n)")) for g in range(2)])
                project(l, F_CK, 512, 0)
                cq = pq[:, :, :].rearrange("p t (a n) -> p t a n", a=C_H)
                pe.wait_ge(prep, prep_at(l, "cq"))
                pairs("cq0", cq, (0, 1))
                pairs("cq1", cq, (2, 3))
                pe.wait_ge(*aux_done("cq1", l))
                for odd in range(2):
                    bank = aux_open(l, f"cmps{odd}")
                    half = slice(64 * odd, 64 * odd + 64)
                    for t in range(NT):
                        for hp in range(C_H // 2):
                            col = (t * C_H // 2 + hp) * 16
                            i = mm(bank[:, col:col + NCMP], cqT[half, hp, t * P:(t + 1) * P],
                                   kcT[half, hp // 2, 0:NCMP], start=True, stop=True)
                    i.then_inc(aux_ready, 1)
                pe.wait_ge(prep, prep_at(l, "cr"))
                pairs("cr0", qr, (0, 1))
                pairs("cr1", qr, (2, 3))
                pe.wait_ge(prep, prep_at(l, "ck"))
                doubled("ks", krd, 0)
                doubled("kw", krd, 2)
                pe.wait_ge(pcopy, l * 10 + 10)
                for n in range(NJ + 3):
                    if n < NJ:
                        if n in (0, A_H, A_H + B_H):
                            pe.wait_ge(*aux_done({0: "ka", A_H: "kb1", A_H + B_H: "kw"}[n], l))
                        scores(l, n)
                    if 0 <= n - 2 < NJ:
                        turn_probs(l, n - 2)
                    if n >= 3:
                        values(l, n - 3)
                    if n == 4:
                        pe.wait_ge(prep, prep_at(l, "cmp"))
                        turn(l, "cmpt", [(g * SEQ + t * P, cp[:, t, 4 * g:4 * g + 4, :].rearrange("p a n -> p (a n)"))
                                         for g in range(2) for t in range(NT)])
                    for k in range(KD):
                        parts = 2 if JOBS[LAST[k]][0] in "ab" else 4
                        for part in range(parts):
                            if n == min(LAST[k] + 5 + part, NJ + 2):
                                mix_out(l, k, part, parts)

            pe.wait_ge(setup, 1)
            pe.wait_ge(s_const, 16)
            pe.wait_ge(s_rows, 16 * 7)
            for r in range(3):
                m = (126, 72, 72)[r]
                i = tr(ps[:, 0, r * P:r * P + m], rows[0:m, r, :], ident[0:m, 0:m])
            i.then_inc(turned, 1)
            pe.wait_ge(s_x, 32)
            xs = u[:, :, :].rearrange("p (t j) n -> p t (j n)", t=NT)
            for b in range(4):
                for e in range(2):
                    for t in range(NT):
                        k = 2 * b + e
                        i = tr(y[:, k, t * P:(t + 1) * P], xs[:, t, k * P:(k + 1) * P], ident)
                i.then_inc(turned, 1)
            pe.wait_ge(acc_ready, 1)
            pe.wait_ge(h_ready, KD)
            for r in range(6):
                for v in range(4):
                    i = tr(ps[:, PRO_BANKS[r], v * P:(v + 1) * P], acc[:, (4 * r + v) * P:(4 * r + v + 1) * P], ident)
                i.then_inc(mod_ps, 1)
            with pe.Fori(0, DEPTH - 1) as l:
                ffn(l, 0)
                mixer(l)
                ffn(l, 1)
            ffn(DEPTH - 1, 0)
            mixer(DEPTH - 1)
            ffn(DEPTH - 1, 1, True)
            pe.wait_ge(h_ready, 8 + 24 * DEPTH)
            for t in range(NT):
                for b in range(2):
                    for k in range(4):
                        i = tr(ps[:, 2 * t + b, k * P:(k + 1) * P], h[:, 4 * b + k, t * P:(t + 1) * P], ident)
                    i.then_inc(out_ps, 1)

        @block.scalar
        def _(act):
            A = nc.scalar.activation
            act.dma_start(cst[:, :], consts[:, :]).then_inc(s_const, 16)
            xs = u[:, :, :].rearrange("p (t j) n -> p t (j n)", t=NT)
            for t in range(NT):
                act.dma_start(xs[:, t, :], x[0, t * P:(t + 1) * P, :]).then_inc(s_x, 16)
            act.dma_start(posi[:, :], positions.rearrange("a (t p) -> p (a t)", p=P),
                          allow_slow_non_contiguous=True).then_inc(s_pos, 16)

            act.wait_ge(turned, 1)
            A(cond[:, :], ps[:, 0, 48:56], ACT.Silu).then_inc(cond_ok, 1)
            for b in range(4):
                act.wait_ge(turned, b + 2)
                nc.scalar.copy(h[:, 2 * b:2 * b + 2, :], y[:, 2 * b:2 * b + 2, :]).then_inc(h_in, 1)
            act.wait_ge(trig_in, 1)
            A(trg[:, 0:192], trg[:, 0:192], ACT.Sin).then_inc(trig, 1)

            def squares(l, j):
                for k in range(KD):
                    act.wait_ge(h_ready, l * 24 + (8 * j + k + 1))
                    A(sq[:, k * SEQ:(k + 1) * SEQ], h[:, k, :], ACT.Square).then_inc(sq_ready, 1)

            def shift(l, j, dst):
                act.wait_ge(mod_ready, l * 3 + (j + 1))
                for k in range(KD):
                    act.wait_ge(hn_ready, l * 24 + (8 * j + k + 1))
                    A(dst[:, k, :], sq[:, k * SEQ:(k + 1) * SEQ], ACT.Identity, bias=mod[:, j, 0, k:k + 1])\
                        .then_inc(u_ready, 1)

            def round_wide(l, f, n0, m, i=0):
                it, a = m // 2, m % 2
                slot = (n0 + it) % 2
                if a == 0:
                    act.wait_ge(wide_in[slot], landed(l, (it, i), n0, WIDE, 32))
                raw = wide[:, slot, :].rearrange("p (g n) -> p g n", n=2 * P)[:, :, a * P:(a + 1) * P]
                nc.scalar.copy(wh[:, a, :, :, :].rearrange("p e k n -> p (e k) n"), raw).then_inc(wh_ready, 1)

            def round_tall(l, j, m0, m, i=0):
                it, a = m // 2, m % 2
                slot = (m0 + it) % 2
                if a == 0:
                    act.wait_ge(tall_in[slot], landed(l, (it, i), m0, TALL, 16))
                nc.scalar.copy(th[:, a, :], tall[:, slot, a * DM:(a + 1) * DM]).then_inc(th_ready, 1)

            def ffn(l, f, last=False):
                n0, m0 = (WIDE_A, TALL_A) if f == 0 else (WIDE_B, TALL_B)
                squares(l, 2 * f)
                if f == 0:
                    round_wide(l, f, n0, 0)
                    round_wide(l, f, n0, 1)
                shift(l, 2 * f, uh)
                if not last:
                    width = (2 - f) * 3 * DM
                    nc.scalar.copy(acc[:, 0:width], zb[:, 0:1].broadcast_to([P, width])).then_inc(acc_zero, 1)

                def tile(m, i=0):
                    act.wait_ge(gu_ready, tile_at(l, f, m, i))
                    A(fs[:, m % 2, :], ps[:, m % 2, 0:SEQ], ACT.Silu).then_inc(silu_ready, 1)
                    round_tall(l, 2 * f, m0, m, i)
                    if m + 2 < 2 * NPAIR:
                        round_wide(l, f, n0, m + 2, i)

                with act.Fori(0, KD // 2) as i:
                    for q in range(4):
                        tile(q, i)
                for m in range(2 * KD, 2 * NPAIR):
                    tile(m)

            def copy_proj(l, chunk):
                fill = CHUNKS[chunk]
                bank = 2 * (chunk % 2)
                for t in range(NT):
                    act.wait_ge(proj, l * 2 * len(CHUNKS) + (2 * chunk + t + 1))
                    src = ps[:, bank + t, :]
                    if fill == F_LAT:
                        nc.scalar.copy(plat[:, t, :], src[:, 0:416]).then_inc(pcopy, 1)
                    elif fill == F_CMPIN:
                        A(pgf[:, t, :], src[:, 256:320], ACT.Silu)
                        nc.scalar.copy(pz[:, t, :, :, :], src[:, 0:256].rearrange("p (a n) -> p a n", a=4)
                                       .unsqueeze(2).broadcast_to([P, 4, 2, HD])).then_inc(pcopy, 1)
                    elif fill == F_CK:
                        nc.scalar.copy(pk[:, t, :].rearrange("p (b a n) -> p a b n", a=2, b=2),
                                       src.rearrange("p (a b n) -> p a b n", a=2, b=2)).then_inc(pcopy, 1)
                    else:
                        dst = {F_A: pa, F_CQ: pq}[fill]
                        nc.scalar.copy(dst[:, t, :], src).then_inc(pcopy, 1)

            def aux_wait(l, name):
                act.wait_ge(aux_ready, aux_at(l, name))

            def out_of(l, name, dst, width=P):
                aux_wait(l, name)
                src = ps[0:width, aux_bank(name), :].rearrange("p (b n) -> p b n", b=2)
                nc.scalar.copy(dst, src).then_inc(aux_act, 1)

            def mixer(l):
                squares(l, 1)
                shift(l, 1, u)
                copy_proj(l, 0)
                copy_proj(l, 1)
                aux_wait(l, "kvgf")
                b = aux_bank("kvgf")
                act.wait_ge(mod_lat, l + 1)
                A(latT[:, 2, :], ps[:, b, 0:SEQ], ACT.Copy, scale=latg[:, 2:3])
                nc.scalar.copy(gfT[:, :], ps[0:HD, b, SEQ:2 * SEQ]).then_inc(aux_act, 1)
                copy_proj(l, 2)
                for t in range(NT):
                    aux_wait(l, f"uq{t}")
                    nc.scalar.copy(qb[:, t, :, :].rearrange("p a n -> p (a n)"), ps[:, aux_bank(f"uq{t}"), 0:384])\
                        .then_inc(aux_act, 1)
                for t in range(NT):
                    aux_wait(l, f"ukv{t}")
                    nc.scalar.copy(kvb[:, t, :, :].rearrange("p a n -> p (a n)"), ps[:, aux_bank(f"ukv{t}"), :])\
                        .then_inc(aux_act, 1)
                aux_wait(l, "hid")
                b = aux_bank("hid")
                A(hidk[:, :, 0:NCMP], ps[:, b, 0:2 * NCMP].rearrange("p (g b) -> p g b", g=2), ACT.Silu)
                A(hidv[:, :, :, 0:NCMP], ps[:, b, 32:32 + 2 * NCMP].rearrange("p (g b) -> p g b", g=2)
                  .unsqueeze(2).broadcast_to([P, 2, 4, NCMP]), ACT.Silu).then_inc(aux_act, 1)
                out_of(l, "qa", qaT[:, :, :])
                out_of(l, "ka", kaT[:, :, :])
                aux_wait(l, "w2")
                b = aux_bank("w2")
                nc.scalar.copy(kcn[0:NCMP, :, :], ps[0:NCMP, b, 0:P].rearrange("p (g n) -> p g n", g=2))
                nc.scalar.copy(vrep[:, :, :], ps[:, b, P:2 * P].rearrange("p (g n) -> p g n", g=2)).then_inc(aux_act, 1)
                copy_proj(l, 3)
                out_of(l, "qb0", qbT[:, 0:2, :], 96)
                out_of(l, "qb1", qbT[:, 2:4, :], 96)
                out_of(l, "kb0", kbT[:, 0:2, :], 96)
                out_of(l, "kb1", kbT[:, 2:4, :], 96)
                aux_wait(l, "kc")
                nc.scalar.copy(kcT[:, :, 0:NCMP], ps[:, aux_bank("kc"), 0:2 * P].rearrange("p (g b) -> p g b", g=2)
                               [:, :, 0:NCMP]).then_inc(aux_act, 1)
                copy_proj(l, 4)
                out_of(l, "cq0", cqT[:, 0:2, :])
                out_of(l, "cq1", cqT[:, 2:4, :])
                out_of(l, "cr0", crT[:, 0:2, :])
                out_of(l, "cr1", crT[:, 2:4, :])
                act.wait_ge(*aux_done("gate", l))
                A(gt[:, :, :], gt[:, :, :], ACT.Exp, scale=-1.0).then_inc(gate_exp, 1)
                act.wait_ge(cmp_shift, l + 1)
                A(csc, csc, ACT.Exp, scale=SC64).then_inc(cmp_exp, 1)
                out_of(l, "ks", ckT[:, 0:2, :])
                out_of(l, "kw", ckT[:, 2:4, :])
                for n in range(NJ + 2):
                    if n >= 2:
                        m = n - 2
                        act.wait_ge(pt_ready, l * NJ + (m + 1))
                        if m >= 2:
                            act.wait_ge(pv_ready, l * NJ + (m - 1))
                        nc.scalar.copy(ET[:, m % 2, :], ps[:, 2, 0:3 * P]).then_inc(et_ready, 1)
                    if n < NJ:
                        act.wait_ge(nm_ready, l * NJ + (n + 1))
                        st = stat[:, n % 4, :]
                        scale = job(n)[4]
                        bank = ps[:, n % 2, :]
                        if JOBS[n][0] == "a":
                            hh = JOBS[n][1]
                            A(st[:, 6:8], st[:, 2:4], ACT.Exp, bias=gn[:, G_SINK + hh:G_SINK + hh + 1])
                        A(E[:, n % 3, 0:P], bank[:, 0:P], ACT.Exp, bias=st[:, 2:3], scale=scale,
                          accum_out=st[:, 4:5])
                        A(E[:, n % 3, P:3 * P], bank[:, P:3 * P], ACT.Exp, bias=st[:, 3:4], scale=scale,
                          accum_out=st[:, 5:6]).then_inc(exp_ready, 1)
                    for k in range(KD):
                        if n == min(LAST[k] + 3, NJ + 1):
                            if k >= 2:
                                act.wait_ge(mix_done, l * (KD - 1) + (k - 1))
                            round_tall(l, 1, TALL_M, k)
                round_wide(l, 1, WIDE_B, 0)
                round_wide(l, 1, WIDE_B, 1)

            act.wait_ge(tables, 1)
            with act.Fori(0, DEPTH - 1) as l:
                ffn(l, 0)
                mixer(l)
                ffn(l, 1)
            ffn(DEPTH - 1, 0)
            mixer(DEPTH - 1)
            ffn(DEPTH - 1, 1, True)
            o = u[:, :, :].rearrange("p (b j) n -> p b (j n)", b=4)
            for b in range(4):
                act.wait_ge(out_ps, b + 1)
                nc.scalar.copy(o[:, b, :], ps[:, b, :]).then_inc(out_sb, 1)

        @block.gpsimd
        def _(pool):
            V = nc.gpsimd
            tt, ts = V.tensor_tensor, V.tensor_scalar
            chain = {"n": 0}

            def link(ins):
                chain["n"] += 1
                ins.then_inc(pool_s, 1)
                pool.wait_ge(pool_s, chain["n"])

            pool.wait_ge(s_const, 16)
            two_pi = 2.0 * np.pi
            c1 = 6.28125
            c2 = float(np.float32(two_pi - c1))
            c3 = float(np.float32(two_pi - c1 - np.float64(np.float32(two_pi - c1))))
            magic = 12582912.0
            angf = trg[:, 192:288]
            ang = angf.rearrange("p (t n) -> p t n", t=NT)
            kk = trg[:, 288:480].rearrange("p (e n) -> p e n", e=2)
            turns = trg[:, 480:672].rearrange("p (e n) -> p e n", e=2)
            rr = trg[:, 0:192].rearrange("p (e n) -> p e n", e=2)
            pool.wait_ge(s_pos, 16)
            link(V.tensor_copy(posf[:, :], posi[:, :]))
            link(tt(ang, cst[:, C_INVF:C_INVF + 48].unsqueeze(1).broadcast_to([P, NT, 48]),
                    posf[:, :].unsqueeze(2).broadcast_to([P, NT, 48]), ALU.mult))
            ts(kk[:, 0, :], angf, 1.0 / two_pi, 0.25, ALU.mult, ALU.add)
            link(ts(kk[:, 1, :], angf, 1.0 / two_pi, None, ALU.mult))
            link(ts(kk, kk, magic, None, ALU.add))
            link(ts(kk, kk, -magic, None, ALU.add))
            both = ang.rearrange("p t n -> p (t n)").unsqueeze(1).broadcast_to([P, 2, 96])
            for part, rest in ((c1, both), (c2, rr), (c3, rr)):
                link(ts(turns, kk, -part, None, ALU.mult))
                link(tt(rr, turns, rest, ALU.add))
            link(ts(rr[:, 0, :], rr[:, 0, :], two_pi / 4, None, ALU.add))
            for cmp, turn_ in ((ALU.is_gt, -two_pi), (ALU.is_lt, two_pi)):
                link(ts(kk, rr, float(np.float32(-turn_ / 2)), turn_, cmp, ALU.mult))
                link(tt(rr, rr, kk, ALU.add))
            ts(rr, rr, 3.1415925, -3.1415925, ALU.min, ALU.max).then_inc(trig_in, 1)
            pool.wait_ge(trig, 1)
            tv = rr.rearrange("p e (t n) -> p e t n", t=NT)
            for cs, lo, hf in ((cs64, 0, 32), (cs32, 32, 16)):
                V.tensor_copy(cs[:, 0, :, 0:hf], tv[:, 0, :, lo:lo + hf])
                V.tensor_copy(cs[:, 0, :, hf:2 * hf], tv[:, 0, :, lo:lo + hf])
                ts(cs[:, 1, :, 0:hf], tv[:, 1, :, lo:lo + hf], -1.0, None, ALU.mult)
                i = V.tensor_copy(cs[:, 1, :, hf:2 * hf], tv[:, 1, :, lo:lo + hf])
            i.then_inc(tables, 1)

        @block.vector
        def _(dve):
            V = nc.vector
            tt, ts, stt = V.tensor_tensor, V.tensor_scalar, V.scalar_tensor_tensor
            chain = {"n": 0}

            def link(ins):
                chain["n"] += 1
                ins.then_inc(chain_s, 1)
                dve.wait_ge(chain_s, chain["n"])

            def rsqrt(n, p=P):
                s, t, r = ssb[0:p, 0:n], newt[0:p, 0:n], rst[0:p, 0:n]
                link(ts(newt_i[0:p, 0:n], s.bitcast(I32), 1, None, ALU.logical_shift_right))
                link(ts(r.bitcast(I32), newt_i[0:p, 0:n], -1.0, float(0x5F3759DF), ALU.mult, ALU.add))
                for _ in range(3):
                    link(tt(t, r, r, ALU.mult))
                    link(stt(t, t, -0.5, s, ALU.mult, ALU.mult))
                    link(stt(r, t, 1.5, r, ALU.add, ALU.mult))

            def heads_rstd(src, dim):
                p, a, n, d = src.shape
                tmp = T1[0:p, 0:a * n * d].rearrange("p (a n d) -> p a n d", a=a, n=n)
                link(tt(tmp, src, src, ALU.mult))
                link(V.tensor_reduce(ssb[0:p, 0:a * n].rearrange("p (a n) -> p a n", a=a), tmp, AX.X, ALU.add))
                link(ts(ssb[0:p, 0:a * n], ssb[0:p, 0:a * n], 1.0 / dim, EPS, ALU.mult, ALU.add))
                rsqrt(a * n, p)

            def by_rstd(src, dst):
                p, a, n, d = src.shape
                r = rst[0:p, 0:a * n].rearrange("p (a n) -> p a n", a=a).unsqueeze(3).broadcast_to([p, a, n, d])
                link(tt(dst, src, r, ALU.mult))

            def gain(ap, lo, dst=None):
                p, a, n, d = ap.shape
                g = gn[0:p, lo:lo + d].unsqueeze(1).unsqueeze(1).broadcast_to([p, a, n, d])
                return tt(ap if dst is None else dst, ap, g, ALU.mult)

            def rope(src, cs, outs):
                p, a, n, d = src.shape
                hf = d // 2
                t1 = T1[:, 0:a * n * d].rearrange("p (a n d) -> p a n d", a=a, n=n)
                t2 = T2[:, 0:a * n * d].rearrange("p (a n d) -> p a n d", a=a, n=n)
                wide_ = lambda ap: ap.unsqueeze(2).broadcast_to([p, a, n, ap.shape[-1]])
                tt(t1, src, wide_(cs[:, 0, :, :]), ALU.mult)
                tt(t2[:, :, :, 0:hf], src[:, :, :, hf:d], wide_(cs[:, 1, :, 0:hf]), ALU.mult)
                link(tt(t2[:, :, :, hf:d], src[:, :, :, 0:hf], wide_(cs[:, 1, :, hf:d]), ALU.mult))
                for o in outs[:-1]:
                    tt(o, t1, t2, ALU.add)
                return tt(outs[-1], t1, t2, ALU.add)

            def sum_parts(r, bank, dst):
                return V.tensor_reduce(dst[:, 4 * r:4 * r + 4], ps[:, bank, :].rearrange("p (a n) -> p a n", a=4),
                                       AX.X, ALU.add)

            def unit(sums, adab, ng, slot, half):
                m = mod[:, slot, :, :].rearrange("p v k -> p (v k)")
                link(tt(m, sums, adab, ALU.add))
                if half:
                    ts(mod[:, slot, 2, :], mod[:, slot, 2, :], 0.5, None, ALU.mult)
                return stt(mod[:, slot, 1, :], mod[:, slot, 1, :], 1.0, ng, ALU.add, ALU.mult)

            dve.sem_inc(ada_used, 2)
            dve.sem_inc(tall_used, 2)
            V.memset(ones[:, :], 1.0)
            V.memset(zb[:, :], 0.0)
            V.memset(hidk[:, :, :], 0.0)
            V.memset(kcd[:, :, :, :], 0.0)
            V.memset(hidv[:, :, :, :], 0.0)
            link(V.memset(mband[:, :], 0.0))
            link(V.memset(mcausal[:, :], 0.0))
            dve.wait_ge(s_const, 16)
            V.tensor_copy(idb[:, :], ident)
            for m in (mcausal, mband):
                V.tensor_copy(m[:, 0:P], cst[:, C_CAUSAL:C_CAUSAL + P])
                V.tensor_copy(m[:, 2 * P:3 * P], cst[:, C_CAUSAL:C_CAUSAL + P])
            V.tensor_copy(mband[:, P:2 * P], cst[:, C_BAND:C_BAND + P]).then_inc(setup, 1)
            dve.wait_ge(turned, 1)
            dve.wait_ge(cond_ok, 1)
            for r in range(3):
                m = (126, 72, 72)[r]
                i = V.tensor_copy(vt[:, r, 0:m], ps[:, 0, r * P:r * P + m])
            link(i)
            n = 0
            for k in range(KD):
                if k in (2, 3):
                    dve.wait_ge(first_in[k - 2], 16)
                    piece = wide[:, k - 2, 0:3 * DM]
                else:
                    dve.wait_ge(ada_in[n % 2], 16 * (n // 2 + 1))
                    piece = ada[:, n % 2, :]
                if k == 0:
                    i = ts(acc[:, 0:3 * DM], piece, cond[:, 0:1], None, ALU.mult)
                else:
                    i = stt(acc[:, 0:3 * DM], piece, cond[:, k:k + 1], acc[:, 0:3 * DM], ALU.mult, ALU.add)
                if k in (2, 3):
                    link(i)
                    dve.sem_inc(wide_used, 1)
                else:
                    i.then_inc(ada_used, 1)
                    n += 1
                    dve.wait_ge(ada_used, 2 + n)
                if k == 1:
                    dve.wait_ge(h_in, 4)
                    dve.sem_inc(h_ready, KD)
            V.memset(small[:, 0:1], 0.0).then_inc(acc_ready, 1)

            for r in range(6):
                dve.wait_ge(mod_ps, r + 1)
                i = sum_parts(r, PRO_BANKS[r], msum)
            link(i)
            unit(msum[:, 0:24], vt[:, 1, 0:24], vt[:, 0, 0:8], 0, True).then_inc(mod_ready, 1)
            dve.wait_ge(mod_ready, 1)

            def rest_wide(l, f, m, i=0):
                it, a = m // 2, m % 2
                slot = ((WIDE_A, WIDE_B)[f] + it) % 2
                raw = wide[:, slot, :].rearrange("p (g n) -> p g n", n=2 * P)[:, :, a * P:(a + 1) * P]
                dve.wait_ge(wh_ready, tile_at(l, f, m, i))
                tt(wl[:, a, :, :, :].rearrange("p e k n -> p (e k) n"), raw,
                   wh[:, a, :, :, :].rearrange("p e k n -> p (e k) n").bitcast(F32), ALU.subtract)\
                    .then_inc(wl_ready, 1)

            def norm(l, j):
                dve.wait_ge(ss_ready, l * 3 + (j + 1))
                for t in range(NT):
                    i = ts(ssb[:, t:t + 1], ps[:, 2 + t, 0:1], 1.0 / DM, EPS, ALU.mult, ALU.add)
                link(i)
                rsqrt(NT)
                for t in range(NT):
                    i = ts(T1[:, t * P:(t + 1) * P], ident, rst[:, t:t + 1], None, ALU.mult)
                i.then_inc(diag_ready, 1)
                dve.wait_ge(r_ready, l * 3 + (j + 1))
                for k in range(KD):
                    stt(sq[:, k * SEQ:(k + 1) * SEQ], h[:, k, :], mod[:, j, 1, k:k + 1], ps[:, 2, 0:SEQ],
                        ALU.mult, ALU.mult).then_inc(hn_ready, 1)

            def residual(l, j):
                for k in range(KD):
                    if k % 2 == 0:
                        dve.wait_ge(y_ready, l * 12 + (4 * j + k // 2 + 1))
                    stt(h[:, k, :], y[:, k, :], mod[:, j, 2, k:k + 1], h[:, k, :], ALU.mult, ALU.add)\
                        .then_inc(h_ready, 1)

            def rest_tall(l, j, m0, m, i=0):
                it, a = m // 2, m % 2
                dve.wait_ge(th_ready, rows_at(l, j, m, i))
                tt(tl[:, a, :], tall[:, (m0 + it) % 2, a * DM:(a + 1) * DM], th[:, a, :].bitcast(F32),
                   ALU.subtract).then_inc(tl_ready, 1)

            def ffn(l, f, last=False):
                j = 2 * f
                n0, m0 = (WIDE_A, TALL_A) if f == 0 else (WIDE_B, TALL_B)
                norm(l, j)
                width = 3 * DM if f == 0 else 1536

                if f == 0:
                    rest_wide(l, 0, 0)
                for k in range(KD):
                    dve.wait_ge(u_ready, l * 24 + (8 * j + k + 1))
                    stt(ul[:, k, :], sq[:, k * SEQ:(k + 1) * SEQ], mod[:, j, 0, k:k + 1], uh[:, k, :].bitcast(F32),
                        ALU.add, ALU.subtract).then_inc(ul_ready, 1)

                def tile(m, i=0):
                    a = m % 2
                    dve.wait_ge(silu_ready, tile_at(l, f, m, i))
                    tt(fa[:, a, :], fs[:, a, :], ps[:, a, SEQ:2 * SEQ], ALU.mult).then_inc(fa_s, 1)
                    dve.wait_ge(fa_s, tile_at(l, f, m, i))
                    V.tensor_copy(fh[:, a, :], fa[:, a, :]).then_inc(fh_s, 1)
                    rest_tall(l, 2 * f, m0, m, i)
                    dve.wait_ge(fh_s, tile_at(l, f, m, i))
                    tt(fl[:, a, :], fa[:, a, :], fh[:, a, :].bitcast(F32), ALU.subtract).then_inc(mul_ready, 1)
                    if a == 1:
                        dve.wait_ge(tl_ready, rows_at(l, 2 * f, m, i))
                        dve.sem_inc(tall_used, 1)
                    if m + 2 < 2 * NPAIR:
                        rest_wide(l, f, m + 2, i)

                def free_wide(m, i=0):
                    dve.wait_ge(wl_ready, tile_at(l, f, m, i))
                    dve.sem_inc(wide_used, 1)

                def ada_step(q, e, i):
                    count = l * ADA_L + (ADA_PRO + f * 2 * KD + 2 * q + e) + 4 * i
                    dve.wait_ge(ada_in[e], l * (ADA_L * 8) + (ADA_PRO * 8 + f * KD * 16 + 16 * (q + 1)) + 32 * i)
                    a = acc[:, e * width:(e + 1) * width]
                    dve.wait_ge(ada_used, count + 1)
                    stt(a, ada[:, e, 0:width], cond[:, bass.ds(2 * i + q, 1)], a, ALU.mult, ALU.add)\
                        .then_inc(ada_used, 1)

                rest_wide(l, f, 1)
                free_wide(1)
                with dve.Fori(0, KD // 2) as i:
                    for q in range(4):
                        tile(q, i)
                        if not last:
                            if q == 0:
                                dve.wait_ge(acc_zero, l * 2 + (f + 1))
                            ada_step(q // 2, q % 2, i)
                        if q % 2:
                            free_wide(q + 2, i)
                if not last:
                    dve.wait_ge(ada_used, l * ADA_L + (ADA_PRO + (f + 1) * 2 * KD + 2))
                    V.memset(small[:, 0:1], 0.0).then_inc(acc_ready, 1)
                rounds = 12 - 6 * f
                for m in range(2 * KD, 2 * NPAIR):
                    tile(m)
                    if m % 2 and m + 2 < 2 * NPAIR:
                        free_wide(m + 2)
                    for r in range(2 * (m - 2 * KD), 2 * (m - 2 * KD) + 2):
                        if r < rounds and not last:
                            dve.wait_ge(mod_ps, l * 18 + (6 + 12 * f + r + 1))
                            sum_parts(r, 2 + r % 2, msum).then_inc(mod_red, 1)
                residual(l, j)
                if last:
                    return
                dve.wait_ge(mod_red, l * 18 + (12 * f + rounds))
                for s in ((1, 2) if f == 0 else (0,)):
                    if f == 0:
                        adab = vt[:, bass.ds(l + 1, 1), 24 * s:24 * s + 24].rearrange("p a n -> p (a n)")
                        ng = vt[:, 0, bass.ds(l * 24 + 8 * s, 8)]
                        i = unit(msum[:, 24 * (s - 1):24 * s], adab, ng, s, s == 2)
                    else:
                        i = unit(msum[:, 0:24], vt[:, DEPTH, 0:24],
                                 vt[:, 0, 24 * (DEPTH - 1):24 * (DEPTH - 1) + 8], 0, True)
                    i.then_inc(mod_ready, 1)
                if f == 0:
                    V.tensor_copy(latg[:, 0:2], vt[:, 0, bass.ds(l * 2 + 56, 2)])
                    V.tensor_copy(pe2[:, :], vt[:, 0, bass.ds(l * 32 + 62, 32)])
                    V.tensor_copy(latg[:, 2:3], vt[:, 0, bass.ds(l + 60, 1)]).then_inc(mod_lat, 1)
                    dve.wait_ge(mod_lat, l + 1)
                dve.wait_ge(mod_ready, l * 3 + (3 if f == 0 else 4))

            def aux_wait(l, name):
                dve.wait_ge(aux_ready, aux_at(l, name))

            def copied(l, chunk):
                dve.wait_ge(pcopy, l * 2 * len(CHUNKS) + 2 * (chunk + 1))

            def out_of(l, name, dst, width=P):
                aux_wait(l, name)
                src = ps[0:width, aux_bank(name), :].rearrange("p (b n) -> p b n", b=2)
                V.tensor_copy(dst, src).then_inc(aux_dve, 1)

            def v4(ap, n):
                return ap.rearrange("p t (n d) -> p t n d", n=n)

            def mixer(l):
                norm(l, 1)
                dve.wait_ge(s_small, (l + 1) * 160)
                dve.wait_ge(u_ready, l * 24 + 16)
                copied(l, 0)
                for lo, hi, part in ((0, 256, 0), (256, 384, 2), (384, 416, 4)):
                    s = plat[:, :, lo:hi].unsqueeze(2)
                    tmp = T1[:, 0:2 * (hi - lo)].rearrange("p (a n d) -> p a n d", a=2, n=1)
                    link(tt(tmp, s, s, ALU.mult))
                    link(V.tensor_reduce(ssb[:, part:part + 2].unsqueeze(2), tmp, AX.X, ALU.add))
                    link(ts(ssb[:, part:part + 2], ssb[:, part:part + 2], 1.0 / (hi - lo), EPS, ALU.mult, ALU.add))
                rsqrt(6)
                for lo, hi, part in ((0, 256, 0), (256, 384, 2), (384, 416, 4)):
                    s = plat[:, :, lo:hi]
                    r = rst[:, part:part + 2].unsqueeze(2).broadcast_to([P, NT, hi - lo])
                    i = tt(s, s, r, ALU.mult)
                i.then_inc(prep, 1)
                dve.wait_ge(prep, prep_at(l, "lat"))
                kr = plat[:, :, 384:416].unsqueeze(2)
                dve.wait_ge(tables, 1)
                link(gain(kr, G_BR + 32))
                link(rope(kr, cs32, [kb[:, :, hh:hh + 1, HD:96] for hh in range(B_H)]))
                for a, name in enumerate(("zk", "zv")):
                    aux_wait(l, name)
                    for hh in range(2):
                        for par in range(2):
                            half = slice(64 * par, 64 * par + 64)
                            src = ps[half, aux_bank(name), hh * SEQ:(hh + 1) * SEQ].rearrange("p (b r) -> p b r", r=16)
                            for late in range(2):
                                z = src[:, late:late + NCMP, par:16:2].rearrange("p b m -> p m b")
                                dst = zc[half, a, hh, 8 * late:8 * late + 8, :]
                                o = pe2[half, a * 16 + 8 * late:a * 16 + 8 * late + 8].unsqueeze(2)\
                                    .broadcast_to([64, 8, NCMP])
                                i = tt(dst, z, o, ALU.add)
                    i.then_inc(aux_dve, 1)
                aux_wait(l, "lat")
                for b in range(2):
                    i = ts(latT[:, b, :], ps[:, aux_bank("lat"), b * SEQ:(b + 1) * SEQ], latg[:, b:b + 1], None, ALU.mult)
                i.then_inc(aux_dve, 1)
                copied(l, 2)
                qk = v4(pa[:, :, 0:384], 6)
                heads_rstd(qk, HD)
                by_rstd(qk, qk)
                gain(qk[:, :, 0:A_H, :], G_A)
                link(gain(qk[:, :, A_H:6, :], G_A + HD))
                link(rope(qk[:, :, 0:A_H, :], cs64, [qa[:, :, :, :]]))
                rope(qk[:, :, A_H:6, :], cs64, [kad[:, :, :, 0, :], kad[:, :, :, 1, :]]).then_inc(prep, 1)
                dve.wait_ge(prep, prep_at(l, "qa"))
                aux_wait(l, "gate")
                tt(gt[:, :, :], ps[:, aux_bank("gate"), 0:48].rearrange("p (t n) -> p t n", t=NT),
                   gn[:, G_GB:G_END].unsqueeze(1).broadcast_to([P, NT, 24]), ALU.add).then_inc(aux_dve, 1)
                dve.wait_ge(*aux_done("uq1", l))
                qn, qp = qb[:, :, :, 0:HD], qb[:, :, :, HD:96]
                heads_rstd(qn, HD)
                by_rstd(qn, qn)
                gain(qn, G_BN)
                heads_rstd(qp, ROPE_B)
                by_rstd(qp, qp)
                link(gain(qp, G_BR))
                rope(qp, cs32, [qp]).then_inc(prep, 1)
                dve.wait_ge(prep, prep_at(l, "qb"))
                dve.wait_ge(*aux_done("ukv1", l))
                kn = kvb[:, :, :, 0:HD]
                heads_rstd(kn, HD)
                by_rstd(kn, kb[:, :, :, 0:HD])
                gain(kb[:, :, :, 0:HD], G_BN + HD).then_inc(prep, 1)
                dve.wait_ge(prep, prep_at(l, "kb"))
                dve.wait_ge(*aux_done("w2", l))
                kc = kcn[0:NCMP, :, :].unsqueeze(2)
                heads_rstd(kc, HD)
                by_rstd(kc, kc)
                for dup in range(2):
                    i = gain(kc, G_C + HD, kcd[0:NCMP, :, dup, :].unsqueeze(2))
                i.then_inc(prep, 1)
                dve.wait_ge(prep, prep_at(l, "kc"))
                copied(l, 3)
                cq = v4(pq, C_H)
                heads_rstd(cq, HD)
                by_rstd(cq, cq)
                gain(cq, G_C).then_inc(prep, 1)
                dve.wait_ge(prep, prep_at(l, "cq"))
                rope(cq, cs64, [qr[:, :, :, :]]).then_inc(prep, 1)
                dve.wait_ge(prep, prep_at(l, "cr"))
                copied(l, 4)
                ck = v4(pk[:, :, 0:256], 4)
                heads_rstd(ck, HD)
                by_rstd(ck, ck)
                gain(ck[:, :, 0:2, :], G_C + 2 * HD)
                link(gain(ck[:, :, 2:4, :], G_C + 3 * HD))
                rope(ck, cs64, [krd[:, :, :, 0, :], krd[:, :, :, 1, :]]).then_inc(prep, 1)
                dve.wait_ge(prep, prep_at(l, "ck"))
                spread = lambda ap, n=C_H: ap.rearrange("p (t b) -> p t b", t=NT).unsqueeze(2)\
                    .broadcast_to([P, NT, n, NCMP])
                over = lambda r: cst16[:, r, :].rearrange("p (t n) -> p t n", t=NT)
                gates = gt[:, :, :].rearrange("p t (n g) -> p t n g", g=3)
                for odd in range(2):
                    aux_wait(l, f"cmps{odd}")
                    sv = ps[:, aux_bank(f"cmps{odd}"), 0:128].rearrange("p (t n b) -> p t n b", t=NT, b=16)
                    tt(csc[:, :, odd:C_H:2, :], sv[:, :, :, 0:NCMP], spread(cst[:, C_NEG:C_NEG + 30], C_H // 2),
                       ALU.add).then_inc(aux_dve, 1)
                dve.wait_ge(*aux_done("cmps1", l))
                link(V.tensor_reduce(over(0), csc, AX.X, ALU.max))
                tt(csc, csc, over(0).unsqueeze(3).broadcast_to([P, NT, C_H, NCMP]), ALU.subtract)\
                    .then_inc(cmp_shift, 1)

                def compressed_probs():
                    dve.wait_ge(gate_exp, l + 1)
                    link(ts(gt[:, :, :], gt[:, :, :], 1.0, None, ALU.add))
                    link(V.reciprocal(gt[:, :, :], gt[:, :, :]))
                    dve.wait_ge(cmp_exp, l + 1)
                    link(V.memset(cp, 0.0))
                    link(V.tensor_reduce(over(1), csc, AX.X, ALU.add))
                    link(V.reciprocal(over(1), over(1)))
                    link(tt(over(2), over(1), gates[:, :, :, 0], ALU.mult))
                    link(tt(csc, csc, spread(cst[:, C_VIS:C_VIS + 30]), ALU.mult))
                    tt(cp[:, :, :, 0:NCMP], csc, over(2).unsqueeze(3).broadcast_to([P, NT, C_H, NCMP]), ALU.mult)\
                        .then_inc(prep, 1)

                for n in range(NJ + 4):
                    if n - 4 in LAST:
                        pair = LAST.index(n - 4)
                        dve.wait_ge(pv_ready, l * NJ + (n - 3))
                        V.tensor_copy(uh[:, pair, :], ps[:, 3, 0:SEQ]).then_inc(oh_s, 1)
                        dve.wait_ge(oh_s, l * KD + (pair + 1))
                        tt(ol[:, pair, :], ps[:, 3, 0:SEQ], uh[:, pair, :].bitcast(F32), ALU.subtract)\
                            .then_inc(o_ready, 1)
                    if n < NJ:
                        br, hh = JOBS[n]
                        st = stat[:, n % 4, :]
                        scale = job(n)[4]
                        bank = ps[:, n % 2, :]
                        dve.wait_ge(s_ready, l * NJ + (n + 1))
                        V.tensor_reduce(st[:, 0:1], bank[:, 0:P], AX.X, ALU.max)
                        link(V.tensor_reduce(st[:, 1:2], bank[:, P:3 * P], AX.X, ALU.max))
                        if br == "a":
                            sink = gn[:, G_SINK + hh:G_SINK + hh + 1].broadcast_to([P, 2])
                            link(stt(st[:, 0:2], st[:, 0:2], scale, sink, ALU.mult, ALU.max))
                            ts(st[:, 2:4], st[:, 0:2], -1.0, None, ALU.mult).then_inc(nm_ready, 1)
                        else:
                            ts(st[:, 2:4], st[:, 0:2], -scale, None, ALU.mult).then_inc(nm_ready, 1)
                    if 1 <= n <= NJ:
                        m = n - 1
                        br, hh = JOBS[m]
                        st = stat[:, m % 4, :]
                        dve.wait_ge(exp_ready, l * NJ + (m + 1))
                        if br == "a":
                            link(tt(st[:, 4:6], st[:, 4:6], st[:, 6:8], ALU.add))
                        link(V.reciprocal(st[:, 4:6], st[:, 4:6]))
                        if br in ("slc", "win"):
                            g = gates[:, :, hh, 1 if br == "slc" else 2]
                            link(tt(st[:, 4:6], st[:, 4:6], g, ALU.mult))
                        ts(E[:, m % 3, 0:P], E[:, m % 3, 0:P], st[:, 4:5], None, ALU.mult)
                        ts(E[:, m % 3, P:3 * P], E[:, m % 3, P:3 * P], st[:, 5:6], None, ALU.mult)\
                            .then_inc(en_ready, 1)
                    if n == 1:
                        compressed_probs()
                    if n == 5:
                        out_of(l, "cmpt", cmpT[:, :, :])
                    for k in range(KD):
                        if n == min(LAST[k] + 4, NJ + 2):
                            rest_tall(l, 1, TALL_M, k)
                            if k % 2:
                                dve.wait_ge(tl_ready, rows_at(l, 1, k))
                                dve.sem_inc(tall_used, 1)
                residual(l, 1)
                rest_wide(l, 1, 0)

            with dve.Fori(0, DEPTH - 1) as l:
                dve.sem_clear(chain_s)
                chain["n"] = 0
                ffn(l, 0)
                mixer(l)
                ffn(l, 1)
            dve.sem_clear(chain_s)
            chain["n"] = 0
            ffn(DEPTH - 1, 0)
            mixer(DEPTH - 1)
            ffn(DEPTH - 1, 1, True)


_INS = ["x", "c", "positions", "ada_w", "ada_b", "norm_g", "ffn_w_in", "ffn_w_out", "w_in", "w_out",
        "a_sinks", "a_qk_g", "b_q_lat_g", "b_kv_lat_g", "b_w_uq", "b_w_ukv", "b_qk_nope_g", "b_qk_rope_g",
        "c_qk_g", "c_cmp_pe", "c_cmp_w1", "c_cmp_w2", "c_gate_w", "c_gate_b"]


def shape_constants():
    t = np.zeros((P, C_END), np.float32)
    q, k = np.arange(P)[:, None], np.arange(P)[None, :]
    t[:, C_ID:C_ID + P] = q == k
    t[:, C_CAUSAL:C_CAUSAL + P] = np.where(k > q, NEG, 0.0)
    t[:, C_BAND:C_BAND + P] = np.where(k <= q, NEG, 0.0)
    for lo, dim in ((0, HD), (HD // 2, ROPE_B)):
        power = np.arange(0, dim, 2, dtype=np.float32) / np.float32(dim)
        t[:, C_INVF + lo:C_INVF + lo + dim // 2] = np.float32(1.0) / np.power(np.float32(10000.0), power)
    for i in range(NT):
        seen = np.arange(NCMP)[None, :] * 16 + CL - 1 <= i * P + q
        t[:, C_NEG + i * NCMP:C_NEG + (i + 1) * NCMP] = np.where(seen, 0.0, NEG)
        t[:, C_VIS + i * NCMP:C_VIS + (i + 1) * NCMP] = seen
    return t


def kernel(**inputs):
    import concourse.bacc as _bacc
    from concourse.bass_utils import run_bass_kernel_spmd as _run

    nc = _bacc.Bacc("TRN2", target_bir_lowering=False, num_devices=1)
    arrays, args = {}, []
    for name in _INS + ["consts"]:
        a = np.ascontiguousarray(inputs[name] if name != "consts" else shape_constants())
        arrays[f"in_{name}_dram"] = a
        args.append(nc.dram_tensor(f"in_{name}_dram", a.shape, mybir.dt.from_np(a.dtype), kind="ExternalInput").ap())
    out = nc.dram_tensor("out_0_dram", (1, SEQ, DM), F32, kind="ExternalOutput").ap()
    hybrid_kernel(nc, *args, out)
    r = _run(nc, [arrays], core_ids=[0])
    return r.results[0]["out_0_dram"]
```
